# Optimizing a Trainium2 kernel written in Bass

```python
import math
import jax, jax.numpy as jnp
from jax import lax
import numpy as np

D_MODEL = 1024
BATCH = 1
SEQ = 512
DEPTH = 2
DEC_BATCH = 8
DEC_SEQ = 8
PAST_LEN = 256
PAGE_SIZE = 128

N_A = DEPTH // 2
N_B = DEPTH - N_A
D_INNER = D_MODEL
CONV_W = 31
N_HEADS = 16
HEAD_DIM = 64
KV_HEADS = 4
GROUP = N_HEADS // KV_HEADS
KV_DIM = KV_HEADS * HEAD_DIM
N_BRANCH = 3
L_CMP = 32
CMP_STRIDE = 16
CMP_HID = 256
L_SLC = 64
N_SEL = 16
WINDOW = 512
Q_BLK = 128
NUM_BUCKETS = 32
MAX_DISTANCE = 128
MAX_EXACT = NUM_BUCKETS // 2
Q_WIDTH = N_HEADS * HEAD_DIM
B_IN = Q_WIDTH + N_BRANCH * Q_WIDTH + N_BRANCH * N_HEADS
EPS = 1e-6
NEG = -1e30
BIG = 1e9

kernel_name = 'yoco_conformer_nsa_decode_step'

def rms_norm(x, g):
    xf = x.astype(jnp.float32)
    y = xf * lax.rsqrt(jnp.mean(xf * xf, axis=-1, keepdims=True) + EPS)
    return (y * g.astype(jnp.float32)).astype(x.dtype)

def layer_norm(x, g, b):
    xf = x.astype(jnp.float32)
    mu = jnp.mean(xf, axis=-1, keepdims=True)
    var = jnp.mean(jnp.square(xf - mu), axis=-1, keepdims=True)
    y = (xf - mu) * lax.rsqrt(var + EPS)
    return (y * g.astype(jnp.float32) + b.astype(jnp.float32)).astype(x.dtype)

def t5_bucket(dist):
    n = jnp.maximum(dist, 0)
    nf = jnp.maximum(n, 1).astype(jnp.float32)
    large = MAX_EXACT + (jnp.log(nf / MAX_EXACT) / math.log(MAX_DISTANCE / MAX_EXACT)
                         * (NUM_BUCKETS - MAX_EXACT)).astype(jnp.int32)
    large = jnp.minimum(large, NUM_BUCKETS - 1)
    return jnp.where(n < MAX_EXACT, n, large)

def masked_softmax(logits, mask, axis):
    l = jnp.where(mask, logits.astype(jnp.float32), NEG)
    m = jnp.max(l, axis=axis, keepdims=True)
    p = jnp.where(mask, jnp.exp(l - m), 0.0)
    d = jnp.sum(p, axis=axis, keepdims=True)
    return p / jnp.maximum(d, 1e-30)

def conformer_layer(x, conv_prev, g_pre, w_in, conv_w, conv_b, ln_g, ln_b, w_out, g_post):
    h = rms_norm(x, g_pre)
    a, b, z = jnp.split(h @ w_in, 3, axis=-1)
    glu = a * jax.nn.sigmoid(b)
    full = jnp.concatenate([conv_prev.astype(glu.dtype), glu], axis=1)
    c = lax.conv_general_dilated(full, conv_w[:, None, :].astype(glu.dtype), (1,), 'VALID',
                                 dimension_numbers=('NWC', 'WIO', 'NWC'),
                                 feature_group_count=D_INNER) + conv_b
    y = jax.nn.silu(layer_norm(c, ln_g, ln_b)) * jax.nn.silu(z)
    return x + rms_norm(y @ w_out, g_post), full[:, -(CONV_W - 1):]

def kv_rows(x, g_kv, w_kv):
    h = rms_norm(x, g_kv)
    kv = (h @ w_kv).reshape(x.shape[0], x.shape[1], N_BRANCH, 2, KV_HEADS, HEAD_DIM)
    return kv[:, :, 0], kv[:, :, 1], kv[:, :, 2]

def compress(rows, pe, w1, w2):
    b, L = rows.shape[:2]
    r_parts = L_CMP // CMP_STRIDE
    n_chunk = L // CMP_STRIDE
    nc = n_chunk - r_parts + 1
    chunks = rows[:, :n_chunk * CMP_STRIDE].reshape(b, n_chunk, CMP_STRIDE, KV_HEADS, HEAD_DIM)
    w1r = w1.reshape(r_parts, CMP_STRIDE, HEAD_DIM, CMP_HID)
    pe_r = pe.reshape(r_parts, CMP_STRIDE, HEAD_DIM)
    pre = jnp.einsum('rsd,rsdh->h', pe_r, w1r)
    for r in range(r_parts):
        pre = pre + jnp.einsum('bnskd,sdh->bnkh', chunks[:, r:r + nc], w1r[r])
    return jax.nn.silu(pre) @ w2

def sparse_keys(cmp_rows, slc_rows, cmp_pe, cmp_w1, cmp_w2):
    kc = compress(cmp_rows[:, :, 0], cmp_pe[0], cmp_w1[0], cmp_w2[0])
    vc = compress(cmp_rows[:, :, 1], cmp_pe[1], cmp_w1[1], cmp_w2[1])
    b, L = slc_rows.shape[:2]
    nb = -(-L // L_SLC)
    s = jnp.pad(slc_rows, ((0, 0), (0, nb * L_SLC - L), (0, 0), (0, 0), (0, 0)))
    s = s.reshape(b, nb, L_SLC, 2, KV_HEADS, HEAD_DIM).transpose(3, 0, 4, 1, 2, 5)
    return kc, vc, s[0], s[1]

def cmp_to_slc(nc, nb):
    cs = jnp.arange(nc)[:, None] * CMP_STRIDE
    js = jnp.arange(nb)[None, :] * L_SLC
    return ((cs <= js + L_SLC - 1) & (cs + L_CMP - 1 >= js)).astype(jnp.float32)

def nsa_block(q, qpos, kc, vc, ks, vs, kw, vw, kwpos, rel_bias):
    f32 = jnp.float32
    scale = HEAD_DIM ** -0.5
    bias_kvg = rel_bias.reshape(NUM_BUCKETS, KV_HEADS, GROUP).astype(f32)
    nc = kc.shape[1]
    nb = ks.shape[2]
    c_end = jnp.arange(nc) * CMP_STRIDE + (L_CMP - 1)
    dist_c = qpos[:, None] - c_end[None, :]
    bias_c = jnp.transpose(bias_kvg[t5_bucket(dist_c)], (2, 3, 0, 1))
    lc = jnp.einsum('btkgd,bckd->bkgtc', q, kc).astype(f32) * scale + bias_c
    pc = masked_softmax(lc, dist_c >= 0, -1)
    o_c = jnp.einsum('bkgtc,bckd->btkgd', pc, vc.astype(f32))
    imp = jnp.einsum('bkgtc,cj->bktj', pc, cmp_to_slc(nc, nb))
    j = jnp.arange(nb)[None, :]
    tb = (qpos // L_SLC)[:, None]
    valid = j * L_SLC <= qpos[:, None]
    forced = (j == 0) | (j == tb) | (j == tb - 1)
    score = jnp.where(valid, jnp.where(forced, BIG, imp), -BIG)
    _, idx = lax.top_k(score, min(N_SEL, nb))
    bi = jnp.arange(q.shape[0])[:, None, None, None]
    ki = jnp.arange(KV_HEADS)[None, :, None, None]
    kg = ks[bi, ki, idx]
    vg = vs[bi, ki, idx]
    s_pos = idx[..., None] * L_SLC + jnp.arange(L_SLC)
    dist_s = qpos[None, None, :, None, None] - s_pos
    bias_s = jnp.moveaxis(bias_kvg[t5_bucket(dist_s), ki[..., None]], -1, 3)
    ls = jnp.einsum('btkgd,bktnld->bktgnl', q, kg).astype(f32) * scale + bias_s
    ps = masked_softmax(ls, (dist_s >= 0)[:, :, :, None], (-2, -1))
    o_s = jnp.einsum('bktgnl,bktnld->btkgd', ps, vg.astype(f32))
    dist_w = qpos[:, None] - kwpos[None, :]
    mask_w = (dist_w >= 0) & (dist_w <= WINDOW) & (kwpos[None, :] >= 0)
    bias_w = jnp.transpose(bias_kvg[t5_bucket(dist_w)], (2, 3, 0, 1))
    lw = jnp.einsum('btkgd,bskd->bkgts', q, kw).astype(f32) * scale + bias_w
    pw = masked_softmax(lw, mask_w, -1)
    o_w = jnp.einsum('bkgts,bskd->btkgd', pw, vw.astype(f32))
    return jnp.stack([o_c, o_s, o_w], axis=2)

def nsa_query_side(x, g_pre, w_in):
    b, t = x.shape[:2]
    u = rms_norm(x, g_pre) @ w_in
    q = u[..., :Q_WIDTH].reshape(b, t, KV_HEADS, GROUP, HEAD_DIM)
    z = u[..., Q_WIDTH:Q_WIDTH * (1 + N_BRANCH)].reshape(b, t, N_BRANCH, N_HEADS, HEAD_DIM)
    gate = jax.nn.sigmoid(u[..., Q_WIDTH * (1 + N_BRANCH):].astype(jnp.float32)).reshape(b, t, N_BRANCH, N_HEADS)
    return q, z, gate

def nsa_output(x, o, z, gate, w_out, g_post):
    b, t = x.shape[:2]
    y = jnp.sum(gate[..., None] * o * jax.nn.silu(z.astype(jnp.float32)), axis=2)
    y = y.reshape(b, t, Q_WIDTH).astype(x.dtype)
    return x + rms_norm(y @ w_out, g_post)

def nsa_attend_prompt(q, kc, vc, ks, vs, k_win, v_win, rel_bias):
    b, t = q.shape[:2]
    nq = t // Q_BLK
    qb = q.reshape(b * nq, Q_BLK, KV_HEADS, GROUP, HEAD_DIM)
    bidx = jnp.repeat(jnp.arange(b), nq)
    t0s = jnp.tile(jnp.arange(nq) * Q_BLK, b)
    pad = ((0, 0), (WINDOW, 0), (0, 0), (0, 0))
    kw_pad = jnp.pad(k_win, pad)
    vw_pad = jnp.pad(v_win, pad)

    def step(args):
        qi, bb, t0 = args
        qpos = t0 + jnp.arange(Q_BLK)
        kw = lax.dynamic_slice_in_dim(kw_pad[bb], t0, WINDOW + Q_BLK, axis=0)[None]
        vw = lax.dynamic_slice_in_dim(vw_pad[bb], t0, WINDOW + Q_BLK, axis=0)[None]
        kwpos = t0 - WINDOW + jnp.arange(WINDOW + Q_BLK)
        return nsa_block(qi[None], qpos, kc[bb][None], vc[bb][None], ks[bb][None], vs[bb][None],
                         kw, vw, kwpos, rel_bias)[0]

    o = lax.map(step, (qb, bidx, t0s))
    return o.reshape(b, t, N_BRANCH, N_HEADS, HEAD_DIM)

def nsa_attend_sample(q, kc, vc, ks, vs, kw, vw, past_len, rel_bias):
    b, tq = q.shape[:2]
    qpos = past_len + jnp.arange(tq)
    kwpos = past_len - (kw.shape[1] - tq) + jnp.arange(kw.shape[1])

    def step(args):
        qi, kci, vci, ksi, vsi, kwi, vwi = args
        return nsa_block(qi[None], qpos, kci[None], vci[None], ksi[None], vsi[None],
                         kwi[None], vwi[None], kwpos, rel_bias)[0]

    o = lax.map(step, (q, kc, vc, ks, vs, kw, vw))
    return o.reshape(b, tq, N_BRANCH, N_HEADS, HEAD_DIM)

def setup_inputs(seed: int = 0) -> dict:
    key = jax.random.key(seed)
    k = jax.random.split(key, 26)
    n_pages = PAST_LEN // PAGE_SIZE
    n_pool = (DEC_BATCH * n_pages * 5) // 4
    w_keep = min(WINDOW, PAST_LEN)

    def nrm(kk, shape, s):
        return jax.random.normal(kk, shape, jnp.float32) * s

    def gain(kk, shape):
        return 1.0 + nrm(kk, shape, 0.05)

    page_table = jax.random.permutation(k[0], n_pool)[:DEC_BATCH * n_pages]
    page_table = page_table.reshape(DEC_BATCH, n_pages).astype(jnp.int32)
    return {
        'x_prompt': nrm(k[1], (BATCH, SEQ, D_MODEL), 1.0),
        'x_sample': nrm(k[2], (DEC_BATCH, DEC_SEQ, D_MODEL), 1.0),
        'state_conv': nrm(k[3], (N_A, DEC_BATCH, CONV_W - 1, D_INNER), 0.5),
        'cache_cmp': nrm(k[4], (n_pool, PAGE_SIZE, 2, KV_HEADS, HEAD_DIM), 1.0),
        'cache_slc': nrm(k[5], (n_pool, PAGE_SIZE, 2, KV_HEADS, HEAD_DIM), 1.0),
        'state_win': nrm(k[6], (DEC_BATCH, w_keep, 2, KV_HEADS, HEAD_DIM), 1.0),
        'page_table': page_table,
        'rel_bias': nrm(k[7], (NUM_BUCKETS, N_HEADS), 0.5),
        'a_norm_pre': gain(k[8], (N_A, D_MODEL)),
        'a_w_in': nrm(k[9], (N_A, D_MODEL, 3 * D_INNER), D_MODEL ** -0.5),
        'a_conv_w': nrm(k[10], (N_A, CONV_W, D_INNER), CONV_W ** -0.5),
        'a_conv_b': nrm(k[11], (N_A, D_INNER), 0.02),
        'a_ln_g': gain(k[12], (N_A, D_INNER)),
        'a_ln_b': nrm(k[13], (N_A, D_INNER), 0.02),
        'a_w_out': nrm(k[14], (N_A, D_INNER, D_MODEL), D_INNER ** -0.5),
        'a_norm_post': gain(k[15], (N_A, D_MODEL)),
        'kv_norm': gain(k[16], (D_MODEL,)),
        'w_kv': nrm(k[17], (D_MODEL, 2 * N_BRANCH * KV_DIM), D_MODEL ** -0.5),
        'cmp_pe': nrm(k[18], (2, L_CMP, HEAD_DIM), 0.1),
        'cmp_w1': nrm(k[19], (2, L_CMP * HEAD_DIM, CMP_HID), (L_CMP * HEAD_DIM) ** -0.5),
        'cmp_w2': nrm(k[20], (2, CMP_HID, HEAD_DIM), CMP_HID ** -0.5),
        'b_norm_pre': gain(k[21], (N_B, D_MODEL)),
        'b_w_in': nrm(k[22], (N_B, D_MODEL, B_IN), D_MODEL ** -0.5),
        'b_w_out': nrm(k[23], (N_B, Q_WIDTH, D_MODEL), Q_WIDTH ** -0.5),
        'b_norm_post': gain(k[24], (N_B, D_MODEL)),
    }

def reference(x_prompt, x_sample, state_conv, cache_cmp, cache_slc, state_win, page_table, rel_bias,
              a_norm_pre, a_w_in, a_conv_w, a_conv_b, a_ln_g, a_ln_b, a_w_out, a_norm_post,
              kv_norm, w_kv, cmp_pe, cmp_w1, cmp_w2,
              b_norm_pre, b_w_in, b_w_out, b_norm_post):
    n_pages = page_table.shape[1]
    past_len = n_pages * PAGE_SIZE
    bp, t_prompt = x_prompt.shape[:2]
    bd = x_sample.shape[0]
    xp, xs = x_prompt, x_sample
    conv_p, conv_s = [], []
    for l in range(N_A):
        zeros = jnp.zeros((bp, CONV_W - 1, D_INNER), xp.dtype)
        xp, cp = conformer_layer(xp, zeros, a_norm_pre[l], a_w_in[l], a_conv_w[l], a_conv_b[l],
                                 a_ln_g[l], a_ln_b[l], a_w_out[l], a_norm_post[l])
        xs, cs = conformer_layer(xs, state_conv[l], a_norm_pre[l], a_w_in[l], a_conv_w[l], a_conv_b[l],
                                 a_ln_g[l], a_ln_b[l], a_w_out[l], a_norm_post[l])
        conv_p.append(cp)
        conv_s.append(cs)
    cmp_p, slc_p, win_p = kv_rows(xp, kv_norm, w_kv)
    cmp_s, slc_s, win_s = kv_rows(xs, kv_norm, w_kv)
    kc_p, vc_p, ks_p, vs_p = sparse_keys(cmp_p, slc_p, cmp_pe, cmp_w1, cmp_w2)
    past_cmp = cache_cmp[page_table].reshape(bd, past_len, 2, KV_HEADS, HEAD_DIM).astype(cmp_s.dtype)
    past_slc = cache_slc[page_table].reshape(bd, past_len, 2, KV_HEADS, HEAD_DIM).astype(slc_s.dtype)
    kc_s, vc_s, ks_s, vs_s = sparse_keys(jnp.concatenate([past_cmp, cmp_s], axis=1),
                                         jnp.concatenate([past_slc, slc_s], axis=1),
                                         cmp_pe, cmp_w1, cmp_w2)
    win_all = jnp.concatenate([state_win.astype(win_s.dtype), win_s], axis=1)
    for l in range(N_B):
        qp, zp, gp = nsa_query_side(xp, b_norm_pre[l], b_w_in[l])
        op = nsa_attend_prompt(qp, kc_p, vc_p, ks_p, vs_p, win_p[:, :, 0], win_p[:, :, 1], rel_bias)
        xp = nsa_output(xp, op, zp, gp, b_w_out[l], b_norm_post[l])
        qs, zs, gs = nsa_query_side(xs, b_norm_pre[l], b_w_in[l])
        os_ = nsa_attend_sample(qs, kc_s, vc_s, ks_s, vs_s, win_all[:, :, 0], win_all[:, :, 1],
                                past_len, rel_bias)
        xs = nsa_output(xs, os_, zs, gs, b_w_out[l], b_norm_post[l])
    new_win_p = win_p[:, -min(WINDOW, t_prompt):]
    new_win_s = win_all[:, -min(WINDOW, win_all.shape[1]):]
    return (xp, xs, jnp.stack(conv_p), jnp.stack(conv_s), cmp_p, cmp_s, slc_p, slc_s, new_win_p, new_win_s)


_drawn_inputs = setup_inputs


def setup_inputs(seed=0):
    import zlib

    import numpy as np

    out = dict(_drawn_inputs(seed))
    spreads = {}
    factors = {'a_ln_b': 2.758}
    for name, (base, spread) in spreads.items():
        noise = np.random.default_rng([zlib.crc32(name.encode()), seed]).standard_normal(out[name].shape)
        drawn = base * np.exp(spread * noise) if base else spread * noise
        out[name] = __import__('jax').numpy.asarray(drawn.astype(out[name].dtype))
    for name, factor in factors.items():
        out[name] = (out[name] * factor).astype(out[name].dtype)
    return out
```

```python
import math
from contextlib import ExitStack

import numpy as np
import concourse.bass as bass
from concourse import mybir

F32 = mybir.dt.float32
I32 = mybir.dt.int32
ALU = mybir.AluOpType
ACT = mybir.ActivationFunctionType
AX = mybir.AxisListType

P = 128
D = 1024
KD = D // P
SEQ = 512
DB, DS = 8, 8
NS = DB * DS
NT = SEQ + NS
HT = NT // 2
TT = 5
W = 31
H, HD, KV, G = 16, 64, 4, 4
NBR = 3
PAST, PAGE = 256, 128
STRIDE = 16
NCP = SEQ // STRIDE - 1
NCS = PAST // STRIDE - 1
KS = PAST + DS
BUCKETS, MAXD = 32, 128
EPS = 1e-6
BIG = 1e30
QSCALE = -(HD ** -0.5)
NX = 640
CH = 256
RING = 6


def bucket_rows():
    n = np.maximum(SEQ - 1 - np.arange(SEQ), 0)
    exact = BUCKETS // 2
    nf = np.maximum(n, 1).astype(np.float32)
    large = exact + (np.log(nf / np.float32(exact)) / np.float32(math.log(MAXD / exact)) * (BUCKETS - exact)).astype(np.int32)
    bucket = np.where(n < exact, n, np.minimum(large, BUCKETS - 1))
    return (bucket[None, :] == np.arange(BUCKETS)[:, None]).astype(np.float32)


def build(nc, I, O):
    ctx = ExitStack()
    with ctx:
        arena = ctx.enter_context(nc.sbuf_tensor("arena", [P, 53150], F32))
        page_sb = ctx.enter_context(nc.sbuf_tensor("page_sb", [1, 2 * DB], I32))
        psum = ctx.enter_context(nc.psum_tensor("psum", [P, 8 * 512], F32))
        bias_dram = nc.dram_tensor("bias_line", [H, NX], F32, kind="Internal").ap()
        bias_copies = nc.dram_tensor("bias_copies", [H, P, NX], F32, kind="Internal").ap()
        gate_dram = nc.dram_tensor("gate_rows", [NBR * H, NS], F32, kind="Internal").ap()
        x1_dram = nc.dram_tensor("x1_rows", [NT, D], F32, kind="Internal").ap()

        def at(off, *dims, p0=0, p1=P):
            n = int(np.prod(dims))
            v = arena[p0:p1, off:off + n]
            if len(dims) == 1:
                return v
            names = "abcdef"[:len(dims)]
            return v.rearrange(f"p ({' '.join(names)}) -> p {' '.join(names)}",
                               **{c: d for c, d in zip(names[1:], dims[1:])})

        def pb(b, *dims, p0=0, p1=P):
            n = int(np.prod(dims))
            v = psum[p0:p1, b * 512:b * 512 + n]
            if len(dims) == 1:
                return v
            names = "abcdef"[:len(dims)]
            return v.rearrange(f"p ({' '.join(names)}) -> p {' '.join(names)}",
                               **{c: d for c, d in zip(names[1:], dims[1:])})

        def halves(b):
            return pb(b, 2, 512)[:, :, 0:HT]

        R_RING, R_H, R_C, R_Z, R_F, R_X, R_G = 0, 12288, 16896, 21504, 26112, 32880, 38000
        R_P = R_G + 11880
        ring = at(R_RING, RING, KD, CH)
        x_sb = at(R_X, TT, D)
        hT = at(R_H, KD, NT)
        xn_a = at(R_C, 2, D)
        state_rows = at(R_C + 2 * D, 2, D)
        junk_a = at(R_Z, D)
        rel_rows = at(R_Z + 1024, H, p1=BUCKETS)
        hot_rows = at(R_Z + 1040, SEQ, p1=BUCKETS)
        pe_rows = at(R_Z + 1552, 2, P, p1=16)
        line = at(R_Z + 1808, NX, p1=H)
        glu_p = at(R_F, KD, SEQ + W - 1)
        glu_s = at(R_F + KD * (SEQ + W - 1), KD, DB, DS + W - 1)
        conv = at(R_C, KD, NT)
        zA = at(R_Z, KD, NT)
        rstd_ln = at(R_H, NT)
        conv_out_p = at(R_H + 1024, D)
        conv_out_s = at(R_H + 2048, D)
        xn_b = at(R_F, 2, D)
        gpost_a = at(R_F + 2048, D)
        junk_b = at(R_F + 3072, D)
        scaled_b = at(R_F + 4096, D)
        uT = at(R_C, KD, NT)
        ctS = at(R_G, 8, 33, 16)
        ctP = at(R_G, 2, 8, KV, 32)
        cmp_rows = at(R_G + 2048, 2, 2, KV, 2 * HD)
        w1_sb = at(R_G + 4224, 16, 256)
        rows_ring = at(R_G + 8320, 2, KV, P)
        new_rows = at(R_G + 8320, KD, NS)
        vecT = at(R_G + 9344, KD, 37)
        ones = at(R_G + 9640, P)
        hid = at(R_G + 9768, 2, 480)
        R_S = R_G + 10728
        sg = at(R_S, 2, NT)
        vec_rows = at(R_S, D)
        cmp_rows_s = at(R_S, 512)
        hid_p = at(R_S + 512, 2, 124)
        wgate = at(R_S + 760, KD, 48)
        k_stage = at(R_Z, 2, TT, CH)
        gateT = at(R_Z + 2560, NT)
        gate_tb = at(R_Z + 3136, DS, DB)
        v_sb = at(R_F, 2, TT, CH)
        ktz = at(R_F + 2560, 2, KV, SEQ)
        qT = at(R_H, KD, NT)
        yT = at(R_Z, KD, NT)
        sz = at(R_G, NBR, G, SEQ)
        tb = at(R_G + 6144, 2, 2, SEQ)
        pt_sb = at(R_G + 8192, 4, SEQ)
        y_tmp = at(R_G + 10240, SEQ)
        qbd = at(R_G + 10752, DB, 2, HD)
        l_sb = at(R_X, 6, SEQ)
        szs = at(R_X + 3072, NBR, KD, NS)
        pc_sb = at(R_X + 4608, 4, P)
        cache_sb = at(R_C, 4, 2, 512)
        kts = at(R_G + 6144, 2, 2, KS)
        pts = at(R_G + 8192, 2, 3, P)
        vnew = at(R_G + 8960, 4, CH, p1=DS)
        ptc = at(R_H, DB, P, p1=4 * NCS)
        orc = at(R_H + 1024, DB, P)
        y_br = at(R_H + 2048, 2, KD, NS)
        orow = at(R_H + 3072, 2, P)
        x1_back = at(R_H, 2, D)
        gpost_b = at(R_H + 2 * D, D)
        junk_c = at(R_H + 3 * D, D)
        y_out = at(R_C, 2, D)
        small = [R_P]

        def keep(*dims):
            off = small[0]
            small[0] += int(np.prod(dims))
            return at(off, *dims)

        ident = keep(P)
        kc_s = keep(DB, 4 * NCS)
        vc_s = keep(DB, P)
        bs = keep(KS)
        bsc = keep(4 * NCS)
        kt_new = keep(2, 2, NS)
        kcbd = keep(2, 64)
        vcbd = keep(2, P)
        pe_sb = keep(2, 16)
        pecol = keep(4)
        ss, ms, sd, rs = (keep(8) for _ in range(4))
        mn, den, rden = (keep(8 + 6) for _ in range(3))
        w2_off = small[0]
        w2_sb = keep(2, 2, P)
        gR = at(w2_off, 4, NBR * H)
        gS = at(w2_off + 192, NBR, DB)
        e2 = at(w2_off + 216, 2, 55)
        gRr = at(w2_off + 326, 4, H)
        assert small[0] <= 53150, small[0]

        def sem(name):
            return ctx.enter_context(nc.semaphore(name))

        S = {n: sem(n) for n in """
            zeroed ident_ready ones_ready zeroes vec_in vec_ps vec_ready state_in bias_in early_mm line_part line_out
            sq_a ms_a sd_a xn_a_ready tr_a h_ready state_tr state_ready
            proj_a sg_ready glu_ready z_ready conv_step
            page_in w1_in pe_in pe_sb_ready pe_ready w2_in ct_tr ct_ready cs_mm pe_col hid_ready kc_mm kc_ready vc_mm vc_ready
            centred sqd stat_mm eps_ready std_ready lnx_ready lns_ready y_ready
            co_tr co_ready co_out new_packed late
            o_mm gpost_in sq_b ms_b sd_b o_scaled x1_ready sq_c ms_c sd_c xn_b_ready tr_b hu_ready x1_out
            kv_mm kv_ready kt_tr kt_ready ctp_tr ctp_ready kv_out cp_mm hidp_ready cpp_mm bd_ready
            q_mm q_ready wg_in gate_mm gate_ready gate_tr gR_ready gate_out gS_in qbd_ready
            z_mm zb_ready bs_in bsc_ready
            e2_ready s_done l_ready cmin_ready exp_done den_ready pn_ready
            t_done pt_a pt_d pv_done y_mul y_add
            skt_tr skt_ready kts_new ss_mm sl_ready se_ready sp_ready st_tr pts_ready so_mm or_ready ot_tr ys_mul y_s
            fo_mm fy
            """.split()}
        ZEROED = {"pad": 1, "slot": 2, "blocks": 4, "bias": 5, "keys": 9, "probs": 10, "table": 11, "queries": 12}
        w_in = [sem(f"w_in{i}") for i in range(RING)]
        x_in = [sem(f"x_in{i}") for i in range(TT)]
        rows_in = [sem(f"rows_in{i}") for i in range(2)]
        tb_in = [sem(f"tb_in{i}") for i in range(2)]
        cache_in = [sem(f"cache_in{i}") for i in range(4)]
        vnew_in = [sem(f"vnew_in{i}") for i in range(4)]
        fy_out = [sem(f"fy_out{i}") for i in range(2)]
        dve_step = sem("dve_step")
        n_dve = [0]

        def link(dve, ins):
            n_dve[0] += 1
            ins.then_inc(dve_step, 1)
            dve.wait_ge(dve_step, n_dve[0])

        def cols(w, c0):
            return [(w[:, c0:c0 + CH].rearrange("(k p) n -> p k n", p=P), None)]

        def paired(w, c0, p, e):
            parts = []
            for half in range(2):
                for g in range(2):
                    c = c0 + p * 512 + half * 256 + (2 * e + g) * HD
                    parts.append((w[:, c:c + HD].rearrange("(k p) n -> p k n", p=P), (2 * g + half) * HD))
            return parts

        a_w = I["a_w_in"][0]
        b_w = I["b_w_in"][0]
        chunks = []
        for c in range(4):
            chunks += [cols(a_w, c * CH), cols(a_w, D + c * CH), cols(a_w, 2 * D + c * CH)]
        C_OA = len(chunks)
        chunks += [cols(I["a_w_out"][0], c * CH) for c in range(4)]
        C_KV = len(chunks)
        chunks += [cols(I["w_kv"], c * CH) for c in range(6)]
        C_Q = len(chunks)
        chunks += [paired(b_w, 0, p, e) for p in range(2) for e in range(2)]
        C_Z = len(chunks)
        chunks += [paired(b_w, D * (1 + br), p, e) for p in range(2) for br in range(NBR) for e in range(2)]
        C_OB = len(chunks)
        for c in range(4):
            parts = []
            for p in range(2):
                for half in range(2):
                    r = p * 512 + half * 256
                    parts.append((I["b_w_out"][0][r:r + 256, c * CH:(c + 1) * CH].rearrange("(g d) n -> d g n", d=HD),
                                  ("out", p, half)))
            chunks.append(parts)

        last_use = {}
        for n in range(12):
            last_use[n] = ("proj_a", 3 * (2 * (n // 3) + 1) + n % 3 + 1)
            last_use[C_Z + n] = ("z_mm", 4 * (n // 2) + 2 * (n % 2) + 2 if n < 6 else 12 + 3 * (2 * (n % 2) + 1) + (n - 6) // 2 + 1)
        for n in range(4):
            last_use[C_OA + n] = ("o_mm", TT)
            last_use[C_Q + n] = ("q_mm", 2 * (n + 1))
        for n in range(6):
            last_use[C_KV + n] = ("kv_mm", TT * (n + 1))

        def chunk_dst(c, how):
            slot = ring[:, c % RING]
            if how is None:
                return slot
            if isinstance(how, tuple):
                _, p, half = how
                return slot[half * HD:half * HD + HD, 4 * p:4 * p + 4, :]
            return slot[:, :, how:how + HD]

        arrived, totals = {}, [0] * RING
        for c, parts in enumerate(chunks):
            totals[c % RING] += 16 * len(parts)
            arrived[c] = totals[c % RING]

        def rows(t):
            return P if t < 4 else NS

        UPM = 1 + 2 * 2 * 4
        items = []
        for m in range(KD):
            items.append((m, 0, None, [UPM * m]))
            for br in (1, 2):
                for i in range(4):
                    u = UPM * m + 1 + 8 * (br - 1) + 2 * i
                    items.append((m, br, i, [u, u + 1]))
        item_of = {u: w for w, it in enumerate(items) for u in it[3]}
        pt_by, n_a, n_d = {}, 0, 0
        for w, (m, br, i, us) in enumerate(items):
            for k, u in enumerate(us):
                if br and k == 0:
                    n_a += 1
                    pt_by[u] = ("pt_a", n_a)
                else:
                    n_d += 1
                    pt_by[u] = ("pt_d", n_d)
        N_UNITS = UPM * KD
        KV_OUT = 16 * (2 * 5 + 2 * 2 + 2 * (1 + DB))

        def stat(w):
            return 8 + 2 * (w % 3)

        z_jobs = [(0, br, g) for br in range(NBR) for g in range(G)] + [(1, br, g) for g in range(G) for br in range(NBR)]
        z_at = {9 * (g + 1) + 1 + 2 * br: 12 + 3 * g + br for g in range(G) for br in range(NBR)}

        block = ctx.enter_context(nc.Block())

        @block.sync
        def _(sp):
            for t in range(TT):
                src = I["x_prompt"][0, t * P:(t + 1) * P, :] if t < 4 else I["x_sample"].rearrange("b t d -> (b t) d")
                sp.dma_start(x_sb[0:rows(t), t], src).then_inc(x_in[t], 16)

            def tables(m):
                if m < 2:
                    sp.wait_ge(S["line_out"], 32)
                    sp.wait_ge(S["cp_mm"], 4)
                else:
                    sp.wait_ge(S["e2_ready"], m - 1)
                    sp.wait_ge(S["l_ready"], UPM * (m - 1))
                for half in range(2):
                    h = 8 * (m // 4) + 4 * half + m % 4
                    src = bass.AP(bias_copies.tensor, h * P * NX + P - 1, [[NX - 1, P], [1, SEQ]])
                    sp.dma_start(tb[:, m % 2, half], src).then_inc(tb_in[m % 2], 16)

            for c, parts in enumerate(chunks):
                if c in (C_OB, C_OB + 1):
                    tables(2 * (c - C_OB) + 2)
                    tables(2 * (c - C_OB) + 3)
                if c >= RING:
                    name, count = last_use[c - RING]
                    sp.wait_ge(S[name], count)
                for src, how in parts:
                    sp.dma_start(chunk_dst(c, how), src).then_inc(w_in[c % RING], 16)
                if c == 2:
                    sp.dma_start(w1_sb, I["cmp_w1"][0].rearrange("(j p) n -> p j n", p=P)).then_inc(S["w1_in"], 16)
                if c == C_OA + 3:
                    sp.wait_ge(S["cs_mm"], 2)
                    sp.dma_start(w1_sb, I["cmp_w1"][1].rearrange("(j p) n -> p j n", p=P)).then_inc(S["w1_in"], 16)
                if c == C_Q + 3:
                    sp.wait_ge(S["cp_mm"], 2)
                    sp.dma_start(w1_sb, I["cmp_w1"][0].rearrange("(j p) n -> p j n", p=P)).then_inc(S["w1_in"], 16)
                if c == C_Z + 5:
                    tables(0)
                    tables(1)
            for m in range(6, KD):
                tables(m)
            sp.wait_ge(S["z_mm"], 24)
            sp.wait_ge(S["page_in"], 16)
            for n in range(2 * DB):
                b, br = n // 2, n % 2
                if n >= 4:
                    sp.wait_ge(S["so_mm"], n - 2)
                if br == 0:
                    for pg in range(2):
                        v = sp.value_load(page_sb[0:1, 2 * b + pg:2 * b + pg + 1], min_val=0, max_val=I["cache_slc"].shape[0] - 1)
                        src = I["cache_slc"].rearrange("g s c k d -> g s (c k d)")[bass.ds(v, 1), :, :]
                        sp.dma_start(cache_sb[:, n % 4, pg], src.rearrange("a s n -> (a s) n")).then_inc(cache_in[n % 4], 16)
                else:
                    for pg in range(2):
                        src = I["state_win"][b, pg * P:(pg + 1) * P].rearrange("s c k d -> s (c k d)")
                        sp.dma_start(cache_sb[:, n % 4, pg], src).then_inc(cache_in[n % 4], 16)
                if n == 0:
                    sp.wait_ge(S["pv_done"], len(items))
                sp.dma_start(vnew[:, n % 4], v_sb[DS * b:DS * b + DS, br, 4, :]).then_inc(vnew_in[n % 4], 16)
            sp.wait_ge(S["x1_out"], 16 * TT)
            sp.wait_ge(S["y_s"], 2)
            for t in range(TT):
                if t >= 2:
                    sp.wait_ge(S["fy"], t - 1)
                sp.dma_start(x1_back[0:rows(t), t % 2], x1_dram[t * P:t * P + rows(t), :]).then_inc(x_in[t % 2], 16)
            for t in range(2):
                sp.wait_ge(x_in[t], 16 * (4 - t))

        @block.gpsimd
        def _(pool):
            pool.dma_start(page_sb[:, :], I["page_table"].rearrange("b (g a) -> a (b g)", a=1)).then_inc(S["page_in"], 16)
            pool.memset(ident, 0.0).then_inc(S["zeroed"], 1)
            pool.wait_ge(S["zeroed"], 1)
            pool.affine_select(out=ident, in_=ident, compare_op=ALU.not_equal, fill=1.0, base=0,
                               pattern=[[-1, P]], channel_multiplier=1).then_inc(S["ident_ready"], 1)
            pool.memset(line[:, SEQ:NX], BIG).then_inc(S["line_part"], 1)
            pool.memset(ones, 1.0 / D).then_inc(S["ones_ready"], 1)
            pool.memset(glu_p[:, :, 0:W - 1], 0.0).then_inc(S["zeroes"], 1)
            pool.memset(ctS[:, :, 32, :], 0.0).then_inc(S["zeroes"], 1)
            pool.memset(kcbd, 0.0).then_inc(S["zeroes"], 1)
            pool.memset(vcbd, 0.0).then_inc(S["zeroes"], 1)
            pool.memset(bsc, BIG).then_inc(S["zeroes"], 1)
            pool.wait_ge(S["page_in"], 16)
            cache = I["cache_cmp"].rearrange("g (s a) c k d -> g s a c k d", a=2)
            for c in range(2):
                for b in range(DB):
                    n = DB * c + b
                    if n >= 2:
                        pool.wait_ge(S["ct_tr"], n - 1)
                    for pg in range(2):
                        v = pool.value_load(page_sb[0:1, 2 * b + pg:2 * b + pg + 1], min_val=0, max_val=I["cache_cmp"].shape[0] - 1)
                        for par in range(2):
                            src = cache[bass.ds(v, 1), :, par, c, :, :]
                            pool.dma_start(rows_ring[pg * 64:pg * 64 + 64, n % 2, :, par * HD:(par + 1) * HD],
                                           src.rearrange("g s k d -> (g s) k d")).then_inc(rows_in[n % 2], 16)
            pool.dma_start(O["conv_sample"][0, :, 0:W - 1 - DS, :], I["state_conv"][0, :, DS:W - 1, :]).then_inc(S["late"], 16)
            pool.dma_start(O["win_sample"][:, 0:PAST], I["state_win"]).then_inc(S["late"], 16)
            pool.wait_ge(S["z_ready"], KD)
            for m in range(KD):
                pool.wait_ge(S["lns_ready"], m + 1)
                pool.tensor_tensor(out=zA[:, m], in0=conv[:, m], in1=zA[:, m], op=ALU.mult).then_inc(S["y_ready"], 1)
            pool.wait_ge(S["tr_b"], TT)
            pool.wait_ge(S["x1_ready"], TT)
            pool.wait_ge(S["sq_c"], TT)
            for lo in range(2):
                for br in range(2):
                    pool.memset(ktz[64 - 64 * lo:P - 64 * lo, br, lo:KV:2, :], 0.0).then_inc(S["zeroes"], 1)
            pool.wait_ge(S["x1_out"], 16 * TT)
            pool.wait_ge(S["xn_b_ready"], TT)
            pool.wait_ge(S["zeroes"], ZEROED["keys"])
            pool.memset(pc_sb, 0.0).then_inc(S["zeroes"], 1)
            pool.wait_ge(S["cpp_mm"], 2)
            pool.wait_ge(S["gate_mm"], 1)
            pool.wait_ge(S["kv_out"], KV_OUT)
            pool.memset(e2, BIG).then_inc(S["zeroes"], 1)
            pool.memset(qbd, 0.0).then_inc(S["zeroes"], 1)
            pool.wait_ge(S["gR_ready"], 5)
            for w in range(len(items) + 3):
                if w < len(items):
                    m, br, i, us = items[w]
                    pool.wait_ge(S["den_ready"], w + 1)
                    if br == 0:
                        if m == 0:
                            pool.wait_ge(S["zeroes"], ZEROED["probs"])
                        else:
                            pool.wait_ge(S["t_done"], UPM * (m - 1) + 1)
                        dst = pc_sb[:, :, 0:64].rearrange("q i (h n) -> q i h n", h=2)[:, :, :, 0:NCP]
                        src = l_sb[:, us[0] % 6, 0:8 * NCP].rearrange("q (i h n) -> q i h n", i=4, h=2)
                        r = rden[:, 0:8].rearrange("q (i h) -> q i h", i=4).unsqueeze(3).broadcast_to([P, 4, 2, NCP])
                        pool.tensor_tensor(out=dst, in0=src, in1=r, op=ALU.mult).then_inc(S["pn_ready"], 1)
                    else:
                        for half, u in enumerate(us):
                            h = br * H + 8 * (m // 4) + 4 * half + m % 4
                            L = l_sb[:, u % 6, 0:P * (i + 1)]
                            pool.tensor_scalar(L, L, rden[:, stat(w) + half:stat(w) + half + 1], gR[:, i, h:h + 1],
                                               ALU.mult, ALU.mult).then_inc(S["pn_ready"], 1)
                if w >= 3 and items[w - 3][1] and items[w - 3][2] == 3:
                    m, br = items[w - 3][:2]
                    pool.wait_ge(S["y_mul"], 3 * m + br + 1)
                    if br == 2:
                        pool.wait_ge(S["y_add"], 2 * m + 1)
                    pool.tensor_tensor(out=yT[:, m, 0:SEQ], in0=yT[:, m, 0:SEQ], in1=y_tmp, op=ALU.add).then_inc(S["y_add"], 1)
            for n in range(2 * DB):
                b, br = n // 2, n % 2
                if n >= 2:
                    pool.wait_ge(S["ss_mm"], n)
                else:
                    pool.wait_ge(S["l_ready"], N_UNITS)
                pool.tensor_copy(kts[:, n % 2, :, PAST:KS], kt_new[:, br, :, DS * b:DS * b + DS]).then_inc(S["kts_new"], 1)

        @block.scalar
        def _(act):
            def copy(out, in_, scale=1.0):
                return nc.scalar.activation(out, in_, ACT.Copy, scale=scale)

            act.dma_start(vec_rows[0:W], I["a_conv_w"][0]).then_inc(S["vec_in"], 16)
            for n, name in enumerate(("a_norm_pre", "a_conv_b", "a_ln_g", "a_ln_b", "kv_norm", "b_norm_pre")):
                src = I[name].rearrange("(a n) -> a n", a=1) if name == "kv_norm" else I[name]
                act.dma_start(vec_rows[W + n:W + n + 1], src).then_inc(S["vec_in"], 16)
            act.dma_start(rel_rows, I["rel_bias"]).then_inc(S["bias_in"], 16)
            act.dma_start(hot_rows, I["bucket_rows"]).then_inc(S["bias_in"], 16)
            for c in range(2):
                act.dma_start(pe_rows[:, c], I["cmp_pe"][c].rearrange("(j a) d -> j (a d)", a=2)).then_inc(S["pe_in"], 16)
            for i in range(2):
                act.dma_start(state_rows[0:120, i], I["state_conv"][0, 4 * i:4 * i + 4].rearrange("b r n -> (b r) n")).then_inc(S["state_in"], 16)
            for c in range(2):
                for ht in range(2):
                    for dup in range(2):
                        act.dma_start(w2_sb[:, c, ht, dup * HD:(dup + 1) * HD], I["cmp_w2"][c, ht * P:(ht + 1) * P, :]).then_inc(S["w2_in"], 16)
            for t in range(TT):
                r = rows(t)
                act.wait_ge(x_in[t], 16)
                if t:
                    act.wait_ge(S["sq_a"], t)
                nc.scalar.activation(junk_a[0:r], x_sb[0:r, t], ACT.Square, accum_out=ss[0:r, t:t + 1]).then_inc(S["sq_a"], 1)
            for t in range(TT):
                r = rows(t)
                act.wait_ge(S["ms_a"], t + 1)
                nc.scalar.activation(sd[0:r, t:t + 1], ms[0:r, t:t + 1], ACT.Sqrt).then_inc(S["sd_a"], 1)
            act.wait_ge(S["early_mm"], 1)
            copy(line[:, 0:SEQ], pb(0, SEQ, p1=H), -1.0).then_inc(S["line_part"], 1)
            act.wait_ge(S["line_part"], 2)
            act.dma_start(bias_dram, line).then_inc(S["line_out"], 16)
            act.wait_ge(S["line_out"], 16)
            act.dma_start(bias_copies, bias_dram.unsqueeze(1).broadcast_to([H, P, NX])).then_inc(S["line_out"], 16)
            act.wait_ge(S["line_out"], 32)
            act.dma_start(bs, bass.AP(bias_copies.tensor, SEQ - 1 - PAST, [[P * NX, H], [NX - 1, DS], [1, KS]])).then_inc(S["bs_in"], 16)
            act.wait_ge(S["early_mm"], 2)
            copy(pe_sb, pb(1, 2, 16)).then_inc(S["pe_sb_ready"], 1)
            act.wait_ge(S["pe_sb_ready"], 1)
            act.wait_ge(S["zeroes"], ZEROED["slot"])

            def pe_slot(c):
                copy(ctS[:, :, 32, 0:2].rearrange("p j c -> p c j"), pe_sb[:, c].rearrange("p (c j) -> p c j", c=2)).then_inc(S["pe_ready"], 1)

            pe_slot(0)
            for n in range(4):
                i, mg = n // 2, n % 2
                act.wait_ge(S["state_tr"], n + 1)
                for b in range(4):
                    copy(glu_s[:, 4 * mg:4 * mg + 4, 4 * i + b, 0:W - 1],
                         pb(6 + n % 2, 4, 120)[:, :, b * (W - 1):(b + 1) * (W - 1)]).then_inc(S["state_ready"], 1)

            def ct_copy(n):
                b = n % DB
                act.wait_ge(S["ct_tr"], n + 1)
                copy(ctS[:, :, KV * b:KV * b + KV, :].rearrange("p j s c -> p s c j"), pb(6 + n % 2, KV, 16, 8)).then_inc(S["ct_ready"], 1)

            for m in range(KD):
                act.wait_ge(S["proj_a"], 3 * m + 2)
                if m >= 2:
                    act.wait_ge(S["glu_ready"], 3 * (m - 1))
                else:
                    act.wait_ge(S["vec_ps"], 1)
                nc.scalar.activation(sg[:, m % 2].rearrange("p (a n) -> p a n", a=2), halves(2), ACT.Sigmoid).then_inc(S["sg_ready"], 1)
                ct_copy(m)
                act.wait_ge(S["proj_a"], 3 * m + 3)
                if m == 0:
                    act.wait_ge(S["sq_a"], TT)
                nc.scalar.activation(zA[:, m].rearrange("p (a n) -> p a n", a=2), halves(4), ACT.Silu).then_inc(S["z_ready"], 1)

            def compress_silu(c):
                for ht in range(2):
                    act.wait_ge(S["cs_mm"], 2 * c + ht + 1)
                    copy(pecol[:, 2 * c + ht:2 * c + ht + 1], pb(6 + ht, 495)[:, 480:481]).then_inc(S["pe_col"], 1)
                    act.wait_ge(S["pe_col"], 2 * c + ht + 1)
                    if c:
                        act.wait_ge(S["kc_mm"], 1)
                    nc.scalar.activation(hid[:, ht], pb(6 + ht, 480), ACT.Silu, bias=pecol[:, 2 * c + ht:2 * c + ht + 1]).then_inc(S["hid_ready"], 1)

            act.wait_ge(S["glu_ready"], 3 * KD)
            for m in range(KD):
                act.wait_ge(S["centred"], m + 1)
                if m >= 2:
                    act.wait_ge(S["stat_mm"], m)
                nc.scalar.activation(sg[:, m % 2], conv[:, m], ACT.Square).then_inc(S["sqd"], 1)
            compress_silu(0)
            act.wait_ge(S["eps_ready"], 1)
            nc.scalar.activation(rstd_ln, rstd_ln, ACT.Sqrt).then_inc(S["std_ready"], 1)
            act.wait_ge(S["kc_mm"], 1)
            copy(kc_s.rearrange("p b n -> p (b n)"), pb(4, 480)).then_inc(S["kc_ready"], 1)
            pe_slot(1)
            for m in range(KD):
                act.wait_ge(S["lnx_ready"], m + 1)
                nc.scalar.activation(conv[:, m], conv[:, m], ACT.Silu, scale=vecT[:, m, W + 2:W + 3],
                                     bias=vecT[:, m, W + 3:W + 4]).then_inc(S["lns_ready"], 1)
                ct_copy(DB + m)
            compress_silu(1)
            act.wait_ge(S["vc_mm"], 1)
            copy(vc_s[0:60].rearrange("p b n -> p (b n)"), pb(4, 1024, p1=60)).then_inc(S["vc_ready"], 1)
            act.wait_ge(S["co_tr"], 1)
            copy(conv_out_p[0:W - 1], pb(0, D, p1=W - 1)).then_inc(S["co_ready"], 1)
            act.wait_ge(S["co_tr"], 2)
            copy(conv_out_s[0:NS], pb(2, D, p1=NS)).then_inc(S["co_ready"], 1)
            act.wait_ge(S["co_ready"], 2)
            act.dma_start(O["conv_prompt"][0, 0], conv_out_p[0:W - 1]).then_inc(S["co_out"], 16)
            for b in range(DB):
                act.dma_start(O["conv_sample"][0, b, W - 1 - DS:W - 1], conv_out_s[DS * b:DS * b + DS]).then_inc(S["co_out"], 16)
            act.dma_start(gpost_a, I["a_norm_post"][0:1, :].broadcast_to([P, D])).then_inc(S["gpost_in"], 16)

            for t in range(TT):
                r = rows(t)
                act.wait_ge(S["o_mm"], t + 1)
                if t:
                    act.wait_ge(S["sq_c"], t)
                    act.wait_ge(S["o_scaled"], t)
                nc.scalar.activation(junk_b[0:r], pb(2 * (t % 2), D, p1=r), ACT.Square, accum_out=ss[0:r, 0:1]).then_inc(S["sq_b"], 1)
                act.wait_ge(S["ms_b"], t + 1)
                nc.scalar.activation(sd[0:r, 0:1], ms[0:r, 0:1], ACT.Sqrt).then_inc(S["sd_b"], 1)
                act.wait_ge(S["x1_ready"], t + 1)
                act.dma_start(x1_dram[t * P:t * P + r, :], x_sb[0:r, t]).then_inc(S["x1_out"], 16)
                act.wait_ge(S["sq_b"], t + 1)
                nc.scalar.activation(junk_b[0:r], x_sb[0:r, t], ACT.Square, accum_out=ss[0:r, 1:2]).then_inc(S["sq_c"], 1)
                act.wait_ge(S["ms_c"], t + 1)
                nc.scalar.activation(sd[0:r, 1:2], ms[0:r, 1:2], ACT.Sqrt).then_inc(S["sd_c"], 1)

            act.wait_ge(S["vc_mm"], 1)
            act.dma_start(wgate, b_w[:, 4 * D:4 * D + 48].rearrange("(k p) n -> p k n", p=P)).then_inc(S["wg_in"], 16)
            for c in range(6):
                br, kind = c // 2, c % 2
                for t in range(TT):
                    n = TT * c + t
                    r = rows(t)
                    act.wait_ge(S["kv_mm"], n + 1)
                    src = pb(n % 6, CH, p1=r)
                    if br == 0 and t < 4:
                        dst = cmp_rows[:, t // 2, kind, :, HD * (t % 2):HD * (t % 2) + HD]
                        src = src.rearrange("p (k d) -> p k d", d=HD)
                    elif br == 0:
                        dst = cmp_rows_s[0:r, kind * CH:(kind + 1) * CH]
                    else:
                        dst = (v_sb if kind else k_stage)[0:r, br - 1, t]
                    copy(dst, src).then_inc(S["kv_ready"], 1)
                act.wait_ge(S["kv_ready"], TT * (c + 1))
                if br == 0:
                    for gi in range(2):
                        for par in range(2):
                            dst = O["cmp_prompt"][0, gi * 256:(gi + 1) * 256, kind].rearrange("(q a) k d -> q a k d", a=2)[:, par]
                            act.dma_start(dst, cmp_rows[:, gi, kind, :, par * HD:par * HD + HD]).then_inc(S["kv_out"], 16)
                    act.dma_start(O["cmp_sample"][:, :, kind].rearrange("b t k d -> (b t) (k d)"),
                                  cmp_rows_s[0:NS, kind * CH:(kind + 1) * CH]).then_inc(S["kv_out"], 16)
                    continue
                name, R = ("slc", "win")[br - 1], (v_sb if kind else k_stage)
                dst = O[name + "_prompt"][0, :, kind].rearrange("(t p) k d -> p t (k d)", p=P)
                act.dma_start(dst, R[:, br - 1, 0:4]).then_inc(S["kv_out"], 16)
                if br == 1:
                    act.dma_start(O["slc_sample"][:, :, kind].rearrange("b t k d -> (b t) (k d)"), R[0:NS, 0, 4]).then_inc(S["kv_out"], 16)
                    continue
                for b in range(DB):
                    act.dma_start(O["win_sample"][b, PAST:KS, kind].rearrange("t k d -> t (k d)"),
                                  R[DS * b:DS * b + DS, 1, 4]).then_inc(S["kv_out"], 16)
            def compress_p_silu(n, c):
                for ht in range(2):
                    act.wait_ge(S["cp_mm"], 2 * n + ht + 1)
                    if n:
                        act.wait_ge(S["cpp_mm"], 1)
                    nc.scalar.activation(hid_p[:, ht], pb(4 + ht, 124), ACT.Silu, bias=pecol[:, 2 * c + ht:2 * c + ht + 1]).then_inc(S["hidp_ready"], 1)
                act.wait_ge(S["cpp_mm"], n + 1)
                act.wait_ge(S["zeroes"], ZEROED["blocks"])
                for p in range(2):
                    for half in range(2):
                        lo = HD * half
                        if c:
                            copy(vcbd[32 * half:32 * half + NCP, p, lo:lo + HD],
                                 pb(2 + p, HD, p0=32 * half, p1=32 * half + NCP)).then_inc(S["bd_ready"], 1)
                        else:
                            copy(kcbd[lo:lo + HD, p, 32 * half:32 * half + NCP],
                                 pb(0, KV, NCP, p0=lo, p1=lo + HD)[:, 2 * p + half]).then_inc(S["bd_ready"], 1)

            compress_p_silu(0, 1)
            for m in range(KD):
                act.wait_ge(S["q_mm"], m + 1)
                copy(qT[:, m].rearrange("p (a n) -> p a n", a=2), halves(2 * (m % 3)), QSCALE).then_inc(S["q_ready"], 1)
            act.wait_ge(S["gate_mm"], 1)
            nc.scalar.activation(gateT[0:48].rearrange("p (a n) -> p a n", a=2), halves(6)[0:48], ACT.Sigmoid).then_inc(S["gate_ready"], 1)
            act.wait_ge(S["gate_ready"], 1)
            copy(gate_tb[0:48], gateT[0:48, SEQ:NT].rearrange("r (b t) -> r t b", b=DB)).then_inc(S["gate_ready"], 1)
            act.wait_ge(S["gate_ready"], 2)
            act.dma_start(gate_dram, gate_tb[0:48].rearrange("r t b -> r (t b)")).then_inc(S["gate_out"], 16)
            compress_p_silu(1, 0)
            act.wait_ge(S["gate_out"], 16)
            for br in range(NBR):
                act.dma_start(gS[:, br], bass.AP(gate_dram.tensor, br * H * NS, [[DB, P], [1, DB]])).then_inc(S["gS_in"], 16)

            def z_silu(n, b0):
                p, br, g = z_jobs[n]
                act.wait_ge(S["z_mm"], n + 1)
                if p:
                    act.wait_ge(S["y_mul"], 3 * (g + 1))
                lo, hi = pb(b0, HT), pb(b0 + 1, HT)
                nc.scalar.activation(sz[:, br, g, 0:HT], lo, ACT.Silu).then_inc(S["zb_ready"], 1)
                nc.scalar.activation(sz[:, br, g, HT:SEQ], hi[:, 0:SEQ - HT], ACT.Silu).then_inc(S["zb_ready"], 1)
                nc.scalar.activation(szs[:, br, 4 * p + g], hi[:, SEQ - HT:HT], ACT.Silu).then_inc(S["zb_ready"], 1)

            act.wait_ge(S["x1_out"], 16 * TT)
            act.wait_ge(S["cp_mm"], 4)
            act.wait_ge(S["kv_out"], KV_OUT)
            for n in range(12):
                z_silu(n, 2 * (n % 2))

            for w in range(len(items) + 2):
                if w < len(items):
                    m, br, i, us = items[w]
                    act.wait_ge(S["l_ready"], us[-1] + 1)
                    if br == 0:
                        act.wait_ge(S["cmin_ready"], m + 1)
                        L = l_sb[:, us[0] % 6, 0:8 * NCP]
                        nc.scalar.activation(L, L, ACT.Exp, scale=-1.0).then_inc(S["exp_done"], 1)
                    else:
                        if w >= 3:
                            act.wait_ge(S["den_ready"], w - 2)
                        for half, u in enumerate(us):
                            L = l_sb[:, u % 6, 0:P * (i + 1)]
                            k = stat(w) + half
                            nc.scalar.activation(L, L, ACT.Exp, scale=-1.0, bias=mn[:, k:k + 1],
                                                 accum_out=den[:, k:k + 1]).then_inc(S["exp_done"], 1)
                if w >= 2 and items[w - 2][1]:
                    i, u = items[w - 2][2], items[w - 2][3][0]
                    act.wait_ge(S["t_done"], u + 1)
                    if u >= 4:
                        act.wait_ge(S["pv_done"], item_of[u - 4] + 1)
                    copy(pt_sb[:, u % 4, 0:P * (i + 1)], pb(3 + u % 2, P * (i + 1))).then_inc(S["pt_a"], 1)
                if w in z_at:
                    z_silu(z_at[w], 6)

            act.wait_ge(S["cmin_ready"], KD + 1)
            L = l_sb[:, 0, 0:480]
            nc.scalar.activation(L, L, ACT.Exp, scale=-1.0).then_inc(S["exp_done"], 1)
            for n in range(2 * DB + 1):
                if n < 2 * DB:
                    act.wait_ge(S["skt_tr"], n + 1)
                    if n >= 2:
                        act.wait_ge(S["ss_mm"], n)
                    act.wait_ge(S["l_ready"], N_UNITS)
                    copy(kts[:, n % 2, :, 0:PAST], pb(n % 2, 2, PAST)).then_inc(S["skt_ready"], 1)
                if n >= 1:
                    k = n - 1
                    act.wait_ge(S["sl_ready"], k + 2)
                    if k >= 4:
                        act.wait_ge(S["sp_ready"], k - 2)
                    L = l_sb[:, 1 + k % 3, 0:KS]
                    nc.scalar.activation(L, L, ACT.Exp, scale=-1.0, bias=mn[:, 8 + k % 4:9 + k % 4],
                                         accum_out=den[:, 8 + k % 4:9 + k % 4]).then_inc(S["se_ready"], 1)
            act.wait_ge(S["y_s"], 2)
            act.dma_start(gpost_b, I["b_norm_post"][0:1, :].broadcast_to([P, D])).then_inc(S["gpost_in"], 16)
            for t in range(TT):
                r = rows(t)
                act.wait_ge(S["fo_mm"], t + 1)
                if t:
                    act.wait_ge(S["sq_a"], TT + t)
                nc.scalar.activation(junk_c[0:r], pb(2 * (t % 2), D, p1=r), ACT.Square, accum_out=ss[0:r, t:t + 1]).then_inc(S["sq_a"], 1)
                act.wait_ge(S["ms_a"], TT + t + 1)
                nc.scalar.activation(sd[0:r, t:t + 1], ms[0:r, t:t + 1], ACT.Sqrt).then_inc(S["sd_a"], 1)
                act.wait_ge(S["fy"], t + 1)
                dst = O["y_prompt"][0, t * P:(t + 1) * P] if t < 4 else O["y_sample"].rearrange("b t d -> (b t) d")
                act.dma_start(dst, y_out[0:r, t % 2]).then_inc(fy_out[t % 2], 16)
            act.wait_ge(fy_out[0], 16 * 3)
            act.wait_ge(fy_out[1], 16 * 2)
            act.wait_ge(S["co_out"], 16 * (1 + DB))
            act.wait_ge(S["late"], 32)

        @block.vector
        def _(dve):
            V = nc.vector
            dve.wait_ge(S["vec_ps"], 1)
            V.tensor_copy(vecT, pb(2, KD, 37)).then_inc(S["vec_ready"], 1)
            dve.wait_ge(S["vec_ready"], 1)

            def mean_sq(col, r, name):
                V.tensor_scalar(ms[0:r, col:col + 1], ss[0:r, col:col + 1], 1.0 / D, EPS, ALU.mult, ALU.add).then_inc(S[name], 1)

            def gain(k, r):
                return vecT[:, :, W + k:W + k + 1].broadcast_to([P, KD, r])

            for t in range(TT):
                dve.wait_ge(S["sq_a"], t + 1)
                mean_sq(t, rows(t), "ms_a")
            for t in range(TT + 1):
                if t < TT:
                    r = rows(t)
                    dve.wait_ge(S["sd_a"], t + 1)
                    link(dve, V.reciprocal(rs[0:r, t:t + 1], sd[0:r, t:t + 1]))
                    if t >= 2:
                        dve.wait_ge(S["tr_a"], t - 1)
                    V.tensor_scalar(xn_a[0:r, t % 2], x_sb[0:r, t], rs[0:r, t:t + 1], None, ALU.mult).then_inc(S["xn_a_ready"], 1)
                if t:
                    k, r = t - 1, rows(t - 1)
                    dve.wait_ge(S["tr_a"], k + 1)
                    V.tensor_tensor(out=hT[:, :, k * P:k * P + r], in0=pb(4 + 2 * (k % 2), KD, P)[:, :, 0:r], in1=gain(0, r),
                                    op=ALU.mult).then_inc(S["h_ready"], 1)
            dve.wait_ge(S["bs_in"], 16)
            dve.wait_ge(S["zeroes"], ZEROED["bias"])
            for kv in range(KV):
                V.tensor_copy(bsc[32 * kv:32 * kv + 32, NCS * kv:NCS * (kv + 1)],
                              bs[32 * kv:32 * kv + 32, 31:31 + 16 * (NCS - 1) + 1:16]).then_inc(S["bsc_ready"], 1)

            dve.wait_ge(S["zeroes"], ZEROED["pad"])
            dve.wait_ge(S["state_ready"], 16)
            for m in range(KD):
                dve.wait_ge(S["proj_a"], 3 * m + 2)
                dve.wait_ge(S["sg_ready"], m + 1)
                a, g = pb(0, 1024), sg[:, m % 2]
                V.tensor_tensor(out=glu_p[:, m, W - 1:W - 1 + HT], in0=a[:, 0:HT], in1=g[:, 0:HT], op=ALU.mult).then_inc(S["glu_ready"], 1)
                V.tensor_tensor(out=glu_p[:, m, W - 1 + HT:W - 1 + SEQ], in0=a[:, 512:512 + SEQ - HT], in1=g[:, HT:SEQ],
                                op=ALU.mult).then_inc(S["glu_ready"], 1)
                V.tensor_tensor(out=glu_s[:, m, :, W - 1:W - 1 + DS],
                                in0=a[:, 512 + SEQ - HT:512 + HT].rearrange("p (b t) -> p b t", b=DB),
                                in1=g[:, SEQ:NT].rearrange("p (b t) -> p b t", b=DB), op=ALU.mult).then_inc(S["glu_ready"], 1)
                dve.wait_ge(S["glu_ready"], 3 * (m + 1))
                for w in range(W):
                    tap = vecT[:, m, w:w + 1]
                    for part, (src, dst) in enumerate(((glu_p[:, m, w:w + SEQ], conv[:, m, 0:SEQ]),
                                                       (glu_s[:, m, :, w:w + DS], conv[:, m, SEQ:NT].rearrange("p (b t) -> p b t", b=DB)))):
                        if w == 0:
                            ins = V.tensor_scalar(dst, src, tap, vecT[:, m, W + 1:W + 2], ALU.mult, ALU.add)
                        else:
                            dve.wait_ge(S["conv_step"], 2 * W * m + 2 * (w - 1) + part + 1)
                            ins = V.scalar_tensor_tensor(out=dst, in0=src, scalar=tap, in1=dst, op0=ALU.mult, op1=ALU.add)
                        ins.then_inc(S["conv_step"], 1)
            dve.wait_ge(S["stat_mm"], 1)
            for m in range(KD):
                dve.wait_ge(S["conv_step"], 2 * W * (m + 1))
                V.tensor_tensor(out=conv[:, m].rearrange("p (a n) -> p a n", a=2), in0=conv[:, m].rearrange("p (a n) -> p a n", a=2),
                                in1=halves(0), op=ALU.subtract).then_inc(S["centred"], 1)
            dve.wait_ge(S["stat_mm"], 1 + KD)
            V.tensor_scalar(rstd_ln.rearrange("p (a n) -> p a n", a=2), halves(2), EPS, None, ALU.add).then_inc(S["eps_ready"], 1)
            dve.wait_ge(S["std_ready"], 1)
            link(dve, V.reciprocal(rstd_ln, rstd_ln))
            dve.wait_ge(S["sqd"], KD)
            for m in range(KD):
                dve.wait_ge(S["centred"], m + 1)
                V.tensor_tensor(out=conv[:, m], in0=conv[:, m], in1=rstd_ln, op=ALU.mult).then_inc(S["lnx_ready"], 1)
            dve.wait_ge(S["ct_tr"], 2 * DB)
            for b in range(DB):
                V.tensor_copy(new_rows[:, :, DS * b:DS * b + DS], glu_s[:, :, b, W - 1:W - 1 + DS]).then_inc(S["new_packed"], 1)

            dve.wait_ge(S["gpost_in"], 16)
            for t in range(TT + 1):
                if t < TT:
                    r = rows(t)
                    dve.wait_ge(S["sq_b"], t + 1)
                    mean_sq(0, r, "ms_b")
                    dve.wait_ge(S["sd_b"], t + 1)
                    link(dve, V.reciprocal(rs[0:r, 0:1], sd[0:r, 0:1]))
                    V.scalar_tensor_tensor(out=scaled_b[0:r], in0=pb(2 * (t % 2), D, p1=r), scalar=rs[0:r, 0:1],
                                           in1=gpost_a[0:r], op0=ALU.mult, op1=ALU.mult).then_inc(S["o_scaled"], 1)
                    dve.wait_ge(S["o_scaled"], t + 1)
                    V.tensor_tensor(out=x_sb[0:r, t], in0=x_sb[0:r, t], in1=scaled_b[0:r], op=ALU.add).then_inc(S["x1_ready"], 1)
                if t:
                    k, rk = t - 1, rows(t - 1)
                    if k == 0:
                        dve.wait_ge(S["y_ready"], KD)
                        dve.wait_ge(S["co_out"], 16 * (1 + DB))
                    dve.wait_ge(S["tr_b"], k + 1)
                    for q, T in enumerate((hT, uT)):
                        V.tensor_tensor(out=T[:, :, k * P:k * P + rk], in0=pb(4 + 2 * (k % 2), KD, P)[:, :, 0:rk],
                                        in1=gain(4 + q, rk), op=ALU.mult).then_inc(S["hu_ready"], 1)
                if t < TT:
                    dve.wait_ge(S["sq_c"], t + 1)
                    mean_sq(1, r, "ms_c")
                    dve.wait_ge(S["sd_c"], t + 1)
                    link(dve, V.reciprocal(rs[0:r, 1:2], sd[0:r, 1:2]))
                    if t >= 2:
                        dve.wait_ge(S["tr_b"], t - 1)
                    dve.wait_ge(S["x1_ready"], t + 1)
                    V.tensor_scalar(xn_b[0:r, t % 2], x_sb[0:r, t], rs[0:r, 1:2], None, ALU.mult).then_inc(S["xn_b_ready"], 1)

            dve.wait_ge(S["zeroes"], ZEROED["keys"])
            for n in range(2 * TT):
                br, t = n // TT, n % TT
                dve.wait_ge(S["kt_tr"], n + 1)
                if t < 4:
                    for lo in range(2):
                        V.tensor_copy(ktz[HD * lo:HD * lo + HD, br, lo:KV:2, t * P:(t + 1) * P],
                                      pb(6 + n % 2, 2, P, p0=HD * lo, p1=HD * lo + HD)).then_inc(S["kt_ready"], 1)
                else:
                    V.tensor_copy(kt_new[:, br], pb(6 + n % 2, 2, P)[:, :, 0:NS]).then_inc(S["kt_ready"], 1)
            dve.wait_ge(S["cs_mm"], 4)
            for n in range(4):
                c, gi = n // 2, n % 2
                dve.wait_ge(S["ctp_tr"], n + 1)
                V.tensor_copy(ctP[:, c, :, :, 16 * gi:16 * gi + 16].rearrange("p j k c -> p k c j"),
                              pb(6 + n % 2, KV, 16, 8)).then_inc(S["ctp_ready"], 1)
            dve.wait_ge(S["zeroes"], ZEROED["queries"])
            dve.wait_ge(S["q_ready"], KD)
            for p in range(2):
                for half in range(2):
                    lo = HD * half
                    V.tensor_copy(qbd[lo:lo + HD, :, p, 32 * half:32 * half + 32].rearrange("p b (g t) -> p b g t", g=G),
                                  qT[lo:lo + HD, 4 * p:4 * p + 4, SEQ:NT].rearrange("p g (b t) -> p b g t", b=DB)).then_inc(S["qbd_ready"], 1)
            dve.wait_ge(S["gate_tr"], 1)
            V.tensor_copy(gR, pb(2, 4, 48)).then_inc(S["gR_ready"], 1)
            dve.wait_ge(S["gR_ready"], 1)
            for i in range(4):
                V.tensor_copy(gRr[:, i], gR[:, 3 - i, 0:H]).then_inc(S["gR_ready"], 1)
            dve.wait_ge(S["gR_ready"], 5)

            dve.wait_ge(S["zeroes"], ZEROED["table"])
            dve.wait_ge(S["x1_out"], 16 * TT)
            dve.wait_ge(S["kv_out"], KV_OUT)
            dve.wait_ge(S["gate_out"], 16)
            for w in range(len(items) + 3):
                if w < len(items):
                    m, br, i, us = items[w]
                    u = us[0]
                    if br == 0:
                        dve.wait_ge(tb_in[m % 2], 32 * (m // 2 + 1))
                        if m:
                            dve.wait_ge(S["l_ready"], UPM * (m - 1) + 1)
                        V.tensor_copy(e2[:, :, 0:31], tb[:, m % 2, :, 31:SEQ:16]).then_inc(S["e2_ready"], 1)
                        dve.wait_ge(S["e2_ready"], m + 1)
                        dve.wait_ge(S["s_done"], u + 1)
                        if u >= 6:
                            dve.wait_ge(S["t_done"], u - 5)
                        L3 = l_sb[:, u % 6, 0:8 * NCP].rearrange("q (i h n) -> q i h n", i=4, h=2)
                        sc = pb(u % 3, 4, 64).rearrange("q i (h n) -> q i h n", h=2)
                        for ir in range(4):
                            ins = V.tensor_tensor(out=L3[:, ir], in0=sc[:, ir, :, 0:NCP], in1=e2[:, :, 8 * ir:8 * ir + NCP], op=ALU.add)
                        ins.then_inc(S["l_ready"], 1)
                        dve.wait_ge(S["l_ready"], u + 1)
                        L2 = l_sb[:, u % 6, 0:8 * NCP].rearrange("q (r n) -> q r n", n=NCP)
                        link(dve, V.tensor_reduce(mn[:, 0:8], L2, AX.X, ALU.min))
                        link(dve, V.tensor_scalar(mn[:, 0:8], mn[:, 0:8], 0.1 * BIG, None, ALU.min))
                        V.tensor_tensor(out=L2, in0=L2, in1=mn[:, 0:8].unsqueeze(2).broadcast_to([P, 8, NCP]),
                                        op=ALU.subtract).then_inc(S["cmin_ready"], 1)
                    else:
                        for half, u in enumerate(us):
                            dve.wait_ge(S["s_done"], u + 1)
                            if u >= 6:
                                dve.wait_ge(S["t_done"], u - 5)
                            k = stat(w) + half
                            if w >= 3:
                                dve.wait_ge(S["exp_done"], items[w - 3][3][-1] + 1)
                            V.tensor_tensor_reduce(l_sb[:, u % 6, 0:P * (i + 1)], pb(u % 3, P * (i + 1)),
                                                   tb[:, m % 2, half, 384 - P * i:SEQ], 1.0, 3 * BIG, ALU.add, ALU.min,
                                                   mn[:, k:k + 1]).then_inc(S["l_ready"], 1)
                if 1 <= w <= len(items):
                    m, br, i, us = items[w - 1]
                    dve.wait_ge(S["exp_done"], us[-1] + 1)
                    if br == 0:
                        if m:
                            dve.wait_ge(S["pn_ready"], UPM * (m - 1) + 1)
                        L2 = l_sb[:, us[0] % 6, 0:8 * NCP].rearrange("q (r n) -> q r n", n=NCP)
                        link(dve, V.tensor_reduce(den[:, 0:8], L2, AX.X, ALU.add))
                        link(dve, V.tensor_scalar(den[:, 0:8], den[:, 0:8], 1e-30, None, ALU.max))
                        link(dve, V.reciprocal(rden[:, 0:8], den[:, 0:8]))
                        h0 = 8 * (m // 4) + m % 4
                        V.tensor_tensor(out=rden[:, 0:8].rearrange("q (i h) -> q i h", h=2),
                                        in0=rden[:, 0:8].rearrange("q (i h) -> q i h", h=2),
                                        in1=gRr[:, :, h0:h0 + 5:4], op=ALU.mult).then_inc(S["den_ready"], 1)
                    else:
                        k = stat(w - 1)
                        if w >= 4:
                            dve.wait_ge(S["pn_ready"], items[w - 4][3][-1] + 1)
                        link(dve, V.tensor_scalar(den[:, k:k + 2], den[:, k:k + 2], 1e-30, None, ALU.max))
                        V.reciprocal(rden[:, k:k + 2], den[:, k:k + 2]).then_inc(S["den_ready"], 1)
                if 2 <= w < len(items) + 2:
                    m, br, i, us = items[w - 2]
                    u = us[-1]
                    n = SEQ if br == 0 else P * (i + 1)
                    dve.wait_ge(S["t_done"], u + 1)
                    if u >= 4:
                        dve.wait_ge(S["pv_done"], item_of[u - 4] + 1)
                    V.tensor_copy(pt_sb[:, u % 4, 0:n], pb(3 + u % 2, n)).then_inc(S["pt_d"], 1)
                if w >= 3 and (items[w - 3][1] == 0 or items[w - 3][2] == 3):
                    m, br = items[w - 3][:2]
                    g = m % 4
                    n_z = z_jobs.index((m // 4, br, g))
                    dve.wait_ge(S["zb_ready"], 3 * (n_z + 1))
                    dve.wait_ge(S["pv_done"], w - 2)
                    if br:
                        prev = 2 * m + br - 1
                        if prev:
                            dve.wait_ge(S["y_add"], prev)
                    V.tensor_tensor(out=y_tmp if br else yT[:, m, 0:SEQ], in0=pb(5, SEQ), in1=sz[:, br, g], op=ALU.mult).then_inc(S["y_mul"], 1)

            dve.wait_ge(S["ss_mm"], 1)
            dve.wait_ge(S["bsc_ready"], KV)
            dve.wait_ge(S["t_done"], N_UNITS)
            dve.wait_ge(S["gS_in"], 16 * NBR)
            L3 = l_sb[:, 0, 0:480].rearrange("q (b n) -> q b n", b=DB)
            V.tensor_tensor(out=L3, in0=pb(2, DB, 60), in1=bsc.unsqueeze(1).broadcast_to([P, DB, 60]), op=ALU.add).then_inc(S["sl_ready"], 1)
            dve.wait_ge(S["sl_ready"], 1)
            link(dve, V.tensor_reduce(mn[:, 0:8], L3, AX.X, ALU.min))
            link(dve, V.tensor_scalar(mn[:, 0:8], mn[:, 0:8], 0.1 * BIG, None, ALU.min))
            V.tensor_tensor(out=L3, in0=L3, in1=mn[:, 0:8].unsqueeze(2).broadcast_to([P, DB, 60]), op=ALU.subtract).then_inc(S["cmin_ready"], 1)
            dve.wait_ge(S["exp_done"], N_UNITS + 1)
            link(dve, V.tensor_reduce(den[:, 0:8], L3, AX.X, ALU.add))
            link(dve, V.tensor_scalar(den[:, 0:8], den[:, 0:8], 1e-30, None, ALU.max))
            link(dve, V.reciprocal(rden[:, 0:8], den[:, 0:8]))
            link(dve, V.tensor_tensor(out=rden[:, 0:8], in0=rden[:, 0:8], in1=gS[:, 0], op=ALU.mult))
            V.tensor_tensor(out=L3, in0=L3, in1=rden[:, 0:8].unsqueeze(2).broadcast_to([P, DB, 60]), op=ALU.mult).then_inc(S["sp_ready"], 1)
            dve.wait_ge(S["st_tr"], 1)
            dve.wait_ge(S["qbd_ready"], 4)
            V.tensor_copy(ptc.rearrange("p b n -> p (b n)"), pb(4, 1024, p1=60)).then_inc(S["pts_ready"], 1)
            dve.wait_ge(S["so_mm"], 1)
            V.tensor_copy(orc.rearrange("p b n -> p (b n)"), pb(6, 1024)).then_inc(S["or_ready"], 1)
            dve.wait_ge(S["zb_ready"], 72)

            def gate_sample(dst, src, br, b):
                for half in range(2):
                    lo = HD * half
                    o_ = src[lo:lo + HD].rearrange("q (p h g t) -> q p h g t", p=2, h=2, g=G)[:, :, half]
                    z_ = szs[lo:lo + HD, br, :, DS * b:DS * b + DS].rearrange("q (p g) t -> q p g t", p=2)
                    d_ = dst[lo:lo + HD].rearrange("q (p g) t -> q p g t", p=2)
                    V.tensor_tensor(out=d_, in0=o_, in1=z_, op=ALU.mult).then_inc(S["ys_mul"], 1)

            dve.wait_ge(S["ot_tr"], 1)
            for b in range(DB):
                gate_sample(yT[:, :, SEQ + DS * b:SEQ + DS * b + DS], pb(4, 1024)[:, b * P:(b + 1) * P], 0, b)
            for w in range(2 * DB + 4):
                n = w
                if n < 2 * DB:
                    dve.wait_ge(S["ss_mm"], n + 2)
                    if n >= 3:
                        dve.wait_ge(S["st_tr"], n - 1)
                    if n >= 4:
                        dve.wait_ge(S["se_ready"], n - 3)
                    k = 8 + n % 4
                    V.tensor_tensor_reduce(l_sb[:, 1 + n % 3, 0:KS], pb(2 + n % 2, KS), bs, 1.0, 3 * BIG, ALU.add, ALU.min,
                                           mn[:, k:k + 1]).then_inc(S["sl_ready"], 1)
                n = w - 1
                if 0 <= n < 2 * DB:
                    b, br = n // 2, n % 2
                    dve.wait_ge(S["se_ready"], n + 1)
                    k = 8 + n % 4
                    link(dve, V.tensor_scalar(den[:, k:k + 1], den[:, k:k + 1], 1e-30, None, ALU.max))
                    link(dve, V.reciprocal(rden[:, k:k + 1], den[:, k:k + 1]))
                    L = l_sb[:, 1 + n % 3, 0:KS]
                    V.tensor_scalar(L, L, rden[:, k:k + 1], gS[:, 1 + br, b:b + 1], ALU.mult, ALU.mult).then_inc(S["sp_ready"], 1)
                n = w - 2
                if 0 <= n < 2 * DB:
                    dve.wait_ge(S["st_tr"], n + 2)
                    if n >= 2:
                        dve.wait_ge(S["so_mm"], n)
                    else:
                        dve.wait_ge(S["pv_done"], len(items))
                    V.tensor_copy(pts[:, n % 2, 0:2], pb(4 + n % 2, 2, P)).then_inc(S["pts_ready"], 1)
                    V.tensor_copy(pts[0:DS, n % 2, 2], pb(4 + n % 2, 3, P, p1=DS)[:, 2]).then_inc(S["pts_ready"], 1)
                n = w - 3
                if 0 <= n < 2 * DB:
                    dve.wait_ge(S["so_mm"], n + 2)
                    if n >= 2:
                        dve.wait_ge(S["ot_tr"], n)
                    for p in range(2):
                        V.tensor_copy(orow[64 * p:64 * p + 64, n % 2], pb(6, 2, P, p0=64 * p, p1=64 * p + 64)[:, p]).then_inc(S["or_ready"], 1)
                n = w - 4
                if 0 <= n < 2 * DB:
                    b, br = n // 2, n % 2
                    dve.wait_ge(S["ot_tr"], n + 2)
                    gate_sample(y_br[:, br, :, DS * b:DS * b + DS], pb(7, P), 1 + br, b)
            dve.wait_ge(S["ys_mul"], 2 * DB * 3)
            ys = yT[:, :, SEQ:NT]
            for br in range(2):
                V.tensor_tensor(out=ys, in0=ys, in1=y_br[:, br], op=ALU.add).then_inc(S["y_s"], 1)
                dve.wait_ge(S["y_s"], br + 1)

            dve.wait_ge(S["gpost_in"], 32)
            for t in range(TT):
                r = rows(t)
                dve.wait_ge(S["sq_a"], TT + t + 1)
                mean_sq(t, r, "ms_a")
                dve.wait_ge(S["sd_a"], TT + t + 1)
                link(dve, V.reciprocal(rs[0:r, t:t + 1], sd[0:r, t:t + 1]))
                if t >= 2:
                    dve.wait_ge(fy_out[t % 2], 16 * (t // 2))
                dve.wait_ge(x_in[t % 2], 16 * (t // 2 + 2))
                link(dve, V.scalar_tensor_tensor(out=y_out[0:r, t % 2], in0=pb(2 * (t % 2), D, p1=r), scalar=rs[0:r, t:t + 1],
                                                 in1=gpost_b[0:r], op0=ALU.mult, op1=ALU.mult))
                V.tensor_tensor(out=y_out[0:r, t % 2], in0=y_out[0:r, t % 2], in1=x1_back[0:r, t % 2], op=ALU.add).then_inc(S["fy"], 1)

        @block.tensor
        def _(pe):
            def product(out, pairs):
                pairs = list(pairs)
                for k, (l, r) in enumerate(pairs):
                    ins = pe.matmul(out, l, r, start=(k == 0), stop=(k == len(pairs) - 1))
                return ins

            def tproduct(b0, lhs, src):
                for k in range(KD):
                    for hf in range(2):
                        ins = pe.matmul(pb(b0 + hf, HT)[0:lhs(k).shape[1]], lhs(k), src[:, k, hf * HT:(hf + 1) * HT],
                                        start=(k == 0), stop=(k == KD - 1))
                return ins

            def await_chunk(c):
                pe.wait_ge(w_in[c % RING], arrived[c])

            pe.wait_ge(S["ident_ready"], 1)
            pe.wait_ge(S["vec_in"], 16 * 7)
            for k in range(KD):
                ins = pe.transpose(pb(2, KD, 37)[:, k], vec_rows[0:37, k * P:(k + 1) * P], ident[0:37, 0:37])
            ins.then_inc(S["vec_ps"], 1)
            for t in range(TT):
                r = rows(t)
                pe.wait_ge(S["xn_a_ready"], t + 1)
                if t >= 2:
                    pe.wait_ge(S["h_ready"], t - 1)
                for k in range(KD):
                    ins = pe.transpose(pb(4 + 2 * (t % 2), KD, P)[:, k, 0:r], xn_a[0:r, t % 2, k * P:(k + 1) * P], ident[0:r, 0:r])
                ins.then_inc(S["tr_a"], 1)
                if t == 1:
                    pe.wait_ge(S["bias_in"], 32)
                    pe.matmul(pb(0, SEQ, p1=H), rel_rows, hot_rows, start=True, stop=True).then_inc(S["early_mm"], 1)
                    pe.wait_ge(S["pe_in"], 32)
                    for c in range(2):
                        ins = pe.transpose(pb(1, 2, 16)[:, c], pe_rows[:, c], ident[0:16, 0:16])
                    ins.then_inc(S["early_mm"], 1)
            pe.wait_ge(S["state_in"], 32)
            pe.wait_ge(S["h_ready"], 4)
            for n in range(4):
                i, mg = n // 2, n % 2
                if n >= 2:
                    pe.wait_ge(S["state_ready"], 4 * (n - 1))
                for k in range(4):
                    ins = pe.transpose(pb(6 + n % 2, 4, 120)[:, k], state_rows[0:120, i, (4 * mg + k) * P:(4 * mg + k + 1) * P],
                                       ident[0:120, 0:120])
                ins.then_inc(S["state_tr"], 1)

            def ct_transposes(n):
                pe.wait_ge(rows_in[n % 2], 64 * (n // 2 + 1))
                if n == DB:
                    pe.wait_ge(S["hid_ready"], 2)
                if n >= 2:
                    pe.wait_ge(S["ct_ready"], n - 1)
                else:
                    pe.wait_ge(S["state_ready"], 16)
                for kv in range(KV):
                    ins = pe.transpose(pb(6 + n % 2, KV, P)[:, kv], rows_ring[:, n % 2, kv], ident)
                ins.then_inc(S["ct_tr"], 1)

            pe.wait_ge(S["h_ready"], TT)
            pe.wait_ge(S["line_part"], 2)
            pe.wait_ge(S["pe_sb_ready"], 1)
            pe.wait_ge(S["vec_ready"], 1)
            for m in range(KD):
                for j in range(3):
                    c = 3 * (m // 2) + j
                    await_chunk(c)
                    if m:
                        pe.wait_ge(*((S["glu_ready"], 3 * m), (S["sg_ready"], m), (S["z_ready"], m))[j])
                    lo = (m % 2) * P
                    ins = tproduct(2 * j, lambda k: ring[:, c % RING, k, lo:lo + P], hT)
                    ins.then_inc(S["proj_a"], 1)
                    if j == 1:
                        ct_transposes(m)
            pe.wait_ge(S["ones_ready"], 1)
            pe.wait_ge(S["glu_ready"], 3 * KD)
            for m in range(KD):
                pe.wait_ge(S["conv_step"], 2 * W * (m + 1))
                for hf in range(2):
                    ins = pe.matmul(pb(hf, HT), ones, conv[:, m, hf * HT:(hf + 1) * HT], start=(m == 0), stop=(m == KD - 1))
            ins.then_inc(S["stat_mm"], 1)

            def compress(c):
                pe.wait_ge(S["w1_in"], 16 * (c + 1))
                pe.wait_ge(S["ct_ready"], DB * (c + 1))
                pe.wait_ge(S["pe_ready"], c + 1)
                for ht in range(2):
                    ins = product(pb(6 + ht, 33, NCS), ((w1_sb[:, j, ht * P:(ht + 1) * P], ctS[:, j % 8, :, j // 8:j // 8 + NCS])
                                                        for j in range(16)))
                    ins.then_inc(S["cs_mm"], 1)

            compress(0)
            for m in range(KD):
                pe.wait_ge(S["sqd"], m + 1)
                for hf in range(2):
                    ins = pe.matmul(pb(2 + hf, HT), ones, sg[:, m % 2, hf * HT:(hf + 1) * HT], start=(m == 0), stop=(m == KD - 1))
                ins.then_inc(S["stat_mm"], 1)
            pe.wait_ge(S["w2_in"], 16 * 8)
            pe.wait_ge(S["hid_ready"], 2)
            pe.wait_ge(S["z_ready"], KD)
            product(pb(4, 480), ((w2_sb[:, 0, ht], hid[:, ht]) for ht in range(2))).then_inc(S["kc_mm"], 1)
            for b in range(DB):
                ct_transposes(DB + b)
            compress(1)
            pe.wait_ge(S["hid_ready"], 4)
            pe.wait_ge(S["kc_ready"], 1)
            for b in range(DB):
                ins = product(pb(4, DB, P, p1=60)[:, b], ((hid[:, ht, 60 * b:60 * b + 60], w2_sb[:, 1, ht]) for ht in range(2)))
            ins.then_inc(S["vc_mm"], 1)
            pe.wait_ge(S["centred"], KD)
            for k in range(KD):
                ins = pe.transpose(pb(0, KD, P, p1=W - 1)[:, k], glu_p[:, k, SEQ:SEQ + W - 1], ident)
            ins.then_inc(S["co_tr"], 1)
            pe.wait_ge(S["eps_ready"], 1)
            pe.wait_ge(S["new_packed"], DB)
            for k in range(KD):
                ins = pe.transpose(pb(2, KD, P, p1=NS)[:, k], new_rows[:, k], ident)
            ins.then_inc(S["co_tr"], 1)

            pe.wait_ge(S["y_ready"], KD)
            pe.wait_ge(S["co_ready"], 2)
            pe.wait_ge(S["vc_ready"], 1)
            pe.wait_ge(S["hid_ready"], 4)

            def turn_b(t):
                r = rows(t)
                pe.wait_ge(S["xn_b_ready"], t + 1)
                if t >= 2:
                    pe.wait_ge(S["hu_ready"], 2 * (t - 1))
                for k in range(KD):
                    ins = pe.transpose(pb(4 + 2 * (t % 2), KD, P)[:, k, 0:r], xn_b[0:r, t % 2, k * P:(k + 1) * P], ident[0:r, 0:r])
                ins.then_inc(S["tr_b"], 1)

            def row_product(t, src, c0, done):
                r = rows(t)
                for c in range(4):
                    await_chunk(c0 + c)
                    ins = product(pb(2 * (t % 2), 4, CH, p1=r)[:, c], ((src[:, k, t * P:t * P + r], ring[:, (c0 + c) % RING, k]) for k in range(KD)))
                ins.then_inc(S[done], 1)
                return ins

            for t in range(TT):
                if t >= 2:
                    pe.wait_ge(S["o_scaled"], t - 1)
                ins = row_product(t, zA, C_OA, "o_mm")
                if t >= 1:
                    turn_b(t - 1)
            turn_b(TT - 1)

            pe.wait_ge(S["hu_ready"], 2 * TT)
            pe.wait_ge(S["o_scaled"], TT)

            def kt_transposes(br):
                for t in range(TT):
                    n = TT * br + t
                    r = rows(t)
                    pe.wait_ge(S["kv_ready"], TT * (2 * br + 2) + t + 1)
                    if n >= 2:
                        pe.wait_ge(S["kt_ready"], sum(2 if q % TT < 4 else 1 for q in range(n - 1)))
                    for p in range(2):
                        ins = pe.transpose(pb(6 + n % 2, 2, P)[:, p, 0:r], k_stage[0:r, br, t, p * P:(p + 1) * P], ident[0:r, 0:r])
                    ins.then_inc(S["kt_tr"], 1)

            for c in range(6):
                await_chunk(C_KV + c)
                for t in range(TT):
                    n = TT * c + t
                    r = rows(t)
                    if n >= 6:
                        pe.wait_ge(S["kv_ready"], n - 5)
                    if c < 2 and t < 4:
                        lhs = hT[:, :, (t // 2) * 256 + t % 2:(t // 2) * 256 + 256:2]
                    else:
                        lhs = hT[:, :, t * P:t * P + r]
                    ins = product(pb(n % 6, CH, p1=r), ((lhs[:, k], ring[:, (C_KV + c) % RING, k]) for k in range(KD)))
                    ins.then_inc(S["kv_mm"], 1)
                if c == 4:
                    kt_transposes(0)
            kt_transposes(1)
            for n in range(4):
                c, gi = n // 2, n % 2
                if n >= 2:
                    pe.wait_ge(S["ctp_ready"], n - 1)
                else:
                    pe.wait_ge(S["kt_ready"], 18)
                for kv in range(KV):
                    ins = pe.transpose(pb(6 + n % 2, KV, P)[:, kv], cmp_rows[:, gi, c, kv], ident)
                ins.then_inc(S["ctp_tr"], 1)
            pe.wait_ge(S["kv_ready"], 30)
            pe.wait_ge(S["ctp_ready"], 4)

            def compress_p(n, c):
                pe.wait_ge(S["w1_in"], 16 * (2 + n))
                if n:
                    pe.wait_ge(S["hidp_ready"], 2)
                for ht in range(2):
                    product(pb(4 + ht, KV, NCP), ((w1_sb[:, j, ht * P:(ht + 1) * P], ctP[:, c, j % 8, :, j // 8:j // 8 + NCP])
                                                  for j in range(16))).then_inc(S["cp_mm"], 1)

            compress_p(0, 1)
            pe.wait_ge(S["hidp_ready"], 2)
            for p in range(2):
                for half in range(2):
                    kv = 2 * p + half
                    ins = product(pb(2 + p, HD, p0=32 * half, p1=32 * half + NCP),
                                  ((hid_p[:, ht, NCP * kv:NCP * (kv + 1)], w2_sb[:, 1, ht, 0:HD]) for ht in range(2)))
            ins.then_inc(S["cpp_mm"], 1)
            for m in range(KD):
                c = C_Q + m // 2
                await_chunk(c)
                if m >= 3:
                    pe.wait_ge(S["q_ready"], m - 2)
                if m == 1:
                    pe.wait_ge(S["bd_ready"], 4)
                if m == 2:
                    pe.wait_ge(S["hidp_ready"], 2)
                lo = (m % 2) * P
                ins = tproduct(2 * (m % 3), lambda k: ring[:, c % RING, k, lo:lo + P], uT)
                ins.then_inc(S["q_mm"], 1)
            pe.wait_ge(S["wg_in"], 16)
            tproduct(6, lambda k: wgate[:, k], uT).then_inc(S["gate_mm"], 1)
            pe.wait_ge(S["q_ready"], 7)
            compress_p(1, 0)
            pe.wait_ge(S["hidp_ready"], 4)
            product(pb(0, 124), ((w2_sb[:, 0, ht], hid_p[:, ht]) for ht in range(2))).then_inc(S["cpp_mm"], 1)
            pe.wait_ge(S["gate_ready"], 1)
            pe.wait_ge(S["q_ready"], KD)
            for i in range(4):
                ins = pe.transpose(pb(2, 4, 48)[:, i], gateT[0:48, i * P:(i + 1) * P], ident[0:48, 0:48])
            ins.then_inc(S["gate_tr"], 1)
            pe.wait_ge(S["gR_ready"], 1)
            pe.wait_ge(S["bd_ready"], 8)

            def z_product(n, b0):
                p, br, g = z_jobs[n]
                c = C_Z + 6 * p + 2 * br + g // 2
                await_chunk(c)
                lo = (g % 2) * P
                ins = tproduct(b0, lambda k: ring[:, c % RING, k, lo:lo + P], uT)
                ins.then_inc(S["z_mm"], 1)

            for n in range(12):
                if n >= 2:
                    pe.wait_ge(S["zb_ready"], 3 * (n - 1))
                z_product(n, 2 * (n % 2))

            pe.wait_ge(S["zb_ready"], 36)
            pe.wait_ge(S["kt_ready"], 18)
            pe.wait_ge(S["zeroes"], ZEROED["keys"])
            for w in range(len(items) + 3):
                if w < len(items):
                    m, br, i, us = items[w]
                    for half, u in enumerate(us):
                        if u >= 3:
                            pe.wait_ge(S["l_ready"], u - 2)
                        if br == 0:
                            for ir in range(4):
                                ins = pe.matmul(pb(u % 3, 4, 64)[:, ir], qT[:, m, (3 - ir) * P:(4 - ir) * P], kcbd[:, m // 4],
                                                start=True, stop=True)
                        else:
                            n = P * (i + 1)
                            ins = pe.matmul(pb(u % 3, n), qT[:, m, i * P:(i + 1) * P], ktz[:, br - 1, 2 * (m // 4) + half, 0:n],
                                            start=True, stop=True)
                        ins.then_inc(S["s_done"], 1)
                if w in z_at:
                    n = z_at[w]
                    if n > 12:
                        pe.wait_ge(S["zb_ready"], 3 * n)
                    z_product(n, 6)
                if 2 <= w < len(items) + 2:
                    m, br, i, us = items[w - 2]
                    for u in us:
                        pe.wait_ge(S["pn_ready"], u + 1)
                        if u >= 2:
                            name, count = pt_by[u - 2]
                            pe.wait_ge(S[name], count)
                        if br == 0:
                            for ir in range(4):
                                ins = pe.transpose(pb(3 + u % 2, 4, P)[:, 3 - ir], pc_sb[:, ir], ident)
                        else:
                            for j in range(i + 1):
                                ins = pe.transpose(pb(3 + u % 2, 4, P)[:, j], l_sb[:, u % 6, j * P:(j + 1) * P], ident)
                        ins.then_inc(S["t_done"], 1)
                if w >= 3:
                    m, br, i, us = items[w - 3]
                    for u in us:
                        name, count = pt_by[u]
                        pe.wait_ge(S[name], count)
                    if 3 * m + br and (br == 0 or i == 0):
                        pe.wait_ge(S["y_mul"], 3 * m + br)
                    if br == 0:
                        ins = pe.matmul(pb(5, SEQ), vcbd[:, m // 4], pt_sb[:, us[0] % 4], start=True, stop=True)
                    else:
                        for j in range(i + 1):
                            for half, u in enumerate(us):
                                kv = 2 * (m // 4) + half
                                ins = pe.matmul(pb(5, SEQ, p0=HD * half, p1=HD * half + HD)[:, i * P:(i + 1) * P],
                                                v_sb[:, br - 1, j, kv * HD:(kv + 1) * HD], pt_sb[:, u % 4, j * P:(j + 1) * P],
                                                start=(j == 0), stop=(j == i))
                    ins.then_inc(S["pv_done"], 1)

            pe.wait_ge(S["l_ready"], N_UNITS)
            pe.wait_ge(S["qbd_ready"], 4)
            pe.wait_ge(S["kc_ready"], 1)
            for b in range(DB):
                for p in range(2):
                    ins = pe.matmul(pb(2, DB, 60, p0=64 * p, p1=64 * p + 64)[:, b], qbd[:, b, p], kc_s[:, b], start=True, stop=True)
            ins.then_inc(S["ss_mm"], 1)
            pe.wait_ge(S["sp_ready"], 1)
            pe.wait_ge(S["y_mul"], 24)
            for b in range(DB):
                ins = pe.transpose(pb(4, DB, P, p1=60)[:, b], l_sb[:, 0, 60 * b:60 * b + 60], ident)
            ins.then_inc(S["st_tr"], 1)
            pe.wait_ge(S["pts_ready"], 1)
            pe.wait_ge(S["zb_ready"], 72)
            for b in range(DB):
                ins = pe.matmul(pb(6, DB, P)[:, b], ptc[:, b], vc_s[0:60, b], start=True, stop=True)
            ins.then_inc(S["so_mm"], 1)
            pe.wait_ge(S["or_ready"], 1)
            for b in range(DB):
                ins = pe.transpose(pb(4, DB, P)[:, b], orc[:, b], ident)
            ins.then_inc(S["ot_tr"], 1)
            for w in range(2 * DB + 3):
                n = w
                if n < 2 * DB:
                    pe.wait_ge(cache_in[n % 4], 32 * (n // 4 + 1))
                    if n >= 2:
                        pe.wait_ge(S["skt_ready"], n - 1)
                    for p in range(2):
                        for pg in range(2):
                            ins = pe.transpose(pb(n % 2, 2, 2, P)[:, p, pg], cache_sb[:, n % 4, pg, p * P:(p + 1) * P], ident)
                    ins.then_inc(S["skt_tr"], 1)
                    pe.wait_ge(S["skt_ready"], n + 1)
                    pe.wait_ge(S["kts_new"], n + 1)
                    pe.wait_ge(S["sl_ready"], max(n, 1))
                    for p in range(2):
                        ins = pe.matmul(pb(2 + n % 2, KS, p0=64 * p, p1=64 * p + 64), qbd[:, n // 2, p], kts[:, n % 2, p],
                                        start=True, stop=True)
                    ins.then_inc(S["ss_mm"], 1)
                n = w - 1
                if 0 <= n < 2 * DB:
                    pe.wait_ge(S["sp_ready"], n + 2)
                    pe.wait_ge(S["ys_mul"], 2 * DB)
                    if n >= 2:
                        pe.wait_ge(S["pts_ready"], 1 + 2 * (n - 1))
                    for j in range(3):
                        k = min(P, KS - j * P)
                        ins = pe.transpose(pb(4 + n % 2, 3, P, p1=k)[:, j], l_sb[:, 1 + n % 3, j * P:j * P + k], ident)
                    ins.then_inc(S["st_tr"], 1)
                n = w - 2
                if 0 <= n < 2 * DB:
                    pe.wait_ge(S["pts_ready"], 1 + 2 * (n + 1))
                    pe.wait_ge(vnew_in[n % 4], 16 * (n // 4 + 1))
                    pe.wait_ge(S["or_ready"], 1 + 2 * n)
                    parts = [(pts[:, n % 2, j], cache_sb[:, n % 4, j, CH:2 * CH]) for j in range(2)]
                    parts.append((pts[0:DS, n % 2, 2], vnew[:, n % 4]))
                    product(pb(6, CH), parts).then_inc(S["so_mm"], 1)
                n = w - 3
                if 0 <= n < 2 * DB:
                    pe.wait_ge(S["or_ready"], 1 + 2 * (n + 1))
                    pe.wait_ge(S["ys_mul"], 2 * DB + 2 * n)
                    pe.transpose(pb(7, P), orow[:, n % 2], ident).then_inc(S["ot_tr"], 1)
            pe.wait_ge(S["y_s"], 2)
            pe.wait_ge(S["y_add"], 2 * KD)
            for t in range(TT):
                if t >= 2:
                    pe.wait_ge(S["fy"], t - 1)
                row_product(t, yT, C_OB, "fo_mm")


INPUTS = ['x_prompt', 'x_sample', 'state_conv', 'cache_cmp', 'cache_slc', 'state_win', 'page_table', 'rel_bias',
          'a_norm_pre', 'a_w_in', 'a_conv_w', 'a_conv_b', 'a_ln_g', 'a_ln_b', 'a_w_out', 'a_norm_post',
          'kv_norm', 'w_kv', 'cmp_pe', 'cmp_w1', 'cmp_w2', 'b_norm_pre', 'b_w_in', 'b_w_out', 'b_norm_post']
OUTPUTS = [('y_prompt', (1, SEQ, D)), ('y_sample', (DB, DS, D)), ('conv_prompt', (1, 1, W - 1, D)),
           ('conv_sample', (1, DB, W - 1, D)), ('cmp_prompt', (1, SEQ, 2, KV, HD)), ('cmp_sample', (DB, DS, 2, KV, HD)),
           ('slc_prompt', (1, SEQ, 2, KV, HD)), ('slc_sample', (DB, DS, 2, KV, HD)),
           ('win_prompt', (1, SEQ, 2, KV, HD)), ('win_sample', (DB, KS, 2, KV, HD))]


def kernel(**inputs):
    import numpy as _np
    import concourse.bacc as _bacc
    from concourse import mybir as _mybir
    from concourse.bass_utils import run_bass_kernel_spmd as _run

    nc = _bacc.Bacc("TRN2", target_bir_lowering=False, num_devices=1)
    arrays, ins = {}, {}
    for name in INPUTS:
        a = _np.ascontiguousarray(inputs[name])
        arrays[f"in_{name}"] = a
        ins[name] = nc.dram_tensor(f"in_{name}", a.shape, _mybir.dt.from_np(a.dtype), kind="ExternalInput").ap()
    a = bucket_rows()
    arrays["bucket_rows"] = a
    ins["bucket_rows"] = nc.dram_tensor("bucket_rows", a.shape, _mybir.dt.float32, kind="ExternalInput").ap()
    outs = {name: nc.dram_tensor(f"out_{name}", shape, _mybir.dt.float32, kind="ExternalOutput").ap() for name, shape in OUTPUTS}
    build(nc, ins, outs)
    r = _run(nc, [arrays], core_ids=[0])
    return tuple(r.results[0][f"out_{name}"] for name, _ in OUTPUTS)
```

```python
import math
from contextlib import ExitStack

import numpy as np
import concourse.bass as bass
from concourse import mybir

F32 = mybir.dt.float32
F32R = mybir.dt.float32r
I32 = mybir.dt.int32
ALU = mybir.AluOpType
ACT = mybir.ActivationFunctionType
AX = mybir.AxisListType

P = 128
D = 1024
KD = D // P
SEQ = 512
DB, DS = 8, 8
NS = DB * DS
NT = SEQ + NS
HT = NT // 2
TT = 5
W = 31
H, HD, KV, G = 16, 64, 4, 4
NBR = 3
PAST, PAGE = 256, 128
STRIDE = 16
NCP = SEQ // STRIDE - 1
NCS = PAST // STRIDE - 1
KS = PAST + DS
BUCKETS, MAXD = 32, 128
EPS = 1e-6
BIG = 1e30
QSCALE = -(HD ** -0.5)
NX = 640
CH = 256
RING = 6
TRING, HRING = 6, 3


def bucket_rows():
    n = np.maximum(SEQ - 1 - np.arange(SEQ), 0)
    exact = BUCKETS // 2
    nf = np.maximum(n, 1).astype(np.float32)
    large = exact + (np.log(nf / np.float32(exact)) / np.float32(math.log(MAXD / exact)) * (BUCKETS - exact)).astype(np.int32)
    bucket = np.where(n < exact, n, np.minimum(large, BUCKETS - 1))
    return (bucket[None, :] == np.arange(BUCKETS)[:, None]).astype(np.float32)


def build(nc, I, O):
    ctx = ExitStack()
    with ctx:
        R_RING, R_H, R_C, R_Z, R_F, R_X, R_G = 0, 12288, 16896, 21504, 26112, 32880, 38000
        R_P = R_G + 11880
        base = -(-nc.sbuf_base // 32) * 32
        arena = ctx.enter_context(nc.sbuf_tensor("arena", [P, R_P], F32))
        kept = ctx.enter_context(nc.sbuf_tensor("kept", [P, 53150 - R_P], F32))
        page_sb = ctx.enter_context(nc.sbuf_tensor("page_sb", [1, 2 * DB], I32))
        psum = ctx.enter_context(nc.psum_tensor("psum", [P, 8 * 512], F32))
        bias_dram = nc.dram_tensor("bias_line", [H, NX], F32, kind="Internal").ap()
        bias_copies = nc.dram_tensor("bias_copies", [H, P, NX], F32, kind="Internal").ap()
        gate_dram = nc.dram_tensor("gate_rows", [NBR * H, NS], F32, kind="Internal").ap()
        x1_dram = nc.dram_tensor("x1_rows", [NT, D], F32, kind="Internal").ap()

        def at(off, *dims, p0=0, p1=P):
            n = int(np.prod(dims))
            v = arena[p0:p1, off:off + n] if off < R_P else kept[p0:p1, off - R_P:off - R_P + n]
            if len(dims) == 1:
                return v
            names = "abcdef"[:len(dims)]
            return v.rearrange(f"p ({' '.join(names)}) -> p {' '.join(names)}",
                               **{c: d for c, d in zip(names[1:], dims[1:])})

        def over(name, off, *dims, dtype=F32R):
            assert off % 8 == 0
            v = nc.alloc_sbuf_tensor_at(name, [P, int(np.prod(dims))], dtype, offset=base + 4 * off)[:, :]
            names = "abcdef"[:len(dims)]
            return v.rearrange(f"p ({' '.join(names)}) -> p {' '.join(names)}",
                               **{c: d for c, d in zip(names[1:], dims[1:])})

        def pb(b, *dims, p0=0, p1=P):
            n = int(np.prod(dims))
            v = psum[p0:p1, b * 512:b * 512 + n]
            if len(dims) == 1:
                return v
            names = "abcdef"[:len(dims)]
            return v.rearrange(f"p ({' '.join(names)}) -> p {' '.join(names)}",
                               **{c: d for c, d in zip(names[1:], dims[1:])})

        def halves(b):
            return pb(b, 2, 512)[:, :, 0:HT]

        ring = at(R_RING, RING, KD, CH)
        x_sb = at(R_X, TT, D)
        hT = at(R_H, KD, NT)
        xn_a = at(R_C, 2, D)
        state_rows = at(R_C + 2 * D, 2, D)
        junk_a = at(R_Z, D)
        rel_rows = at(R_Z + 1024, H, p1=BUCKETS)
        hot_rows = at(R_Z + 1040, SEQ, p1=BUCKETS)
        pe_rows = at(R_Z + 1552, 2, P, p1=16)
        line = at(R_Z + 1808, NX, p1=H)
        glu_p = at(R_F, KD, SEQ + W - 1)
        glu_s = at(R_F + KD * (SEQ + W - 1), KD, DB, DS + W - 1)
        conv = at(R_C, KD, NT)
        zA = at(R_Z, KD, NT)
        rstd_ln = at(R_H, NT)
        conv_out_p = at(R_H + 1024, D)
        conv_out_s = at(R_H + 2048, D)
        xn_b = at(R_F, 2, D)
        gpost_a = at(R_F + 2048, D)
        junk_b = at(R_F + 3072, D)
        scaled_b = at(R_F + 4096, D)
        uT = over("u_whole", R_C, KD, NT, dtype=F32)
        u_hi = over("u_hi", R_X, KD, NT)
        u_lo = over("u_lo", R_C, KD, NT)
        tile_w = over("tile_whole", R_RING, TRING, KD, P, dtype=F32)
        tile_lo = over("tile_lo", R_RING, TRING, KD, P)
        tile_hi = over("tile_hi", R_RING + TRING * D, HRING, KD, P)
        ctS = at(R_G, 8, 33, 16)
        ctP = at(R_G, 2, 8, KV, 32)
        cmp_rows = at(R_G + 2048, 2, 2, KV, 2 * HD)
        w1_sb = at(R_G + 4224, 16, 256)
        rows_ring = at(R_G + 8320, 2, KV, P)
        new_rows = at(R_G + 8320, KD, NS)
        vecT = at(R_G + 9344, KD, 37)
        ones = at(R_G + 9640, P)
        hid = at(R_G + 9768, 2, 480)
        R_S = R_G + 10728
        sg = at(R_S, 2, NT)
        vec_rows = at(R_S, D)
        cmp_rows_s = at(R_S, 512)
        hid_p = at(R_S + 512, 2, 124)
        wgate = over("wgate_whole", R_S + 760, KD, 48, dtype=F32)
        wgate_lo = over("wgate_lo", R_S + 760, KD, 48)
        wgate_hi = over("wgate_hi", R_Z + 3200, KD, 48)
        k_stage = at(R_Z, 2, TT, CH)
        gateT = at(R_Z + 2560, NT)
        gate_tb = at(R_Z + 3136, DS, DB)
        v_sb = at(R_F, 2, TT, CH)
        ktz = at(R_F + 2560, 2, KV, SEQ)
        qT = at(R_H, KD, NT)
        yT = at(R_Z, KD, NT)
        sz = at(R_G, NBR, 2, SEQ)
        tb = at(R_G + 6144, 2, 2, SEQ)
        pt_sb = at(R_G + 8192, 4, SEQ)
        y_tmp = at(R_G + 10240, SEQ)
        qbd = at(R_G + 10752, DB, 2, HD)
        l_sb = at(R_RING + (TRING + HRING) * D, 6, SEQ)
        szs = at(R_G + 4096, NBR, KD, NS)
        pc_sb = at(R_X + 4608, 4, P)
        cache_sb = [at(R_C + 1024 * i, 2, 512) for i in range(4)] + [at(R_G + 1024 * i, 2, 512) for i in range(2)]
        kts = at(R_G + 6144, 2, 2, KS)
        pts = at(R_G + 8192, 2, 3, P)
        vnew = at(R_G + 8960, 6, CH, p1=DS)
        ptc = at(R_H, DB, P, p1=4 * NCS)
        orc = at(R_H + 1024, DB, P)
        y_br = at(R_H + 2048, 2, KD, NS)
        orow = at(R_H + 3072, 2, P)
        x1_back = at(R_F + 2560, 2, D)
        gpost_b = at(R_F + 2560 + 2 * D, D)
        junk_c = at(R_F + 2560 + 3 * D, D)
        y_out = at(R_G + 2048, 2, D)
        small = [R_P]

        def keep(*dims):
            off = small[0]
            small[0] += int(np.prod(dims))
            return at(off, *dims)

        ident = keep(P)
        kc_s = keep(DB, 4 * NCS)
        late_slots = at(small[0], 2, KV, P)
        vc_s = keep(DB, P)
        bs = keep(KS)
        bsc = keep(4 * NCS)
        kt_new = keep(2, 2, NS)
        kcbd = keep(2, 64)
        vcbd = keep(2, P)
        pe_sb = keep(2, 16)
        pecol = keep(4)
        ss, ms, sd, rs = (keep(8) for _ in range(4))
        mn, den, rden = (keep(8 + 6) for _ in range(3))
        w2_off = small[0]
        w2_sb = keep(2, 2, P)
        gR = at(w2_off, 4, NBR * H)
        gS = at(w2_off + 192, NBR, DB)
        e2 = at(w2_off + 216, 2, 55)
        gRr = at(w2_off + 326, 4, H)
        assert small[0] <= 53150, small[0]

        def sem(name):
            return ctx.enter_context(nc.semaphore(name))

        S = {n: sem(n) for n in """
            zeroed ident_ready ones_ready zeroes vec_in vec_ps vec_ready state_in bias_in early_mm line_part line_out
            sq_a ms_a sd_a xn_a_ready tr_a h_ready state_tr state_ready
            proj_a sg_ready glu_ready z_ready conv_step
            page_in w1_in pe_in pe_sb_ready pe_ready w2_in ct_tr ct_ready cs_mm pe_col hid_ready kc_mm kc_ready vc_mm vc_ready
            centred sqd stat_mm eps_ready std_ready lnx_ready lns_ready y_ready
            co_tr co_ready co_out new_packed late
            o_mm gpost_in sq_b ms_b sd_b o_scaled x1_ready sq_c ms_c sd_c xn_b_ready tr_b hu_ready x1_out
            kv_mm kv_ready uh_ready ul_ready hi_ready lo_ready kt_tr kt_ready ctp_tr ctp_ready kv_out cp_mm hidp_ready cpp_mm bd_ready
            q_mm q_ready wg_in gate_mm gate_ready gate_tr gR_ready gate_out gS_in qbd_ready
            z_mm zb_ready silu_ready bs_in bsc_ready
            e2_ready s_done l_ready cmin_ready exp_done den_ready pn_ready
            t_done pt_a pt_d pv_done y_mul y_add
            skt_tr skt_ready kts_new ss_mm sl_ready se_ready sp_ready st_tr pts_ready so_mm or_ready ot_tr ys_mul y_s
            fo_mm fy
            """.split()}
        ZEROED = {"pad": 1, "slot": 2, "blocks": 4, "bias": 5, "keys": 9, "probs": 10, "table": 11, "queries": 12}
        w_in = [sem(f"w_in{i}") for i in range(RING)]
        x_in = [sem(f"x_in{i}") for i in range(TT)]
        rows_in = [sem(f"rows_in{i}") for i in range(4)]
        tb_in = [sem(f"tb_in{i}") for i in range(2)]
        slot_in = [sem(f"slot_in{i}") for i in range(TRING)]
        fy_out = [sem(f"fy_out{i}") for i in range(2)]
        dve_step = sem("dve_step")
        n_dve = [0]

        def kv_bank(n):
            return (2, 3, 0, 1, 4, 5)[n % 6]

        def rows_slot(n):
            return rows_ring[:, n % 4] if n % 4 < 2 else late_slots[:, n % 4 - 2]

        def link(dve, ins):
            n_dve[0] += 1
            ins.then_inc(dve_step, 1)
            dve.wait_ge(dve_step, n_dve[0])

        def cols(w, c0):
            return [(w[:, c0:c0 + CH].rearrange("(k p) n -> p k n", p=P), None)]

        def tile_cols(w, c0, m):
            c = c0 + ((m // 4) * 8 + m % 4) * HD
            return [(w[:, c + half * 256:c + half * 256 + HD].rearrange("(k p) n -> p k n", p=P), half * HD) for half in range(2)]

        a_w = I["a_w_in"][0]
        b_w = I["b_w_in"][0]
        chunks = []
        for c in range(4):
            chunks += [cols(a_w, c * CH), cols(a_w, D + c * CH), cols(a_w, 2 * D + c * CH)]
        C_OA = len(chunks)
        chunks += [cols(I["a_w_out"][0], c * CH) for c in range(4)]
        C_KV = len(chunks)
        chunks += [cols(I["w_kv"], c * CH) for c in range(6)]
        C_Q = len(chunks)
        chunks += [tile_cols(b_w, 0, m) for m in range(KD)]
        C_Z = len(chunks)
        chunks += [tile_cols(b_w, D * (1 + br), m) for m in range(KD) for br in range(NBR)]
        C_OB = len(chunks)
        for c in range(4):
            parts = []
            for p in range(2):
                for half in range(2):
                    r = p * 512 + half * 256
                    parts.append((I["b_w_out"][0][r:r + 256, c * CH:(c + 1) * CH].rearrange("(g d) n -> d g n", d=HD),
                                  ("out", p, half)))
            chunks.append(parts)

        last_use = {}
        for n in range(12):
            last_use[n] = ("proj_a", 3 * (2 * (n // 3) + 1) + n % 3 + 1)
        for n in range(4):
            last_use[C_OA + n] = ("o_mm", TT)
        for n in range(6):
            last_use[C_KV + n] = ("kv_mm", TT * (n + 1))
        for m in range(KD):
            last_use[C_Q + m] = ("q_mm", m + 1)
        for n in range(NBR * KD):
            last_use[C_Z + n] = ("z_mm", n + 1)

        place = {}
        for c in range(len(chunks)):
            if C_Q <= c < C_OB:
                i = (c - C_Q) % TRING
                place[c] = (D * i, D, slot_in[i])
            else:
                i = (4, 5, 3, 0, 1, 2)[c - C_KV] if C_KV <= c < C_Q else c % RING if c < C_KV else c - C_OB
                place[c] = (2 * D * i, 2 * D, w_in[i])
        waited = {}

        def frees(c):
            lo, n, _ = place[c]
            need = {"z_mm": NBR * KD} if c == C_OB + 3 else {}
            for b in range(c):
                if place[b][0] < lo + n and lo < place[b][0] + place[b][1]:
                    name, count = last_use[b]
                    need[name] = max(count, need.get(name, 0))
            need = {k: v for k, v in need.items() if v > waited.get(k, 0)}
            waited.update(need)
            return need.items()

        def chunk_sb(c):
            return ring[:, place[c][0] // (2 * D)]

        def chunk_dst(c, how):
            if C_Q <= c < C_OB:
                return tile_w[:, (c - C_Q) % TRING, :, how:how + HD]
            slot = chunk_sb(c)
            if how is None:
                return slot
            _, p, half = how
            return slot[half * HD:half * HD + HD, 4 * p:4 * p + 4, :]

        arrived, totals = {}, {}
        for c, parts in enumerate(chunks):
            into = place[c][2]
            totals[into] = totals.get(into, 0) + 16 * len(parts)
            arrived[c] = totals[into]

        def product_before(j):
            j -= HRING
            return ("q_mm", j + 1) if j < KD else ("z_mm", j - KD + 1)

        def rows(t):
            return P if t < 4 else NS

        UPM = 1 + 2 * 2 * 4
        items = []
        for m in range(KD):
            items.append((m, 0, None, [UPM * m]))
            for br in (1, 2):
                for i in range(4):
                    u = UPM * m + 1 + 8 * (br - 1) + 2 * i
                    items.append((m, br, i, [u, u + 1]))
        item_of = {u: w for w, it in enumerate(items) for u in it[3]}
        pt_by, n_a, n_d = {}, 0, 0
        for w, (m, br, i, us) in enumerate(items):
            for k, u in enumerate(us):
                if br and k == 0:
                    n_a += 1
                    pt_by[u] = ("pt_a", n_a)
                else:
                    n_d += 1
                    pt_by[u] = ("pt_d", n_d)
        N_UNITS = UPM * KD
        KV_OUT = 16 * (2 * 5 + 2 * 2 + 2 * (1 + DB))

        def stat(w):
            return 8 + 2 * (w % 3)

        z_at = {9 * (m - 1) + 3 * br + 1: NBR * m + br for m in range(1, KD) for br in range(NBR)}

        block = ctx.enter_context(nc.Block())

        @block.sync
        def _(sp):
            for t in range(TT):
                src = I["x_prompt"][0, t * P:(t + 1) * P, :] if t < 4 else I["x_sample"].rearrange("b t d -> (b t) d")
                sp.dma_start(x_sb[0:rows(t), t], src).then_inc(x_in[t], 16)
            sp.dma_start(vec_rows[0:W], I["a_conv_w"][0]).then_inc(S["vec_in"], 16)
            for n, name in enumerate(("a_norm_pre", "a_conv_b", "a_ln_g", "a_ln_b", "kv_norm", "b_norm_pre")):
                src = I[name].rearrange("(a n) -> a n", a=1) if name == "kv_norm" else I[name]
                sp.dma_start(vec_rows[W + n:W + n + 1], src).then_inc(S["vec_in"], 16)

            def tables(m):
                if m < 2:
                    sp.wait_ge(S["line_out"], 80)
                    sp.wait_ge(S["cp_mm"], 4)
                else:
                    sp.wait_ge(S["e2_ready"], m - 1)
                    sp.wait_ge(S["l_ready"], UPM * (m - 1))
                for half in range(2):
                    h = 8 * (m // 4) + 4 * half + m % 4
                    src = bass.AP(bias_copies.tensor, h * P * NX + P - 1, [[NX - 1, P], [1, SEQ]])
                    sp.dma_start(tb[:, m % 2, half], src).then_inc(tb_in[m % 2], 16)

            tables_at = {C_Z + 6: (0, 1), C_Z + 12: (2,), C_Z + 15: (3,), C_Z + 18: (4,), C_Z + 21: (5,), C_OB: (6, 7)}
            for c, parts in enumerate(chunks):
                for m in tables_at.get(c, ()):
                    tables(m)
                for name, count in frees(c):
                    sp.wait_ge(S[name], count)
                for src, how in parts:
                    sp.dma_start(chunk_dst(c, how), src).then_inc(place[c][2], 16)
                if c == 0:
                    for i in range(2):
                        sp.dma_start(state_rows[0:120, i], I["state_conv"][0, 4 * i:4 * i + 4].rearrange("b r n -> (b r) n")).then_inc(S["state_in"], 16)
                    sp.dma_start(rel_rows, I["rel_bias"]).then_inc(S["bias_in"], 16)
                    sp.dma_start(hot_rows, I["bucket_rows"]).then_inc(S["bias_in"], 16)
                    for k in range(2):
                        sp.dma_start(pe_rows[:, k], I["cmp_pe"][k].rearrange("(j a) d -> j (a d)", a=2)).then_inc(S["pe_in"], 16)
                if c == 3:
                    for k in range(2):
                        for ht in range(2):
                            for dup in range(2):
                                sp.dma_start(w2_sb[:, k, ht, dup * HD:(dup + 1) * HD], I["cmp_w2"][k, ht * P:(ht + 1) * P, :]).then_inc(S["w2_in"], 16)
                if c == 6:
                    sp.wait_ge(S["line_part"], 2)
                    sp.dma_start(bias_dram, line).then_inc(S["line_out"], 16)
                if 7 <= c < 11:
                    sp.wait_ge(S["line_out"], 16 * (c - 6))
                    h0 = 4 * (c - 7)
                    sp.dma_start(bias_copies[h0:h0 + 4], bias_dram[h0:h0 + 4].unsqueeze(1).broadcast_to([4, P, NX])).then_inc(S["line_out"], 16)
                if c == 11:
                    sp.wait_ge(S["line_out"], 80)
                    sp.dma_start(bs, bass.AP(bias_copies.tensor, SEQ - 1 - PAST, [[P * NX, H], [NX - 1, DS], [1, KS]])).then_inc(S["bs_in"], 16)
                if c == 2:
                    sp.dma_start(w1_sb, I["cmp_w1"][0].rearrange("(j p) n -> p j n", p=P)).then_inc(S["w1_in"], 16)
                if c == C_OA + 1:
                    sp.wait_ge(S["cs_mm"], 2)
                    sp.dma_start(w1_sb, I["cmp_w1"][1].rearrange("(j p) n -> p j n", p=P)).then_inc(S["w1_in"], 16)
                if c == C_Q + 5:
                    sp.wait_ge(S["cp_mm"], 2)
                    sp.dma_start(w1_sb, I["cmp_w1"][0].rearrange("(j p) n -> p j n", p=P)).then_inc(S["w1_in"], 16)
            sp.wait_ge(S["z_mm"], 24)
            sp.wait_ge(S["page_in"], 16)

            def past_rows(n):
                b, br = n // 2, n % 2
                for pg in range(2):
                    if br == 0:
                        v = sp.value_load(page_sb[0:1, 2 * b + pg:2 * b + pg + 1], min_val=0, max_val=I["cache_slc"].shape[0] - 1)
                        src = I["cache_slc"].rearrange("g s c k d -> g s (c k d)")[bass.ds(v, 1), :, :].rearrange("a s n -> (a s) n")
                    else:
                        src = I["state_win"][b, pg * P:(pg + 1) * P].rearrange("s c k d -> s (c k d)")
                    sp.dma_start(cache_sb[n % 6][:, pg], src).then_inc(slot_in[n % 6], 16)

            def new_v_rows(n):
                b, br = n // 2, n % 2
                sp.dma_start(vnew[:, n % 6], v_sb[DS * b:DS * b + DS, br, 4, :]).then_inc(slot_in[n % 6], 16)

            def x1_rows(t):
                if t >= 2:
                    sp.wait_ge(S["fy"], t - 1)
                sp.dma_start(x1_back[0:rows(t), t % 2], x1_dram[t * P:t * P + rows(t), :]).then_inc(x_in[t % 2], 16)

            for n in range(4):
                past_rows(n)
            sp.wait_ge(S["x1_out"], 16 * TT)
            sp.wait_ge(S["t_done"], N_UNITS)
            sp.dma_start(gpost_b, I["b_norm_post"][0:1, :].broadcast_to([P, D])).then_inc(S["gpost_in"], 16)
            x1_rows(0)
            x1_rows(1)
            sp.wait_ge(S["y_mul"], 24)
            sp.wait_ge(S["pv_done"], len(items))
            sp.wait_ge(S["y_add"], 2 * KD)
            for n in range(2 * DB):
                if n >= 6:
                    sp.wait_ge(S["so_mm"], n - 4)
                if n >= 4:
                    past_rows(n)
                new_v_rows(n)
                if n in (8, 12):
                    x1_rows(n // 4)
            x1_rows(4)
            for t in range(2):
                sp.wait_ge(x_in[t], 16 * (4 - t))

        @block.gpsimd
        def _(pool):
            pool.memset(ident, 0.0).then_inc(S["zeroed"], 1)
            pool.wait_ge(S["zeroed"], 1)
            pool.affine_select(out=ident, in_=ident, compare_op=ALU.not_equal, fill=1.0, base=0,
                               pattern=[[-1, P]], channel_multiplier=1).then_inc(S["ident_ready"], 1)
            pool.dma_start(page_sb[:, :], I["page_table"].rearrange("b (g a) -> a (b g)", a=1)).then_inc(S["page_in"], 16)
            pool.memset(line[:, SEQ:NX], BIG).then_inc(S["line_part"], 1)
            pool.memset(ones, 1.0 / D).then_inc(S["ones_ready"], 1)
            pool.memset(glu_p[:, :, 0:W - 1], 0.0).then_inc(S["zeroes"], 1)
            pool.memset(ctS[:, :, 32, :], 0.0).then_inc(S["zeroes"], 1)
            pool.memset(kcbd, 0.0).then_inc(S["zeroes"], 1)
            pool.memset(vcbd, 0.0).then_inc(S["zeroes"], 1)
            pool.memset(bsc, BIG).then_inc(S["zeroes"], 1)
            pool.wait_ge(S["page_in"], 16)
            cache = I["cache_cmp"].rearrange("g (s a) c k d -> g s a c k d", a=2)
            for c in range(2):
                for b in range(DB):
                    n = DB * c + b
                    if n >= 4:
                        pool.wait_ge(S["ct_tr"], n - 3)
                    for pg in range(2):
                        v = pool.value_load(page_sb[0:1, 2 * b + pg:2 * b + pg + 1], min_val=0, max_val=I["cache_cmp"].shape[0] - 1)
                        for par in range(2):
                            src = cache[bass.ds(v, 1), :, par, c, :, :]
                            pool.dma_start(rows_slot(n)[pg * 64:pg * 64 + 64, :, par * HD:(par + 1) * HD],
                                           src.rearrange("g s k d -> (g s) k d")).then_inc(rows_in[n % 4], 16)
            pool.dma_start(O["conv_sample"][0, :, 0:W - 1 - DS, :], I["state_conv"][0, :, DS:W - 1, :]).then_inc(S["late"], 16)
            pool.dma_start(O["win_sample"][:, 0:PAST], I["state_win"]).then_inc(S["late"], 16)
            pool.wait_ge(S["z_ready"], KD)
            for m in range(KD):
                pool.wait_ge(S["lns_ready"], m + 1)
                pool.tensor_tensor(out=zA[:, m], in0=conv[:, m], in1=zA[:, m], op=ALU.mult).then_inc(S["y_ready"], 1)
            pool.wait_ge(S["tr_b"], TT)
            pool.wait_ge(S["x1_ready"], TT)
            pool.wait_ge(S["sq_c"], TT)
            for lo in range(2):
                for br in range(2):
                    pool.memset(ktz[64 - 64 * lo:P - 64 * lo, br, lo:KV:2, :], 0.0).then_inc(S["zeroes"], 1)
            pool.wait_ge(S["x1_out"], 16 * TT)
            pool.wait_ge(S["xn_b_ready"], TT)
            pool.wait_ge(S["zeroes"], ZEROED["keys"])
            pool.memset(pc_sb, 0.0).then_inc(S["zeroes"], 1)
            pool.wait_ge(S["cpp_mm"], 2)
            pool.wait_ge(S["gate_mm"], 1)
            pool.wait_ge(S["kv_out"], KV_OUT)
            pool.memset(e2, BIG).then_inc(S["zeroes"], 1)
            pool.memset(qbd, 0.0).then_inc(S["zeroes"], 1)
            pool.wait_ge(S["gR_ready"], 5)
            for w in range(len(items) + 3):
                if w < len(items):
                    m, br, i, us = items[w]
                    pool.wait_ge(S["den_ready"], w + 1)
                    if br == 0:
                        if m == 0:
                            pool.wait_ge(S["zeroes"], ZEROED["probs"])
                        else:
                            pool.wait_ge(S["t_done"], UPM * (m - 1) + 1)
                        dst = pc_sb[:, :, 0:64].rearrange("q i (h n) -> q i h n", h=2)[:, :, :, 0:NCP]
                        src = l_sb[:, us[0] % 6, 0:8 * NCP].rearrange("q (i h n) -> q i h n", i=4, h=2)
                        r = rden[:, 0:8].rearrange("q (i h) -> q i h", i=4).unsqueeze(3).broadcast_to([P, 4, 2, NCP])
                        pool.tensor_tensor(out=dst, in0=src, in1=r, op=ALU.mult).then_inc(S["pn_ready"], 1)
                    else:
                        for half, u in enumerate(us):
                            h = br * H + 8 * (m // 4) + 4 * half + m % 4
                            L = l_sb[:, u % 6, 0:P * (i + 1)]
                            pool.tensor_scalar(L, L, rden[:, stat(w) + half:stat(w) + half + 1], gR[:, i, h:h + 1],
                                               ALU.mult, ALU.mult).then_inc(S["pn_ready"], 1)
                if w >= 3 and items[w - 3][1] and items[w - 3][2] == 3:
                    m, br = items[w - 3][:2]
                    pool.wait_ge(S["y_mul"], 3 * m + br + 1)
                    if br == 2:
                        pool.wait_ge(S["y_add"], 2 * m + 1)
                    pool.tensor_tensor(out=yT[:, m, 0:SEQ], in0=yT[:, m, 0:SEQ], in1=y_tmp, op=ALU.add).then_inc(S["y_add"], 1)
            for n in range(2 * DB):
                b, br = n // 2, n % 2
                if n >= 2:
                    pool.wait_ge(S["ss_mm"], n)
                else:
                    pool.wait_ge(S["l_ready"], N_UNITS)
                pool.tensor_copy(kts[:, n % 2, :, PAST:KS], kt_new[:, br, :, DS * b:DS * b + DS]).then_inc(S["kts_new"], 1)

        @block.scalar
        def _(act):
            def copy(out, in_, scale=1.0):
                return nc.scalar.activation(out, in_, ACT.Copy, scale=scale)

            for t in range(TT):
                r = rows(t)
                act.wait_ge(x_in[t], 16)
                if t:
                    act.wait_ge(S["sq_a"], t)
                nc.scalar.activation(junk_a[0:r], x_sb[0:r, t], ACT.Square, accum_out=ss[0:r, t:t + 1]).then_inc(S["sq_a"], 1)
            for t in range(TT):
                r = rows(t)
                act.wait_ge(S["ms_a"], t + 1)
                nc.scalar.activation(sd[0:r, t:t + 1], ms[0:r, t:t + 1], ACT.Sqrt).then_inc(S["sd_a"], 1)
            act.wait_ge(S["early_mm"], 1)
            copy(line[:, 0:SEQ], pb(0, SEQ, p1=H), -1.0).then_inc(S["line_part"], 1)
            act.wait_ge(S["early_mm"], 2)
            copy(pe_sb, pb(1, 2, 16)).then_inc(S["pe_sb_ready"], 1)
            act.wait_ge(S["pe_sb_ready"], 1)
            act.wait_ge(S["zeroes"], ZEROED["slot"])

            def pe_slot(c):
                copy(ctS[:, :, 32, 0:2].rearrange("p j c -> p c j"), pe_sb[:, c].rearrange("p (c j) -> p c j", c=2)).then_inc(S["pe_ready"], 1)

            pe_slot(0)
            for n in range(4):
                i, mg = n // 2, n % 2
                act.wait_ge(S["state_tr"], n + 1)
                for b in range(4):
                    copy(glu_s[:, 4 * mg:4 * mg + 4, 4 * i + b, 0:W - 1],
                         pb(6 + n % 2, 4, 120)[:, :, b * (W - 1):(b + 1) * (W - 1)]).then_inc(S["state_ready"], 1)

            def ct_copy(n):
                b = n % DB
                act.wait_ge(S["ct_tr"], n + 1)
                copy(ctS[:, :, KV * b:KV * b + KV, :].rearrange("p j s c -> p s c j"), pb(6 + n % 2, KV, 16, 8)).then_inc(S["ct_ready"], 1)

            def compress_silu(c):
                for ht in range(2):
                    act.wait_ge(S["cs_mm"], 2 * c + ht + 1)
                    copy(pecol[:, 2 * c + ht:2 * c + ht + 1], pb(6 + ht, 495)[:, 480:481]).then_inc(S["pe_col"], 1)
                    act.wait_ge(S["pe_col"], 2 * c + ht + 1)
                    if c:
                        act.wait_ge(S["kc_mm"], 1)
                    nc.scalar.activation(hid[:, ht], pb(6 + ht, 480), ACT.Silu, bias=pecol[:, 2 * c + ht:2 * c + ht + 1]).then_inc(S["hid_ready"], 1)

            for m in range(KD):
                if m == 7:
                    compress_silu(0)
                    pe_slot(1)
                act.wait_ge(S["proj_a"], 3 * m + 2)
                if m >= 2:
                    act.wait_ge(S["glu_ready"], 3 * (m - 1))
                else:
                    act.wait_ge(S["vec_ps"], 1)
                nc.scalar.activation(sg[:, m % 2].rearrange("p (a n) -> p a n", a=2), halves(2), ACT.Sigmoid).then_inc(S["sg_ready"], 1)
                if m < 3:
                    for n in range(3 * m, min(3 * m + 3, DB)):
                        ct_copy(n)
                if m == 7:
                    act.wait_ge(S["kc_mm"], 1)
                    copy(kc_s.rearrange("p b n -> p (b n)"), pb(6, 480)).then_inc(S["kc_ready"], 1)
                act.wait_ge(S["proj_a"], 3 * m + 3)
                if m == 0:
                    act.wait_ge(S["sq_a"], TT)
                if m == 3:
                    act.wait_ge(S["line_out"], 16)
                nc.scalar.activation(zA[:, m].rearrange("p (a n) -> p a n", a=2), halves(4), ACT.Silu).then_inc(S["z_ready"], 1)

            for b in range(6):
                ct_copy(DB + b)
            act.wait_ge(S["glu_ready"], 3 * KD)
            for m in range(KD):
                act.wait_ge(S["centred"], m + 1)
                if m >= 2:
                    act.wait_ge(S["stat_mm"], m)
                nc.scalar.activation(sg[:, m % 2], conv[:, m], ACT.Square).then_inc(S["sqd"], 1)
            for b in range(6, DB):
                ct_copy(DB + b)
            act.wait_ge(S["eps_ready"], 1)
            nc.scalar.activation(rstd_ln, rstd_ln, ACT.Sqrt).then_inc(S["std_ready"], 1)
            for m in range(KD):
                act.wait_ge(S["lnx_ready"], m + 1)
                nc.scalar.activation(conv[:, m], conv[:, m], ACT.Silu, scale=vecT[:, m, W + 2:W + 3],
                                     bias=vecT[:, m, W + 3:W + 4]).then_inc(S["lns_ready"], 1)
            compress_silu(1)
            act.wait_ge(S["vc_mm"], 1)
            copy(vc_s[0:60].rearrange("p b n -> p (b n)"), pb(4, 1024, p1=60)).then_inc(S["vc_ready"], 1)
            act.wait_ge(S["co_tr"], 1)
            copy(conv_out_p[0:W - 1], pb(0, D, p1=W - 1)).then_inc(S["co_ready"], 1)
            act.wait_ge(S["co_tr"], 2)
            copy(conv_out_s[0:NS], pb(2, D, p1=NS)).then_inc(S["co_ready"], 1)
            act.wait_ge(S["co_ready"], 2)
            act.dma_start(O["conv_prompt"][0, 0], conv_out_p[0:W - 1]).then_inc(S["co_out"], 16)
            for b in range(DB):
                act.dma_start(O["conv_sample"][0, b, W - 1 - DS:W - 1], conv_out_s[DS * b:DS * b + DS]).then_inc(S["co_out"], 16)
            act.dma_start(gpost_a, I["a_norm_post"][0:1, :].broadcast_to([P, D])).then_inc(S["gpost_in"], 16)

            for t in range(TT):
                r = rows(t)
                act.wait_ge(S["o_mm"], t + 1)
                if t:
                    act.wait_ge(S["sq_c"], t)
                    act.wait_ge(S["o_scaled"], t)
                nc.scalar.activation(junk_b[0:r], pb(2 * (t % 2), D, p1=r), ACT.Square, accum_out=ss[0:r, 0:1]).then_inc(S["sq_b"], 1)
                act.wait_ge(S["ms_b"], t + 1)
                nc.scalar.activation(sd[0:r, 0:1], ms[0:r, 0:1], ACT.Sqrt).then_inc(S["sd_b"], 1)
                act.wait_ge(S["x1_ready"], t + 1)
                act.dma_start(x1_dram[t * P:t * P + r, :], x_sb[0:r, t]).then_inc(S["x1_out"], 16)
                act.wait_ge(S["sq_b"], t + 1)
                nc.scalar.activation(junk_b[0:r], x_sb[0:r, t], ACT.Square, accum_out=ss[0:r, 1:2]).then_inc(S["sq_c"], 1)
                act.wait_ge(S["ms_c"], t + 1)
                nc.scalar.activation(sd[0:r, 1:2], ms[0:r, 1:2], ACT.Sqrt).then_inc(S["sd_c"], 1)

            act.wait_ge(S["vc_mm"], 1)
            act.dma_start(wgate, b_w[:, 4 * D:4 * D + 48].rearrange("(k p) n -> p k n", p=P)).then_inc(S["wg_in"], 16)
            def split_hi(j):
                if j == KD:
                    act.wait_ge(S["wg_in"], 16)
                    act.wait_ge(S["o_mm"], TT)
                    copy(wgate_hi, wgate).then_inc(S["hi_ready"], 1)
                    return
                j -= j > KD
                act.wait_ge(slot_in[j % TRING], arrived[C_Q + j])
                if j >= HRING:
                    name, count = product_before(j)
                    act.wait_ge(S[name], count)
                copy(tile_hi[:, j % HRING], tile_w[:, j % TRING]).then_inc(S["hi_ready"], 1)

            for c in range(6):
                br, kind = c // 2, c % 2
                if c == 2:
                    act.wait_ge(S["x1_out"], 16 * TT)
                    act.wait_ge(S["xn_b_ready"], TT)
                    act.wait_ge(S["hu_ready"], 2 * TT)
                    for m in range(KD):
                        copy(u_hi[:, m], uT[:, m]).then_inc(S["uh_ready"], 1)
                if c == 5:
                    for j in range(HRING):
                        split_hi(j)
                for t in range(TT):
                    n = TT * c + t
                    r = rows(t)
                    act.wait_ge(S["kv_mm"], n + 1)
                    src = pb(kv_bank(n), CH, p1=r)
                    if br == 0 and t < 4:
                        dst = cmp_rows[:, t // 2, kind, :, HD * (t % 2):HD * (t % 2) + HD]
                        src = src.rearrange("p (k d) -> p k d", d=HD)
                    elif br == 0:
                        dst = cmp_rows_s[0:r, kind * CH:(kind + 1) * CH]
                    else:
                        dst = (v_sb if kind else k_stage)[0:r, br - 1, t]
                    copy(dst, src).then_inc(S["kv_ready"], 1)
                act.wait_ge(S["kv_ready"], TT * (c + 1))
                if br == 0:
                    for gi in range(2):
                        for par in range(2):
                            dst = O["cmp_prompt"][0, gi * 256:(gi + 1) * 256, kind].rearrange("(q a) k d -> q a k d", a=2)[:, par]
                            act.dma_start(dst, cmp_rows[:, gi, kind, :, par * HD:par * HD + HD]).then_inc(S["kv_out"], 16)
                    act.dma_start(O["cmp_sample"][:, :, kind].rearrange("b t k d -> (b t) (k d)"),
                                  cmp_rows_s[0:NS, kind * CH:(kind + 1) * CH]).then_inc(S["kv_out"], 16)
                    continue
                name, R = ("slc", "win")[br - 1], (v_sb if kind else k_stage)
                dst = O[name + "_prompt"][0, :, kind].rearrange("(t p) k d -> p t (k d)", p=P)
                act.dma_start(dst, R[:, br - 1, 0:4]).then_inc(S["kv_out"], 16)
                if br == 1:
                    act.dma_start(O["slc_sample"][:, :, kind].rearrange("b t k d -> (b t) (k d)"), R[0:NS, 0, 4]).then_inc(S["kv_out"], 16)
                    continue
                for b in range(DB):
                    act.dma_start(O["win_sample"][b, PAST:KS, kind].rearrange("t k d -> t (k d)"),
                                  R[DS * b:DS * b + DS, 1, 4]).then_inc(S["kv_out"], 16)
            def compress_p_silu(n, c):
                for ht in range(2):
                    act.wait_ge(S["cp_mm"], 2 * n + ht + 1)
                    if n:
                        act.wait_ge(S["cpp_mm"], 1)
                    nc.scalar.activation(hid_p[:, ht], pb(4 + ht, 124), ACT.Silu, bias=pecol[:, 2 * c + ht:2 * c + ht + 1]).then_inc(S["hidp_ready"], 1)
                act.wait_ge(S["cpp_mm"], n + 1)
                act.wait_ge(S["zeroes"], ZEROED["blocks"])
                for p in range(2):
                    for half in range(2):
                        lo = HD * half
                        if c:
                            copy(vcbd[32 * half:32 * half + NCP, p, lo:lo + HD],
                                 pb(2 + p, HD, p0=32 * half, p1=32 * half + NCP)).then_inc(S["bd_ready"], 1)
                        else:
                            copy(kcbd[lo:lo + HD, p, 32 * half:32 * half + NCP],
                                 pb(0, KV, NCP, p0=lo, p1=lo + HD)[:, 2 * p + half]).then_inc(S["bd_ready"], 1)

            compress_p_silu(0, 1)
            for m in range(KD):
                act.wait_ge(S["q_mm"], m + 1)
                copy(qT[:, m].rearrange("p (a n) -> p a n", a=2), halves(2 * (m % 3)), QSCALE).then_inc(S["q_ready"], 1)
                split_hi(m + HRING)
            split_hi(KD + HRING)
            act.wait_ge(S["gate_mm"], 1)
            nc.scalar.activation(gateT[0:48].rearrange("p (a n) -> p a n", a=2), halves(6)[0:48], ACT.Sigmoid).then_inc(S["gate_ready"], 1)
            act.wait_ge(S["gate_ready"], 1)
            copy(gate_tb[0:48], gateT[0:48, SEQ:NT].rearrange("r (b t) -> r t b", b=DB)).then_inc(S["gate_ready"], 1)
            act.wait_ge(S["gate_ready"], 2)
            act.dma_start(gate_dram, gate_tb[0:48].rearrange("r t b -> r (t b)")).then_inc(S["gate_out"], 16)
            compress_p_silu(1, 0)
            act.wait_ge(S["gate_out"], 16)
            for br in range(NBR):
                act.dma_start(gS[:, br], bass.AP(gate_dram.tensor, br * H * NS, [[DB, P], [1, DB]])).then_inc(S["gS_in"], 16)

            def z_copy(n, b0):
                m, br = n // NBR, n % NBR
                act.wait_ge(S["z_mm"], n + 1)
                if m >= 2:
                    act.wait_ge(S["y_mul"], 3 * (m - 2) + br + 1)
                lo, hi = pb(b0, HT), pb(b0 + 1, HT)
                copy(sz[:, br, m % 2, 0:HT], lo).then_inc(S["zb_ready"], 1)
                copy(sz[:, br, m % 2, HT:SEQ], hi[:, 0:SEQ - HT]).then_inc(S["zb_ready"], 1)
                copy(szs[:, br, m], hi[:, SEQ - HT:HT]).then_inc(S["zb_ready"], 1)

            def z_silu(m):
                act.wait_ge(S["zb_ready"], 3 * NBR * (m + 1))
                for z in (sz[:, :, m % 2], szs[:, :, m]):
                    nc.scalar.activation(z, z, ACT.Silu).then_inc(S["silu_ready"], 1)

            act.wait_ge(S["x1_out"], 16 * TT)
            act.wait_ge(S["cp_mm"], 4)
            act.wait_ge(S["kv_out"], KV_OUT)
            for n in range(NBR):
                z_copy(n, 2 * (n % 2))
                split_hi(KD + 1 + n + HRING)
            z_silu(0)

            for w in range(len(items) + 2):
                if w < len(items):
                    m, br, i, us = items[w]
                    act.wait_ge(S["l_ready"], us[-1] + 1)
                    if br == 0:
                        act.wait_ge(S["cmin_ready"], m + 1)
                        L = l_sb[:, us[0] % 6, 0:8 * NCP]
                        nc.scalar.activation(L, L, ACT.Exp, scale=-1.0).then_inc(S["exp_done"], 1)
                    else:
                        if w >= 3:
                            act.wait_ge(S["den_ready"], w - 2)
                        for half, u in enumerate(us):
                            L = l_sb[:, u % 6, 0:P * (i + 1)]
                            k = stat(w) + half
                            nc.scalar.activation(L, L, ACT.Exp, scale=-1.0, bias=mn[:, k:k + 1],
                                                 accum_out=den[:, k:k + 1]).then_inc(S["exp_done"], 1)
                if w >= 2 and items[w - 2][1]:
                    i, u = items[w - 2][2], items[w - 2][3][0]
                    act.wait_ge(S["t_done"], u + 1)
                    if u >= 4:
                        act.wait_ge(S["pv_done"], item_of[u - 4] + 1)
                    copy(pt_sb[:, u % 4, 0:P * (i + 1)], pb(3 + u % 2, P * (i + 1))).then_inc(S["pt_a"], 1)
                if w in z_at:
                    z_copy(z_at[w], 6)
                if w - 1 in z_at and z_at[w - 1] + HRING < NBR * KD:
                    split_hi(KD + 1 + z_at[w - 1] + HRING)
                if w % 9 == 8 and w < 9 * (KD - 1):
                    z_silu(w // 9 + 1)

            def last_square(t):
                r = rows(t)
                act.wait_ge(S["fo_mm"], t + 1)
                if t:
                    act.wait_ge(S["sq_a"], TT + t)
                else:
                    act.wait_ge(S["t_done"], N_UNITS)
                nc.scalar.activation(junk_c[0:r], pb(4 + 2 * (t % 2), D, p1=r), ACT.Square, accum_out=ss[0:r, t:t + 1]).then_inc(S["sq_a"], 1)

            def last_root(t):
                r = rows(t)
                act.wait_ge(S["ms_a"], TT + t + 1)
                nc.scalar.activation(sd[0:r, t:t + 1], ms[0:r, t:t + 1], ACT.Sqrt).then_inc(S["sd_a"], 1)

            def last_out(t):
                act.wait_ge(S["fy"], t + 1)
                dst = O["y_prompt"][0, t * P:(t + 1) * P] if t < 4 else O["y_sample"].rearrange("b t d -> (b t) d")
                act.dma_start(dst, y_out[0:rows(t), t % 2]).then_inc(fy_out[t % 2], 16)

            act.wait_ge(S["cmin_ready"], KD + 1)
            L = l_sb[:, 0, 0:480]
            nc.scalar.activation(L, L, ACT.Exp, scale=-1.0).then_inc(S["exp_done"], 1)
            for n in range(2 * DB + 1):
                if n < 2 * DB:
                    act.wait_ge(S["skt_tr"], n + 1)
                    if n >= 2:
                        act.wait_ge(S["ss_mm"], n)
                    act.wait_ge(S["l_ready"], N_UNITS)
                    copy(kts[:, n % 2, :, 0:PAST], pb(0, 2, PAST)).then_inc(S["skt_ready"], 1)
                if n >= 1:
                    k = n - 1
                    act.wait_ge(S["sl_ready"], k + 2)
                    if k >= 4:
                        act.wait_ge(S["sp_ready"], k - 2)
                    L = l_sb[:, 1 + k % 3, 0:KS]
                    nc.scalar.activation(L, L, ACT.Exp, scale=-1.0, bias=mn[:, 8 + k % 4:9 + k % 4],
                                         accum_out=den[:, 8 + k % 4:9 + k % 4]).then_inc(S["se_ready"], 1)
                if n % 4 == 0 and n < 16:
                    last_square(n // 4)
                    last_root(n // 4)
                if n % 4 == 2 and n < 16:
                    last_out(n // 4)
            last_square(4)
            last_root(4)
            last_out(4)
            act.wait_ge(fy_out[0], 16 * 3)
            act.wait_ge(fy_out[1], 16 * 2)
            act.wait_ge(S["co_out"], 16 * (1 + DB))
            act.wait_ge(S["late"], 32)

        @block.vector
        def _(dve):
            V = nc.vector
            def mean_sq(col, r, name):
                V.tensor_scalar(ms[0:r, col:col + 1], ss[0:r, col:col + 1], 1.0 / D, EPS, ALU.mult, ALU.add).then_inc(S[name], 1)

            def gain(k, r):
                return vecT[:, :, W + k:W + k + 1].broadcast_to([P, KD, r])

            for t in range(TT):
                dve.wait_ge(S["sq_a"], t + 1)
                mean_sq(t, rows(t), "ms_a")
            for t in range(TT + 1):
                if t == 1:
                    dve.wait_ge(S["vec_ps"], 1)
                    V.tensor_copy(vecT, pb(2, KD, 37)).then_inc(S["vec_ready"], 1)
                    dve.wait_ge(S["vec_ready"], 1)
                if t < TT:
                    r = rows(t)
                    dve.wait_ge(S["sd_a"], t + 1)
                    link(dve, V.reciprocal(rs[0:r, t:t + 1], sd[0:r, t:t + 1]))
                    if t >= 2:
                        dve.wait_ge(S["tr_a"], t - 1)
                    V.tensor_scalar(xn_a[0:r, t % 2], x_sb[0:r, t], rs[0:r, t:t + 1], None, ALU.mult).then_inc(S["xn_a_ready"], 1)
                if t:
                    k, r = t - 1, rows(t - 1)
                    dve.wait_ge(S["tr_a"], k + 1)
                    V.tensor_tensor(out=hT[:, :, k * P:k * P + r], in0=pb(4 + 2 * (k % 2), KD, P)[:, :, 0:r], in1=gain(0, r),
                                    op=ALU.mult).then_inc(S["h_ready"], 1)
            dve.wait_ge(S["zeroes"], ZEROED["pad"])
            dve.wait_ge(S["state_ready"], 16)
            for m in range(KD):
                dve.wait_ge(S["proj_a"], 3 * m + 2)
                dve.wait_ge(S["sg_ready"], m + 1)
                a, g = pb(0, 1024), sg[:, m % 2]
                V.tensor_tensor(out=glu_p[:, m, W - 1:W - 1 + HT], in0=a[:, 0:HT], in1=g[:, 0:HT], op=ALU.mult).then_inc(S["glu_ready"], 1)
                V.tensor_tensor(out=glu_p[:, m, W - 1 + HT:W - 1 + SEQ], in0=a[:, 512:512 + SEQ - HT], in1=g[:, HT:SEQ],
                                op=ALU.mult).then_inc(S["glu_ready"], 1)
                V.tensor_tensor(out=glu_s[:, m, :, W - 1:W - 1 + DS],
                                in0=a[:, 512 + SEQ - HT:512 + HT].rearrange("p (b t) -> p b t", b=DB),
                                in1=g[:, SEQ:NT].rearrange("p (b t) -> p b t", b=DB), op=ALU.mult).then_inc(S["glu_ready"], 1)
                dve.wait_ge(S["glu_ready"], 3 * (m + 1))
                for w in range(W):
                    tap = vecT[:, m, w:w + 1]
                    for part, (src, dst) in enumerate(((glu_p[:, m, w:w + SEQ], conv[:, m, 0:SEQ]),
                                                       (glu_s[:, m, :, w:w + DS], conv[:, m, SEQ:NT].rearrange("p (b t) -> p b t", b=DB)))):
                        if w == 0:
                            ins = V.tensor_scalar(dst, src, tap, vecT[:, m, W + 1:W + 2], ALU.mult, ALU.add)
                        else:
                            dve.wait_ge(S["conv_step"], 2 * W * m + 2 * (w - 1) + part + 1)
                            ins = V.scalar_tensor_tensor(out=dst, in0=src, scalar=tap, in1=dst, op0=ALU.mult, op1=ALU.add)
                        ins.then_inc(S["conv_step"], 1)
            dve.wait_ge(S["bs_in"], 16)
            dve.wait_ge(S["zeroes"], ZEROED["bias"])
            for kv in range(KV):
                V.tensor_copy(bsc[32 * kv:32 * kv + 32, NCS * kv:NCS * (kv + 1)],
                              bs[32 * kv:32 * kv + 32, 31:31 + 16 * (NCS - 1) + 1:16]).then_inc(S["bsc_ready"], 1)

            dve.wait_ge(S["stat_mm"], 1)
            for m in range(KD):
                dve.wait_ge(S["conv_step"], 2 * W * (m + 1))
                V.tensor_tensor(out=conv[:, m].rearrange("p (a n) -> p a n", a=2), in0=conv[:, m].rearrange("p (a n) -> p a n", a=2),
                                in1=halves(0), op=ALU.subtract).then_inc(S["centred"], 1)
            dve.wait_ge(S["stat_mm"], 1 + KD)
            V.tensor_scalar(rstd_ln.rearrange("p (a n) -> p a n", a=2), halves(2), EPS, None, ALU.add).then_inc(S["eps_ready"], 1)
            dve.wait_ge(S["std_ready"], 1)
            link(dve, V.reciprocal(rstd_ln, rstd_ln))
            dve.wait_ge(S["sqd"], KD)
            for m in range(KD):
                dve.wait_ge(S["centred"], m + 1)
                V.tensor_tensor(out=conv[:, m], in0=conv[:, m], in1=rstd_ln, op=ALU.mult).then_inc(S["lnx_ready"], 1)
            dve.wait_ge(S["ct_tr"], 2 * DB)
            for b in range(DB):
                V.tensor_copy(new_rows[:, :, DS * b:DS * b + DS], glu_s[:, :, b, W - 1:W - 1 + DS]).then_inc(S["new_packed"], 1)

            dve.wait_ge(S["gpost_in"], 16)
            for t in range(TT + 1):
                if t < TT:
                    r = rows(t)
                    dve.wait_ge(S["sq_b"], t + 1)
                    mean_sq(0, r, "ms_b")
                    dve.wait_ge(S["sd_b"], t + 1)
                    link(dve, V.reciprocal(rs[0:r, 0:1], sd[0:r, 0:1]))
                    V.scalar_tensor_tensor(out=scaled_b[0:r], in0=pb(2 * (t % 2), D, p1=r), scalar=rs[0:r, 0:1],
                                           in1=gpost_a[0:r], op0=ALU.mult, op1=ALU.mult).then_inc(S["o_scaled"], 1)
                    dve.wait_ge(S["o_scaled"], t + 1)
                    V.tensor_tensor(out=x_sb[0:r, t], in0=x_sb[0:r, t], in1=scaled_b[0:r], op=ALU.add).then_inc(S["x1_ready"], 1)
                if t:
                    k, rk = t - 1, rows(t - 1)
                    if k == 0:
                        dve.wait_ge(S["y_ready"], KD)
                        dve.wait_ge(S["co_out"], 16 * (1 + DB))
                    dve.wait_ge(S["tr_b"], k + 1)
                    for q, T in enumerate((hT, uT)):
                        V.tensor_tensor(out=T[:, :, k * P:k * P + rk], in0=pb(4 + 2 * (k % 2), KD, P)[:, :, 0:rk],
                                        in1=gain(4 + q, rk), op=ALU.mult).then_inc(S["hu_ready"], 1)
                if t < TT:
                    dve.wait_ge(S["sq_c"], t + 1)
                    mean_sq(1, r, "ms_c")
                    dve.wait_ge(S["sd_c"], t + 1)
                    link(dve, V.reciprocal(rs[0:r, 1:2], sd[0:r, 1:2]))
                    if t >= 2:
                        dve.wait_ge(S["tr_b"], t - 1)
                    dve.wait_ge(S["x1_ready"], t + 1)
                    V.tensor_scalar(xn_b[0:r, t % 2], x_sb[0:r, t], rs[0:r, 1:2], None, ALU.mult).then_inc(S["xn_b_ready"], 1)

            def split_lo(j):
                dve.wait_ge(S["hi_ready"], j + 1)
                if j == KD:
                    V.tensor_tensor(out=wgate_lo, in0=wgate, in1=wgate_hi, op=ALU.subtract).then_inc(S["lo_ready"], 1)
                    return
                j -= j > KD
                V.tensor_tensor(out=tile_lo[:, j % TRING], in0=tile_w[:, j % TRING], in1=tile_hi[:, j % HRING],
                                op=ALU.subtract).then_inc(S["lo_ready"], 1)

            dve.wait_ge(S["hu_ready"], 2 * TT)
            for m in range(KD):
                dve.wait_ge(S["uh_ready"], m + 1)
                V.tensor_tensor(out=u_lo[:, m], in0=uT[:, m], in1=u_hi[:, m], op=ALU.subtract).then_inc(S["ul_ready"], 1)
            dve.wait_ge(S["zeroes"], ZEROED["keys"])
            for n in range(2 * TT):
                br, t = n // TT, n % TT
                dve.wait_ge(S["kt_tr"], n + 1)
                if t < 4:
                    for lo in range(2):
                        V.tensor_copy(ktz[HD * lo:HD * lo + HD, br, lo:KV:2, t * P:(t + 1) * P],
                                      pb(6 + n % 2, 2, P, p0=HD * lo, p1=HD * lo + HD)).then_inc(S["kt_ready"], 1)
                else:
                    V.tensor_copy(kt_new[:, br], pb(6 + n % 2, 2, P)[:, :, 0:NS]).then_inc(S["kt_ready"], 1)
            for j in range(HRING):
                split_lo(j)
            dve.wait_ge(S["cs_mm"], 4)
            for n in range(4):
                c, gi = n // 2, n % 2
                dve.wait_ge(S["ctp_tr"], n + 1)
                V.tensor_copy(ctP[:, c, :, :, 16 * gi:16 * gi + 16].rearrange("p j k c -> p k c j"),
                              pb(6 + n % 2, KV, 16, 8)).then_inc(S["ctp_ready"], 1)
            for j in range(HRING, KD + HRING):
                split_lo(j)
            dve.wait_ge(S["zeroes"], ZEROED["queries"])
            dve.wait_ge(S["q_ready"], KD)
            for p in range(2):
                for half in range(2):
                    lo = HD * half
                    V.tensor_copy(qbd[lo:lo + HD, :, p, 32 * half:32 * half + 32].rearrange("p b (g t) -> p b g t", g=G),
                                  qT[lo:lo + HD, 4 * p:4 * p + 4, SEQ:NT].rearrange("p g (b t) -> p b g t", b=DB)).then_inc(S["qbd_ready"], 1)
            split_lo(KD + HRING)
            dve.wait_ge(S["gate_tr"], 1)
            V.tensor_copy(gR, pb(2, 4, 48)).then_inc(S["gR_ready"], 1)
            dve.wait_ge(S["gR_ready"], 1)
            for i in range(4):
                V.tensor_copy(gRr[:, i], gR[:, 3 - i, 0:H]).then_inc(S["gR_ready"], 1)
            dve.wait_ge(S["gR_ready"], 5)

            for n in range(NBR):
                split_lo(KD + 1 + n + HRING)

            dve.wait_ge(S["zeroes"], ZEROED["table"])
            dve.wait_ge(S["x1_out"], 16 * TT)
            dve.wait_ge(S["kv_out"], KV_OUT)
            dve.wait_ge(S["gate_out"], 16)
            for w in range(len(items) + 3):
                if w < len(items):
                    m, br, i, us = items[w]
                    u = us[0]
                    if br == 0:
                        dve.wait_ge(tb_in[m % 2], 32 * (m // 2 + 1))
                        if m:
                            dve.wait_ge(S["l_ready"], UPM * (m - 1) + 1)
                        V.tensor_copy(e2[:, :, 0:31], tb[:, m % 2, :, 31:SEQ:16]).then_inc(S["e2_ready"], 1)
                        dve.wait_ge(S["e2_ready"], m + 1)
                        dve.wait_ge(S["s_done"], u + 1)
                        if u >= 6:
                            dve.wait_ge(S["t_done"], u - 5)
                        L3 = l_sb[:, u % 6, 0:8 * NCP].rearrange("q (i h n) -> q i h n", i=4, h=2)
                        sc = pb(u % 3, 4, 64).rearrange("q i (h n) -> q i h n", h=2)
                        for ir in range(4):
                            ins = V.tensor_tensor(out=L3[:, ir], in0=sc[:, ir, :, 0:NCP], in1=e2[:, :, 8 * ir:8 * ir + NCP], op=ALU.add)
                        ins.then_inc(S["l_ready"], 1)
                        dve.wait_ge(S["l_ready"], u + 1)
                        L2 = l_sb[:, u % 6, 0:8 * NCP].rearrange("q (r n) -> q r n", n=NCP)
                        link(dve, V.tensor_reduce(mn[:, 0:8], L2, AX.X, ALU.min))
                        link(dve, V.tensor_scalar(mn[:, 0:8], mn[:, 0:8], 0.1 * BIG, None, ALU.min))
                        V.tensor_tensor(out=L2, in0=L2, in1=mn[:, 0:8].unsqueeze(2).broadcast_to([P, 8, NCP]),
                                        op=ALU.subtract).then_inc(S["cmin_ready"], 1)
                    else:
                        for half, u in enumerate(us):
                            dve.wait_ge(S["s_done"], u + 1)
                            if u >= 6:
                                dve.wait_ge(S["t_done"], u - 5)
                            k = stat(w) + half
                            if w >= 3:
                                dve.wait_ge(S["exp_done"], items[w - 3][3][-1] + 1)
                            V.tensor_tensor_reduce(l_sb[:, u % 6, 0:P * (i + 1)], pb(u % 3, P * (i + 1)),
                                                   tb[:, m % 2, half, 384 - P * i:SEQ], 1.0, 3 * BIG, ALU.add, ALU.min,
                                                   mn[:, k:k + 1]).then_inc(S["l_ready"], 1)
                if 1 <= w <= len(items):
                    m, br, i, us = items[w - 1]
                    dve.wait_ge(S["exp_done"], us[-1] + 1)
                    if br == 0:
                        if m:
                            dve.wait_ge(S["pn_ready"], UPM * (m - 1) + 1)
                        L2 = l_sb[:, us[0] % 6, 0:8 * NCP].rearrange("q (r n) -> q r n", n=NCP)
                        link(dve, V.tensor_reduce(den[:, 0:8], L2, AX.X, ALU.add))
                        link(dve, V.tensor_scalar(den[:, 0:8], den[:, 0:8], 1e-30, None, ALU.max))
                        link(dve, V.reciprocal(rden[:, 0:8], den[:, 0:8]))
                        h0 = 8 * (m // 4) + m % 4
                        V.tensor_tensor(out=rden[:, 0:8].rearrange("q (i h) -> q i h", h=2),
                                        in0=rden[:, 0:8].rearrange("q (i h) -> q i h", h=2),
                                        in1=gRr[:, :, h0:h0 + 5:4], op=ALU.mult).then_inc(S["den_ready"], 1)
                    else:
                        k = stat(w - 1)
                        if w >= 4:
                            dve.wait_ge(S["pn_ready"], items[w - 4][3][-1] + 1)
                        link(dve, V.tensor_scalar(den[:, k:k + 2], den[:, k:k + 2], 1e-30, None, ALU.max))
                        V.reciprocal(rden[:, k:k + 2], den[:, k:k + 2]).then_inc(S["den_ready"], 1)
                if 2 <= w < len(items) + 2:
                    m, br, i, us = items[w - 2]
                    u = us[-1]
                    n = SEQ if br == 0 else P * (i + 1)
                    dve.wait_ge(S["t_done"], u + 1)
                    if u >= 4:
                        dve.wait_ge(S["pv_done"], item_of[u - 4] + 1)
                    V.tensor_copy(pt_sb[:, u % 4, 0:n], pb(3 + u % 2, n)).then_inc(S["pt_d"], 1)
                if w >= 3 and (items[w - 3][1] == 0 or items[w - 3][2] == 3):
                    m, br = items[w - 3][:2]
                    dve.wait_ge(S["silu_ready"], 2 * m + 1)
                    dve.wait_ge(S["pv_done"], w - 2)
                    if br:
                        prev = 2 * m + br - 1
                        if prev:
                            dve.wait_ge(S["y_add"], prev)
                    V.tensor_tensor(out=y_tmp if br else yT[:, m, 0:SEQ], in0=pb(5, SEQ), in1=sz[:, br, m % 2], op=ALU.mult).then_inc(S["y_mul"], 1)

                if w - 1 in z_at and z_at[w - 1] + HRING < NBR * KD:
                    split_lo(KD + 1 + z_at[w - 1] + HRING)

            dve.wait_ge(S["ss_mm"], 1)
            dve.wait_ge(S["bsc_ready"], KV)
            dve.wait_ge(S["t_done"], N_UNITS)
            dve.wait_ge(S["gS_in"], 16 * NBR)
            L3 = l_sb[:, 0, 0:480].rearrange("q (b n) -> q b n", b=DB)
            V.tensor_tensor(out=L3, in0=pb(1, DB, 60), in1=bsc.unsqueeze(1).broadcast_to([P, DB, 60]), op=ALU.add).then_inc(S["sl_ready"], 1)
            dve.wait_ge(S["sl_ready"], 1)
            link(dve, V.tensor_reduce(mn[:, 0:8], L3, AX.X, ALU.min))
            link(dve, V.tensor_scalar(mn[:, 0:8], mn[:, 0:8], 0.1 * BIG, None, ALU.min))
            V.tensor_tensor(out=L3, in0=L3, in1=mn[:, 0:8].unsqueeze(2).broadcast_to([P, DB, 60]), op=ALU.subtract).then_inc(S["cmin_ready"], 1)
            dve.wait_ge(S["exp_done"], N_UNITS + 1)
            link(dve, V.tensor_reduce(den[:, 0:8], L3, AX.X, ALU.add))
            link(dve, V.tensor_scalar(den[:, 0:8], den[:, 0:8], 1e-30, None, ALU.max))
            link(dve, V.reciprocal(rden[:, 0:8], den[:, 0:8]))
            link(dve, V.tensor_tensor(out=rden[:, 0:8], in0=rden[:, 0:8], in1=gS[:, 0], op=ALU.mult))
            V.tensor_tensor(out=L3, in0=L3, in1=rden[:, 0:8].unsqueeze(2).broadcast_to([P, DB, 60]), op=ALU.mult).then_inc(S["sp_ready"], 1)
            dve.wait_ge(S["st_tr"], 1)
            dve.wait_ge(S["qbd_ready"], 4)
            V.tensor_copy(ptc.rearrange("p b n -> p (b n)"), pb(2, 1024, p1=60)).then_inc(S["pts_ready"], 1)
            dve.wait_ge(S["so_mm"], 1)
            V.tensor_copy(orc.rearrange("p b n -> p (b n)"), pb(0, 1024)).then_inc(S["or_ready"], 1)
            dve.wait_ge(S["silu_ready"], 2 * KD)

            def gate_sample(dst, src, br, b):
                for half in range(2):
                    lo = HD * half
                    o_ = src[lo:lo + HD].rearrange("q (p h g t) -> q p h g t", p=2, h=2, g=G)[:, :, half]
                    z_ = szs[lo:lo + HD, br, :, DS * b:DS * b + DS].rearrange("q (p g) t -> q p g t", p=2)
                    d_ = dst[lo:lo + HD].rearrange("q (p g) t -> q p g t", p=2)
                    V.tensor_tensor(out=d_, in0=o_, in1=z_, op=ALU.mult).then_inc(S["ys_mul"], 1)

            dve.wait_ge(S["ot_tr"], 1)
            for b in range(DB):
                gate_sample(yT[:, :, SEQ + DS * b:SEQ + DS * b + DS], pb(2, 1024)[:, b * P:(b + 1) * P], 0, b)
            def last_mean(t):
                dve.wait_ge(S["sq_a"], TT + t + 1)
                mean_sq(t, rows(t), "ms_a")

            def last_rows(t):
                r = rows(t)
                dve.wait_ge(S["sd_a"], TT + t + 1)
                link(dve, V.reciprocal(rs[0:r, t:t + 1], sd[0:r, t:t + 1]))
                if t >= 2:
                    dve.wait_ge(fy_out[t % 2], 16 * (t // 2))
                dve.wait_ge(S["gpost_in"], 32)
                dve.wait_ge(x_in[t % 2], 16 * (t // 2 + 2))
                link(dve, V.scalar_tensor_tensor(out=y_out[0:r, t % 2], in0=pb(4 + 2 * (t % 2), D, p1=r), scalar=rs[0:r, t:t + 1],
                                                 in1=gpost_b[0:r], op0=ALU.mult, op1=ALU.mult))
                V.tensor_tensor(out=y_out[0:r, t % 2], in0=y_out[0:r, t % 2], in1=x1_back[0:r, t % 2], op=ALU.add).then_inc(S["fy"], 1)

            for w in range(2 * DB + 4):
                n = w - 4
                if 0 <= n < 2 * DB:
                    b, br = n // 2, n % 2
                    dve.wait_ge(S["ot_tr"], n + 2)
                    gate_sample(y_br[:, br, :, DS * b:DS * b + DS], pb(3, P), 1 + br, b)
                n = w - 2
                if 0 <= n < 2 * DB:
                    b, br = n // 2, n % 2
                    dve.wait_ge(S["se_ready"], n + 1)
                    k = 8 + n % 4
                    link(dve, V.tensor_scalar(den[:, k:k + 1], den[:, k:k + 1], 1e-30, None, ALU.max))
                    link(dve, V.reciprocal(rden[:, k:k + 1], den[:, k:k + 1]))
                    L = l_sb[:, 1 + n % 3, 0:KS]
                    V.tensor_scalar(L, L, rden[:, k:k + 1], gS[:, 1 + br, b:b + 1], ALU.mult, ALU.mult).then_inc(S["sp_ready"], 1)
                n = w - 1
                if 0 <= n < 2 * DB:
                    dve.wait_ge(S["ss_mm"], n + 2)
                    if n >= 3:
                        dve.wait_ge(S["st_tr"], n - 1)
                    if n >= 4:
                        dve.wait_ge(S["se_ready"], n - 3)
                    k = 8 + n % 4
                    V.tensor_tensor_reduce(l_sb[:, 1 + n % 3, 0:KS], pb(1, KS), bs, 1.0, 3 * BIG, ALU.add, ALU.min,
                                           mn[:, k:k + 1]).then_inc(S["sl_ready"], 1)
                n = w - 2
                if 0 <= n < 2 * DB:
                    dve.wait_ge(S["st_tr"], n + 2)
                    if n >= 2:
                        dve.wait_ge(S["so_mm"], n)
                    else:
                        dve.wait_ge(S["pv_done"], len(items))
                    V.tensor_copy(pts[:, n % 2, 0:2], pb(2, 2, P)).then_inc(S["pts_ready"], 1)
                    V.tensor_copy(pts[0:DS, n % 2, 2], pb(2, 3, P, p1=DS)[:, 2]).then_inc(S["pts_ready"], 1)
                n = w - 3
                if 0 <= n < 2 * DB:
                    dve.wait_ge(S["so_mm"], n + 2)
                    if n >= 2:
                        dve.wait_ge(S["ot_tr"], n)
                    for p in range(2):
                        V.tensor_copy(orow[64 * p:64 * p + 64, n % 2], pb(3, 2, P, p0=64 * p, p1=64 * p + 64)[:, p]).then_inc(S["or_ready"], 1)
                if w % 4 == 0 and w < 16:
                    last_mean(w // 4)
                if w % 4 == 1 and w < 16:
                    last_rows(w // 4)
            dve.wait_ge(S["ys_mul"], 2 * DB * 3)
            ys = yT[:, :, SEQ:NT]
            for br in range(2):
                V.tensor_tensor(out=ys, in0=ys, in1=y_br[:, br], op=ALU.add).then_inc(S["y_s"], 1)
                dve.wait_ge(S["y_s"], br + 1)

            last_mean(4)
            last_rows(4)

        @block.tensor
        def _(pe):
            def product(out, pairs):
                pairs = list(pairs)
                for k, (l, r) in enumerate(pairs):
                    ins = pe.matmul(out, l, r, start=(k == 0), stop=(k == len(pairs) - 1))
                return ins

            def tproduct(b0, lhs, src):
                for k in range(KD):
                    for hf in range(2):
                        ins = pe.matmul(pb(b0 + hf, HT)[0:lhs(k).shape[1]], lhs(k), src[:, k, hf * HT:(hf + 1) * HT],
                                        start=(k == 0), stop=(k == KD - 1))
                return ins

            def await_chunk(c):
                pe.wait_ge(place[c][2], arrived[c])

            def split_product(b0, j, w_hi, w_lo):
                pe.wait_ge(S["lo_ready"], j + 1)
                for k in range(KD):
                    for hf in range(2):
                        out = pb(b0 + hf, HT)[0:w_hi.shape[2]]
                        h, l = (x[:, k, hf * HT:(hf + 1) * HT] for x in (u_hi, u_lo))
                        pe.matmul(out, w_hi[:, k], h, start=(k == 0), stop=False)
                        pe.matmul(out, w_hi[:, k], l, start=False, stop=False)
                        ins = pe.matmul(out, w_lo[:, k], h, start=False, stop=(k == KD - 1))
                return ins

            def tile_product(b0, j):
                c = j - (j > KD)
                return split_product(b0, j, tile_hi[:, c % HRING], tile_lo[:, c % TRING])

            pe.wait_ge(S["ident_ready"], 1)
            for t in range(TT):
                r = rows(t)
                pe.wait_ge(S["xn_a_ready"], t + 1)
                if t >= 2:
                    pe.wait_ge(S["h_ready"], t - 1)
                for k in range(KD):
                    ins = pe.transpose(pb(4 + 2 * (t % 2), KD, P)[:, k, 0:r], xn_a[0:r, t % 2, k * P:(k + 1) * P], ident[0:r, 0:r])
                ins.then_inc(S["tr_a"], 1)
                if t == 0:
                    pe.wait_ge(S["vec_in"], 16 * 7)
                    for k in range(KD):
                        ins = pe.transpose(pb(2, KD, 37)[:, k], vec_rows[0:37, k * P:(k + 1) * P], ident[0:37, 0:37])
                    ins.then_inc(S["vec_ps"], 1)
                if t == 1:
                    pe.wait_ge(S["bias_in"], 32)
                    pe.matmul(pb(0, SEQ, p1=H), rel_rows, hot_rows, start=True, stop=True).then_inc(S["early_mm"], 1)
                    pe.wait_ge(S["pe_in"], 32)
                    for c in range(2):
                        ins = pe.transpose(pb(1, 2, 16)[:, c], pe_rows[:, c], ident[0:16, 0:16])
                    ins.then_inc(S["early_mm"], 1)
            pe.wait_ge(S["state_in"], 32)
            pe.wait_ge(S["h_ready"], 4)
            for n in range(4):
                i, mg = n // 2, n % 2
                if n >= 2:
                    pe.wait_ge(S["state_ready"], 4 * (n - 1))
                for k in range(4):
                    ins = pe.transpose(pb(6 + n % 2, 4, 120)[:, k], state_rows[0:120, i, (4 * mg + k) * P:(4 * mg + k + 1) * P],
                                       ident[0:120, 0:120])
                ins.then_inc(S["state_tr"], 1)

            def ct_transposes(n):
                pe.wait_ge(rows_in[n % 4], 64 * (n // 4 + 1))
                if n == DB:
                    pe.wait_ge(S["hid_ready"], 2)
                    pe.wait_ge(S["kc_ready"], 1)
                if n >= 2:
                    pe.wait_ge(S["ct_ready"], n - 1)
                else:
                    pe.wait_ge(S["state_ready"], 16)
                for kv in range(KV):
                    ins = pe.transpose(pb(6 + n % 2, KV, P)[:, kv], rows_slot(n)[:, kv], ident)
                ins.then_inc(S["ct_tr"], 1)

            def compress(c, ht, part):
                if ht == 0 and part == 0:
                    pe.wait_ge(S["w1_in"], 16 * (c + 1))
                    pe.wait_ge(S["ct_ready"], DB * (c + 1))
                    pe.wait_ge(S["pe_ready"], c + 1)
                for j in range(8 * part, 8 * part + 8):
                    ins = pe.matmul(pb(6 + ht, 33, NCS), w1_sb[:, j, ht * P:(ht + 1) * P],
                                    ctS[:, j % 8, :, j // 8:j // 8 + NCS], start=(j == 0), stop=(j == 15))
                if part:
                    ins.then_inc(S["cs_mm"], 1)

            pe.wait_ge(S["h_ready"], TT)
            pe.wait_ge(S["line_part"], 2)
            pe.wait_ge(S["pe_sb_ready"], 1)
            pe.wait_ge(S["vec_ready"], 1)
            for m in range(KD):
                for j in range(3):
                    c = 3 * (m // 2) + j
                    await_chunk(c)
                    if m:
                        pe.wait_ge(*((S["glu_ready"], 3 * m), (S["sg_ready"], m), (S["z_ready"], m))[j])
                    lo = (m % 2) * P
                    ins = tproduct(2 * j, lambda k: chunk_sb(c)[:, k, lo:lo + P], hT)
                    ins.then_inc(S["proj_a"], 1)
                    if j == 1 and m < 3:
                        for n in range(3 * m, min(3 * m + 3, DB)):
                            ct_transposes(n)
                    if j == 1 and 3 <= m < 7:
                        compress(0, (m - 3) // 2, (m - 3) % 2)
                    if j == 1 and m == 7:
                        pe.wait_ge(S["w2_in"], 16 * 8)
                        pe.wait_ge(S["hid_ready"], 2)
                        product(pb(6, 480), ((w2_sb[:, 0, ht], hid[:, ht]) for ht in range(2))).then_inc(S["kc_mm"], 1)
            for b in range(3):
                ct_transposes(DB + b)
            pe.wait_ge(S["ones_ready"], 1)
            pe.wait_ge(S["glu_ready"], 3 * KD)
            for m in range(KD):
                if m == KD - 1:
                    for b in range(3, 6):
                        ct_transposes(DB + b)
                pe.wait_ge(S["conv_step"], 2 * W * (m + 1))
                for hf in range(2):
                    ins = pe.matmul(pb(hf, HT), ones, conv[:, m, hf * HT:(hf + 1) * HT], start=(m == 0), stop=(m == KD - 1))
            ins.then_inc(S["stat_mm"], 1)

            for m in range(KD):
                pe.wait_ge(S["sqd"], m + 1)
                for hf in range(2):
                    ins = pe.matmul(pb(2 + hf, HT), ones, sg[:, m % 2, hf * HT:(hf + 1) * HT], start=(m == 0), stop=(m == KD - 1))
                ins.then_inc(S["stat_mm"], 1)
            for b in range(6, DB):
                ct_transposes(DB + b)
            for ht in range(2):
                for part in range(2):
                    compress(1, ht, part)
            pe.wait_ge(S["hid_ready"], 4)
            pe.wait_ge(S["z_ready"], KD)
            for b in range(DB):
                ins = product(pb(4, DB, P, p1=60)[:, b], ((hid[:, ht, 60 * b:60 * b + 60], w2_sb[:, 1, ht]) for ht in range(2)))
            ins.then_inc(S["vc_mm"], 1)
            pe.wait_ge(S["centred"], KD)
            for k in range(KD):
                ins = pe.transpose(pb(0, KD, P, p1=W - 1)[:, k], glu_p[:, k, SEQ:SEQ + W - 1], ident)
            ins.then_inc(S["co_tr"], 1)
            pe.wait_ge(S["eps_ready"], 1)
            pe.wait_ge(S["new_packed"], DB)
            for k in range(KD):
                ins = pe.transpose(pb(2, KD, P, p1=NS)[:, k], new_rows[:, k], ident)
            ins.then_inc(S["co_tr"], 1)

            pe.wait_ge(S["y_ready"], KD)
            pe.wait_ge(S["co_ready"], 2)
            pe.wait_ge(S["vc_ready"], 1)
            pe.wait_ge(S["hid_ready"], 4)

            def turn_b(t):
                r = rows(t)
                pe.wait_ge(S["xn_b_ready"], t + 1)
                if t >= 2:
                    pe.wait_ge(S["hu_ready"], 2 * (t - 1))
                for k in range(KD):
                    ins = pe.transpose(pb(4 + 2 * (t % 2), KD, P)[:, k, 0:r], xn_b[0:r, t % 2, k * P:(k + 1) * P], ident[0:r, 0:r])
                ins.then_inc(S["tr_b"], 1)

            def row_product(t, src, c0, done):
                r = rows(t)
                for c in range(4):
                    await_chunk(c0 + c)
                    ins = product(pb(2 * (t % 2), 4, CH, p1=r)[:, c], ((src[:, k, t * P:t * P + r], chunk_sb(c0 + c)[:, k]) for k in range(KD)))
                ins.then_inc(S[done], 1)
                return ins

            for t in range(TT):
                if t >= 2:
                    pe.wait_ge(S["o_scaled"], t - 1)
                ins = row_product(t, zA, C_OA, "o_mm")
                if t >= 1:
                    turn_b(t - 1)

            def kt_transposes(br):
                for t in range(TT):
                    n = TT * br + t
                    r = rows(t)
                    pe.wait_ge(S["kv_ready"], TT * (2 * br + 2) + t + 1)
                    if n >= 2:
                        pe.wait_ge(S["kt_ready"], sum(2 if q % TT < 4 else 1 for q in range(n - 1)))
                    for p in range(2):
                        ins = pe.transpose(pb(6 + n % 2, 2, P)[:, p, 0:r], k_stage[0:r, br, t, p * P:(p + 1) * P], ident[0:r, 0:r])
                    ins.then_inc(S["kt_tr"], 1)

            for c in range(6):
                await_chunk(C_KV + c)
                for t in range(TT):
                    n = TT * c + t
                    r = rows(t)
                    if n == 2:
                        turn_b(TT - 1)
                    if n < 2:
                        pe.wait_ge(S["hu_ready"], 2 * (n + 1))
                        pe.wait_ge(S["o_scaled"], 4)
                    elif n < 6:
                        pe.wait_ge(S["hu_ready"], 2 * TT if n >= 4 else 2 * (n + 1))
                        pe.wait_ge(S["o_scaled"], TT)
                    else:
                        pe.wait_ge(S["kv_ready"], n - 5)
                    if c < 2 and t < 4:
                        lhs = hT[:, :, (t // 2) * 256 + t % 2:(t // 2) * 256 + 256:2]
                    else:
                        lhs = hT[:, :, t * P:t * P + r]
                    ins = product(pb(kv_bank(n), CH, p1=r), ((lhs[:, k], chunk_sb(C_KV + c)[:, k]) for k in range(KD)))
                    ins.then_inc(S["kv_mm"], 1)
                if c == 4:
                    kt_transposes(0)
            kt_transposes(1)
            for n in range(4):
                c, gi = n // 2, n % 2
                if n >= 2:
                    pe.wait_ge(S["ctp_ready"], n - 1)
                else:
                    pe.wait_ge(S["kt_ready"], 18)
                for kv in range(KV):
                    ins = pe.transpose(pb(6 + n % 2, KV, P)[:, kv], cmp_rows[:, gi, c, kv], ident)
                ins.then_inc(S["ctp_tr"], 1)
            pe.wait_ge(S["kv_ready"], 30)
            pe.wait_ge(S["ctp_ready"], 4)

            def compress_p(n, c):
                pe.wait_ge(S["w1_in"], 16 * (2 + n))
                if n:
                    pe.wait_ge(S["hidp_ready"], 2)
                for ht in range(2):
                    product(pb(4 + ht, KV, NCP), ((w1_sb[:, j, ht * P:(ht + 1) * P], ctP[:, c, j % 8, :, j // 8:j // 8 + NCP])
                                                  for j in range(16))).then_inc(S["cp_mm"], 1)

            compress_p(0, 1)
            pe.wait_ge(S["hidp_ready"], 2)
            for p in range(2):
                for half in range(2):
                    kv = 2 * p + half
                    ins = product(pb(2 + p, HD, p0=32 * half, p1=32 * half + NCP),
                                  ((hid_p[:, ht, NCP * kv:NCP * (kv + 1)], w2_sb[:, 1, ht, 0:HD]) for ht in range(2)))
            ins.then_inc(S["cpp_mm"], 1)
            pe.wait_ge(S["ul_ready"], KD)
            for m in range(KD):
                if m >= 3:
                    pe.wait_ge(S["q_ready"], m - 2)
                if m == 1:
                    pe.wait_ge(S["bd_ready"], 4)
                if m == 2:
                    pe.wait_ge(S["hidp_ready"], 2)
                tile_product(2 * (m % 3), m).then_inc(S["q_mm"], 1)
            split_product(6, KD, wgate_hi, wgate_lo).then_inc(S["gate_mm"], 1)
            pe.wait_ge(S["q_ready"], 7)
            compress_p(1, 0)
            pe.wait_ge(S["hidp_ready"], 4)
            product(pb(0, 124), ((w2_sb[:, 0, ht], hid_p[:, ht]) for ht in range(2))).then_inc(S["cpp_mm"], 1)
            pe.wait_ge(S["gate_ready"], 1)
            pe.wait_ge(S["q_ready"], KD)
            for i in range(4):
                ins = pe.transpose(pb(2, 4, 48)[:, i], gateT[0:48, i * P:(i + 1) * P], ident[0:48, 0:48])
            ins.then_inc(S["gate_tr"], 1)
            pe.wait_ge(S["gR_ready"], 1)
            pe.wait_ge(S["bd_ready"], 8)

            def z_product(n, b0):
                tile_product(b0, KD + 1 + n).then_inc(S["z_mm"], 1)

            for n in range(NBR):
                if n >= 2:
                    pe.wait_ge(S["zb_ready"], 3 * (n - 1))
                z_product(n, 2 * (n % 2))

            pe.wait_ge(S["zb_ready"], 3 * NBR)
            pe.wait_ge(S["kt_ready"], 18)
            pe.wait_ge(S["zeroes"], ZEROED["keys"])
            for w in range(len(items) + 3):
                if w < len(items):
                    m, br, i, us = items[w]
                    for half, u in enumerate(us):
                        if u >= 3:
                            pe.wait_ge(S["l_ready"], u - 2)
                        if br == 0:
                            for ir in range(4):
                                ins = pe.matmul(pb(u % 3, 4, 64)[:, ir], qT[:, m, (3 - ir) * P:(4 - ir) * P], kcbd[:, m // 4],
                                                start=True, stop=True)
                        else:
                            n = P * (i + 1)
                            ins = pe.matmul(pb(u % 3, n), qT[:, m, i * P:(i + 1) * P], ktz[:, br - 1, 2 * (m // 4) + half, 0:n],
                                            start=True, stop=True)
                        ins.then_inc(S["s_done"], 1)
                if w in z_at:
                    n = z_at[w]
                    pe.wait_ge(S["zb_ready"], 3 * n)
                    z_product(n, 6)
                if 2 <= w < len(items) + 2:
                    m, br, i, us = items[w - 2]
                    for u in us:
                        pe.wait_ge(S["pn_ready"], u + 1)
                        if u >= 2:
                            name, count = pt_by[u - 2]
                            pe.wait_ge(S[name], count)
                        if br == 0:
                            for ir in range(4):
                                ins = pe.transpose(pb(3 + u % 2, 4, P)[:, 3 - ir], pc_sb[:, ir], ident)
                        else:
                            for j in range(i + 1):
                                ins = pe.transpose(pb(3 + u % 2, 4, P)[:, j], l_sb[:, u % 6, j * P:(j + 1) * P], ident)
                        ins.then_inc(S["t_done"], 1)
                if w >= 3:
                    m, br, i, us = items[w - 3]
                    for u in us:
                        name, count = pt_by[u]
                        pe.wait_ge(S[name], count)
                    if 3 * m + br and (br == 0 or i == 0):
                        pe.wait_ge(S["y_mul"], 3 * m + br)
                    if br == 0:
                        ins = pe.matmul(pb(5, SEQ), vcbd[:, m // 4], pt_sb[:, us[0] % 4], start=True, stop=True)
                    else:
                        for j in range(i + 1):
                            for half, u in enumerate(us):
                                kv = 2 * (m // 4) + half
                                ins = pe.matmul(pb(5, SEQ, p0=HD * half, p1=HD * half + HD)[:, i * P:(i + 1) * P],
                                                v_sb[:, br - 1, j, kv * HD:(kv + 1) * HD], pt_sb[:, u % 4, j * P:(j + 1) * P],
                                                start=(j == 0), stop=(j == i))
                    ins.then_inc(S["pv_done"], 1)

            def last_part(job):
                t, c = job // 4, job % 4
                if job == 0:
                    pe.wait_ge(S["y_add"], 2 * KD)
                    pe.wait_ge(S["pv_done"], len(items))
                    pe.wait_ge(S["zb_ready"], 72)
                if c == 0 and t >= 2:
                    pe.wait_ge(S["fy"], t - 1)
                r = rows(t)
                await_chunk(C_OB + c)
                ins = product(pb(4 + 2 * (t % 2), 4, CH, p1=r)[:, c],
                              ((yT[:, k, t * P:t * P + r], chunk_sb(C_OB + c)[:, k]) for k in range(KD)))
                if c == 3:
                    ins.then_inc(S["fo_mm"], 1)

            pe.wait_ge(S["l_ready"], N_UNITS)
            pe.wait_ge(S["qbd_ready"], 4)
            pe.wait_ge(S["kc_ready"], 1)
            for b in range(DB):
                for p in range(2):
                    ins = pe.matmul(pb(1, DB, 60, p0=64 * p, p1=64 * p + 64)[:, b], qbd[:, b, p], kc_s[:, b], start=True, stop=True)
            ins.then_inc(S["ss_mm"], 1)
            last_part(0)
            last_part(1)
            pe.wait_ge(S["sp_ready"], 1)
            for b in range(DB):
                ins = pe.transpose(pb(2, DB, P, p1=60)[:, b], l_sb[:, 0, 60 * b:60 * b + 60], ident)
            ins.then_inc(S["st_tr"], 1)
            last_part(2)
            pe.wait_ge(S["pts_ready"], 1)
            for b in range(DB):
                ins = pe.matmul(pb(0, DB, P)[:, b], ptc[:, b], vc_s[0:60, b], start=True, stop=True)
            ins.then_inc(S["so_mm"], 1)
            last_part(3)
            pe.wait_ge(S["or_ready"], 1)
            for b in range(DB):
                ins = pe.transpose(pb(2, DB, P)[:, b], orc[:, b], ident)
            ins.then_inc(S["ot_tr"], 1)
            for w in range(2 * DB + 4):
                n = w
                if n < 2 * DB:
                    pe.wait_ge(slot_in[n % 6], totals[slot_in[n % 6]] + 48 * (n // 6 + 1))
                    if n:
                        pe.wait_ge(S["skt_ready"], n)
                    for p in range(2):
                        for pg in range(2):
                            ins = pe.transpose(pb(0, 2, 2, P)[:, p, pg], cache_sb[n % 6][:, pg, p * P:(p + 1) * P], ident)
                    ins.then_inc(S["skt_tr"], 1)
                n = w - 4
                if 0 <= n < 2 * DB:
                    pe.wait_ge(S["or_ready"], 1 + 2 * (n + 1))
                    pe.transpose(pb(3, P), orow[:, n % 2], ident).then_inc(S["ot_tr"], 1)
                if w < 12:
                    last_part(4 + w)
                n = w - 1
                if 0 <= n < 2 * DB:
                    pe.wait_ge(S["skt_ready"], n + 1)
                    pe.wait_ge(S["kts_new"], n + 1)
                    pe.wait_ge(S["sl_ready"], n + 1)
                    for p in range(2):
                        ins = pe.matmul(pb(1, KS, p0=64 * p, p1=64 * p + 64), qbd[:, n // 2, p], kts[:, n % 2, p],
                                        start=True, stop=True)
                    ins.then_inc(S["ss_mm"], 1)
                n = w - 2
                if 0 <= n < 2 * DB:
                    pe.wait_ge(S["sp_ready"], n + 2)
                    if n == 0:
                        pe.wait_ge(S["ys_mul"], 2 * DB)
                    else:
                        pe.wait_ge(S["pts_ready"], 1 + 2 * n)
                    for j in range(3):
                        k = min(P, KS - j * P)
                        ins = pe.transpose(pb(2, 3, P, p1=k)[:, j], l_sb[:, 1 + n % 3, j * P:j * P + k], ident)
                    ins.then_inc(S["st_tr"], 1)
                n = w - 3
                if 0 <= n < 2 * DB:
                    pe.wait_ge(S["pts_ready"], 1 + 2 * (n + 1))
                    pe.wait_ge(S["ys_mul"], 2 * DB + 2 * n)
                    parts = [(pts[:, n % 2, j], cache_sb[n % 6][:, j, CH:2 * CH]) for j in range(2)]
                    parts.append((pts[0:DS, n % 2, 2], vnew[:, n % 6]))
                    product(pb(3, CH), parts).then_inc(S["so_mm"], 1)
            pe.wait_ge(S["y_s"], 2)
            for c in range(4):
                last_part(16 + c)


INPUTS = ['x_prompt', 'x_sample', 'state_conv', 'cache_cmp', 'cache_slc', 'state_win', 'page_table', 'rel_bias',
          'a_norm_pre', 'a_w_in', 'a_conv_w', 'a_conv_b', 'a_ln_g', 'a_ln_b', 'a_w_out', 'a_norm_post',
          'kv_norm', 'w_kv', 'cmp_pe', 'cmp_w1', 'cmp_w2', 'b_norm_pre', 'b_w_in', 'b_w_out', 'b_norm_post']
OUTPUTS = [('y_prompt', (1, SEQ, D)), ('y_sample', (DB, DS, D)), ('conv_prompt', (1, 1, W - 1, D)),
           ('conv_sample', (1, DB, W - 1, D)), ('cmp_prompt', (1, SEQ, 2, KV, HD)), ('cmp_sample', (DB, DS, 2, KV, HD)),
           ('slc_prompt', (1, SEQ, 2, KV, HD)), ('slc_sample', (DB, DS, 2, KV, HD)),
           ('win_prompt', (1, SEQ, 2, KV, HD)), ('win_sample', (DB, KS, 2, KV, HD))]


def kernel(**inputs):
    import numpy as _np
    import concourse.bacc as _bacc
    from concourse import mybir as _mybir
    from concourse.bass_utils import run_bass_kernel_spmd as _run

    nc = _bacc.Bacc("TRN2", target_bir_lowering=False, num_devices=1)
    arrays, ins = {}, {}
    for name in INPUTS:
        a = _np.ascontiguousarray(inputs[name])
        arrays[f"in_{name}"] = a
        ins[name] = nc.dram_tensor(f"in_{name}", a.shape, _mybir.dt.from_np(a.dtype), kind="ExternalInput").ap()
    a = bucket_rows()
    arrays["bucket_rows"] = a
    ins["bucket_rows"] = nc.dram_tensor("bucket_rows", a.shape, _mybir.dt.float32, kind="ExternalInput").ap()
    outs = {name: nc.dram_tensor(f"out_{name}", shape, _mybir.dt.float32, kind="ExternalOutput").ap() for name, shape in OUTPUTS}
    build(nc, ins, outs)
    r = _run(nc, [arrays], core_ids=[0])
    return tuple(r.results[0][f"out_{name}"] for name, _ in OUTPUTS)
```

```python
import math
from contextlib import ExitStack

import numpy as np
import concourse.bass as bass
from concourse import mybir

F32 = mybir.dt.float32
F32R = mybir.dt.float32r
I32 = mybir.dt.int32
ALU = mybir.AluOpType
ACT = mybir.ActivationFunctionType
AX = mybir.AxisListType

P = 128
D = 1024
KD = D // P
SEQ = 512
DB, DS = 8, 8
NS = DB * DS
NT = SEQ + NS
HT = NT // 2
TT = 5
W = 31
W_OFF = 6
CONV = 2 * W - W_OFF + 1
H, HD, KV, G = 16, 64, 4, 4
NBR = 3
PAST, PAGE = 256, 128
STRIDE = 16
NCP = SEQ // STRIDE - 1
NCS = PAST // STRIDE - 1
KS = PAST + DS
BUCKETS, MAXD = 32, 128
EPS = 1e-6
BIG = 1e30
QSCALE = -(HD ** -0.5)
NX = 640
CH = 256
RING = 6
TRING, HRING = 6, 3


def bucket_rows():
    n = np.maximum(SEQ - 1 - np.arange(SEQ), 0)
    exact = BUCKETS // 2
    nf = np.maximum(n, 1).astype(np.float32)
    large = exact + (np.log(nf / np.float32(exact)) / np.float32(math.log(MAXD / exact)) * (BUCKETS - exact)).astype(np.int32)
    bucket = np.where(n < exact, n, np.minimum(large, BUCKETS - 1))
    return (bucket[None, :] == np.arange(BUCKETS)[:, None]).astype(np.float32)


def build(nc, I, O):
    ctx = ExitStack()
    with ctx:
        R_RING, R_H, R_C, R_Z, R_F, R_X, R_G = 0, 12288, 16896, 21504, 26112, 32880, 38000
        R_P = R_G + 11880
        base = -(-nc.sbuf_base // 32) * 32
        arena = ctx.enter_context(nc.sbuf_tensor("arena", [P, R_P], F32))
        kept = ctx.enter_context(nc.sbuf_tensor("kept", [P, 53150 - R_P], F32))
        page_sb = ctx.enter_context(nc.sbuf_tensor("page_sb", [1, 2 * DB], I32))
        psum = ctx.enter_context(nc.psum_tensor("psum", [P, 8 * 512], F32))
        bias_dram = nc.dram_tensor("bias_line", [H, NX], F32, kind="Internal").ap()
        bias_copies = nc.dram_tensor("bias_copies", [H, P, NX], F32, kind="Internal").ap()
        gate_dram = nc.dram_tensor("gate_rows", [NBR * H, NS], F32, kind="Internal").ap()
        x1_dram = nc.dram_tensor("x1_rows", [NT, D], F32, kind="Internal").ap()

        def at(off, *dims, p0=0, p1=P):
            n = int(np.prod(dims))
            v = arena[p0:p1, off:off + n] if off < R_P else kept[p0:p1, off - R_P:off - R_P + n]
            if len(dims) == 1:
                return v
            names = "abcdef"[:len(dims)]
            return v.rearrange(f"p ({' '.join(names)}) -> p {' '.join(names)}",
                               **{c: d for c, d in zip(names[1:], dims[1:])})

        def over(name, off, *dims, dtype=F32R):
            assert off % 8 == 0
            v = nc.alloc_sbuf_tensor_at(name, [P, int(np.prod(dims))], dtype, offset=base + 4 * off)[:, :]
            names = "abcdef"[:len(dims)]
            return v.rearrange(f"p ({' '.join(names)}) -> p {' '.join(names)}",
                               **{c: d for c, d in zip(names[1:], dims[1:])})

        def pb(b, *dims, p0=0, p1=P):
            n = int(np.prod(dims))
            v = psum[p0:p1, b * 512:b * 512 + n]
            if len(dims) == 1:
                return v
            names = "abcdef"[:len(dims)]
            return v.rearrange(f"p ({' '.join(names)}) -> p {' '.join(names)}",
                               **{c: d for c, d in zip(names[1:], dims[1:])})

        def halves(b):
            return pb(b, 2, 512)[:, :, 0:HT]

        ring = at(R_RING, RING, KD, CH)
        x_first = at(R_F, TT, D)
        x_sb = at(R_X, TT, D)
        h_whole = over("h_whole", R_H, KD, NT, dtype=F32)
        h_lo = over("h_lo", R_H, KD, NT)
        h_hi = over("h_hi", R_X, KD, NT)
        tap_sum = at(R_X + KD * NT, SEQ)
        hT = at(R_H, KD, NT)
        xn_a = at(R_C, 2, D)
        state_rows = at(R_C + 2 * D, 2, D)
        junk_a = at(R_Z, D)
        rel_rows = at(R_Z + 1024, H, p1=BUCKETS)
        hot_rows = at(R_Z + 1040, SEQ, p1=BUCKETS)
        pe_rows = at(R_Z + 1552, 2, P, p1=16)
        line = at(R_Z + 1808, NX, p1=H)
        glu_p = at(R_F, KD, SEQ + W - 1)
        glu_s = at(R_F + KD * (SEQ + W - 1), KD, DB, DS + W - 1)
        conv = at(R_C, KD, NT)
        zA = at(R_Z, KD, NT)
        rstd_ln = at(R_H, NT)
        conv_out_p = at(R_H + 1024, D)
        conv_out_s = at(R_H + 2048, D)
        xn_b = at(R_F, 2, D)
        gpost_a = at(R_F + 2048, D)
        junk_b = at(R_F + 3072, D)
        scaled_b = at(R_F + 4096, D)
        uT = over("u_whole", R_C, KD, NT, dtype=F32)
        u_hi = over("u_hi", R_X, KD, NT)
        u_lo = over("u_lo", R_C, KD, NT)
        tile_w = over("tile_whole", R_RING, TRING, KD, P, dtype=F32)
        tile_lo = over("tile_lo", R_RING, TRING, KD, P)
        tile_hi = over("tile_hi", R_RING + TRING * D, HRING, KD, P)
        ctS = at(R_G, 8, 33, 16)
        ctP = at(R_G, 2, 8, KV, 32)
        cmp_rows = at(R_G + 2048, 2, 2, KV, 2 * HD)
        w1_sb = at(R_G + 4224, 16, 256)
        rows_ring = at(R_G + 8320, 2, KV, P)
        new_rows = at(R_G + 8320, KD, NS)
        vecT = at(R_G + 9344, KD, 37)
        ones = at(R_G + 9640, P)
        hid = at(R_G + 9768, 2, 480)
        R_S = R_G + 10728
        sg = at(R_S, 2, NT)
        vec_rows = at(R_S, D)
        cmp_rows_s = at(R_S, 512)
        hid_p = at(R_S + 512, 2, 124)
        wgate = over("wgate_whole", R_S + 760, KD, 48, dtype=F32)
        wgate_lo = over("wgate_lo", R_S + 760, KD, 48)
        wgate_hi = over("wgate_hi", R_Z + 3200, KD, 48)
        k_stage = at(R_Z, 2, TT, CH)
        gateT = at(R_Z + 2560, NT)
        gate_tb = at(R_Z + 3136, DS, DB)
        v_sb = at(R_F, 2, TT, CH)
        ktz = at(R_F + 2560, 2, KV, SEQ)
        qT = at(R_H, KD, NT)
        yT = at(R_Z, KD, NT)
        sz = at(R_G, NBR, 2, SEQ)
        tb = at(R_G + 6144, 2, 2, SEQ)
        pt_sb = at(R_G + 8192, 4, SEQ)
        y_tmp = at(R_G + 10240, SEQ)
        qbd = at(R_G + 10752, DB, 2, HD)
        l_sb = at(R_RING + (TRING + HRING) * D, 6, SEQ)
        szs = at(R_G + 4096, NBR, KD, NS)
        pc_sb = at(R_X + 4608, 4, P)
        cache_sb = [at(R_C + 1024 * i, 2, 512) for i in range(4)] + [at(R_G + 1024 * i, 2, 512) for i in range(2)]
        kts = at(R_G + 6144, 2, 2, KS)
        pts = at(R_G + 8192, 2, 3, P)
        vnew = at(R_G + 8960, 6, CH, p1=DS)
        ptc = at(R_H, DB, P, p1=4 * NCS)
        orc = at(R_H + 1024, DB, P)
        y_br = at(R_H + 2048, 2, KD, NS)
        orow = at(R_H + 3072, 2, P)
        x1_back = at(R_F + 2560, 2, D)
        gpost_b = at(R_F + 2560 + 2 * D, D)
        junk_c = at(R_F + 2560 + 3 * D, D)
        y_out = at(R_G + 2048, 2, D)
        small = [R_P]

        def keep(*dims):
            off = small[0]
            small[0] += int(np.prod(dims))
            return at(off, *dims)

        ident = keep(P)
        kc_s = keep(DB, 4 * NCS)
        late_slots = at(small[0], 2, KV, P)
        vc_s = keep(DB, P)
        bsc = keep(4 * NCS)
        tap_term = at(small[0], SEQ)
        kt_new = keep(2, 2, NS)
        bs = keep(KS)
        kcbd = keep(2, 64)
        fold = at(small[0], P)
        vcbd = keep(2, P)
        pe_sb = keep(2, 16)
        pecol = keep(4)
        ss, ms, sd, rs = (keep(8) for _ in range(4))
        mn, den, rden = (keep(8 + 6) for _ in range(3))
        w2_off = small[0]
        w2_sb = keep(2, 2, P)
        gR = at(w2_off, 4, NBR * H)
        gS = at(w2_off + 192, NBR, DB)
        e2 = at(w2_off + 216, 2, 55)
        gRr = at(w2_off + 326, 4, H)
        assert small[0] <= 53150, small[0]

        def sem(name):
            return ctx.enter_context(nc.semaphore(name))

        S = {n: sem(n) for n in """
            zeroed ident_ready ones_ready zeroes vec_in vec_ps vec_ready state_in bias_in early_mm line_part line_out
            sq_a ms_a sd_a xn_a_ready tr_a h_ready state_tr state_ready
            proj_a sg_ready glu_ready z_ready conv_step term_ready term_added
            page_in w1_in pe_in pe_sb_ready pe_ready w2_in ct_tr ct_ready cs_mm pe_col hid_ready kc_mm kc_ready vc_mm vc_ready
            centred sqd stat_mm eps_ready std_ready lnx_ready lns_ready y_ready
            co_tr co_ready co_out new_packed late
            o_mm gpost_in sq_b ms_b sd_b o_scaled x1_ready sq_c ms_c sd_c xn_b_ready tr_b hu_ready x1_out
            kv_mm kv_ready uh_ready ul_ready hi_ready lo_ready lo_pool hh_ready hl_ready kt_tr kt_ready ctp_tr ctp_ready kv_out cp_mm hidp_ready cpp_mm bd_ready
            q_mm q_ready wg_in gate_mm gate_ready gate_tr gR_ready gate_out gS_in qbd_ready
            z_mm zb_ready silu_ready bs_in bsc_ready
            e2_ready s_done l_ready cmin_ready exp_done den_ready pn_ready
            t_done pt_a pt_d pv_done y_mul y_add
            skt_tr skt_ready kts_new ss_mm sl_ready se_ready sp_ready st_tr pts_ready so_mm or_ready ot_tr ys_mul y_s
            fo_mm fy
            """.split()}
        ZEROED = {"slot": 1, "blocks": 3, "bias": 4, "pad": 5, "keys": 9, "probs": 10, "table": 11, "queries": 12}
        w_in = [sem(f"w_in{i}") for i in range(RING)]
        x_in = [sem(f"x_in{i}") for i in range(TT)]
        rows_in = [sem(f"rows_in{i}") for i in range(4)]
        tb_in = [sem(f"tb_in{i}") for i in range(2)]
        slot_in = [sem(f"slot_in{i}") for i in range(TRING)]
        fy_out = [sem(f"fy_out{i}") for i in range(2)]
        dve_step = sem("dve_step")
        n_dve = [0]

        def kv_bank(n):
            return (2, 3, 0, 1, 4, 5)[n % 6]

        def rows_slot(n):
            return rows_ring[:, n % 4] if n % 4 < 2 else late_slots[:, n % 4 - 2]

        def link(dve, ins):
            n_dve[0] += 1
            ins.then_inc(dve_step, 1)
            dve.wait_ge(dve_step, n_dve[0])

        def cols(w, c0):
            return [(w[:, c0:c0 + CH].rearrange("(k p) n -> p k n", p=P), None)]

        def tile_cols(w, c0, m):
            c = c0 + ((m // 4) * 8 + m % 4) * HD
            return [(w[:, c + half * 256:c + half * 256 + HD].rearrange("(k p) n -> p k n", p=P), half * HD) for half in range(2)]

        a_w = I["a_w_in"][0]
        b_w = I["b_w_in"][0]
        chunks = [[(a_w[:, n * D + m * P:n * D + (m + 1) * P].rearrange("(k p) n -> p k n", p=P), 0)] for m in range(KD) for n in range(3)]
        C_OA = len(chunks)
        chunks += [cols(I["a_w_out"][0], c * CH) for c in range(4)]
        C_KV = len(chunks)
        chunks += [cols(I["w_kv"], c * CH) for c in range(6)]
        C_Q = len(chunks)
        chunks += [tile_cols(b_w, 0, m) for m in range(KD)]
        C_Z = len(chunks)
        chunks += [tile_cols(b_w, D * (1 + br), m) for m in range(KD) for br in range(NBR)]
        C_OB = len(chunks)
        for c in range(4):
            parts = []
            for p in range(2):
                for half in range(2):
                    r = p * 512 + half * 256
                    parts.append((I["b_w_out"][0][r:r + 256, c * CH:(c + 1) * CH].rearrange("(g d) n -> d g n", d=HD),
                                  ("out", p, half)))
            chunks.append(parts)

        def kv_at(c, t):
            return 10 * (c // 2) + (4 * (c % 2) + t if t < 4 else 8 + c % 2)

        last_use = {}
        for n in range(C_OA):
            last_use[n] = ("proj_a", n + 1)
        for n in range(4):
            last_use[C_OA + n] = ("o_mm", TT)
        for n in range(6):
            last_use[C_KV + n] = ("kv_mm", kv_at(n, 4) + 1)
        for m in range(KD):
            last_use[C_Q + m] = ("q_mm", m + 1)
        for n in range(NBR * KD):
            last_use[C_Z + n] = ("z_mm", n + 1)

        place = {}
        for c in range(len(chunks)):
            if C_Q <= c < C_OB or c < C_OA:
                i = (c - C_Q if c >= C_Q else c) % TRING
                place[c] = (D * i, D, slot_in[i])
            else:
                i = (4, 5, 3, 0, 1, 2)[c - C_KV] if C_KV <= c < C_Q else c % RING if c < C_KV else c - C_OB
                place[c] = (2 * D * i, 2 * D, w_in[i])
        kv_jobs = {kv_at(c, t): (c, t) for c in range(6) for t in range(TT)}
        waited = {}

        def frees(c):
            lo, n, _ = place[c]
            need = {}
            if lo < (TRING + HRING) * D and TRING * D < lo + n:
                need = {"z_mm": NBR * KD} if c >= C_OB else {"proj_a": C_OA}
            for b in range(c):
                if place[b][0] < lo + n and lo < place[b][0] + place[b][1]:
                    name, count = last_use[b]
                    need[name] = max(count, need.get(name, 0))
            need = {k: v for k, v in need.items() if v > waited.get(k, 0)}
            waited.update(need)
            return need.items()

        def chunk_sb(c):
            return ring[:, place[c][0] // (2 * D)]

        def chunk_dst(c, how):
            if c < C_OA:
                return tile_w[:, c % TRING]
            if C_Q <= c < C_OB:
                return tile_w[:, (c - C_Q) % TRING, :, how:how + HD]
            slot = chunk_sb(c)
            if how is None:
                return slot
            _, p, half = how
            return slot[half * HD:half * HD + HD, 4 * p:4 * p + 4, :]

        arrived, totals = {}, {}
        for c, parts in enumerate(chunks):
            into = place[c][2]
            totals[into] = totals.get(into, 0) + 16 * len(parts)
            arrived[c] = totals[into]

        def product_before(j):
            j -= HRING
            return ("q_mm", j + 1) if j < KD else ("z_mm", j - KD + 1)

        def rows(t):
            return P if t < 4 else NS

        UPM = 1 + 2 * 2 * 4
        items = []
        for m in range(KD):
            items.append((m, 0, None, [UPM * m]))
            for br in (1, 2):
                for i in range(4):
                    u = UPM * m + 1 + 8 * (br - 1) + 2 * i
                    items.append((m, br, i, [u, u + 1]))
        item_of = {u: w for w, it in enumerate(items) for u in it[3]}
        pt_by, n_a, n_d = {}, 0, 0
        for w, (m, br, i, us) in enumerate(items):
            for k, u in enumerate(us):
                if br and k == 0:
                    n_a += 1
                    pt_by[u] = ("pt_a", n_a)
                else:
                    n_d += 1
                    pt_by[u] = ("pt_d", n_d)
        N_UNITS = UPM * KD
        KV_OUT = 16 * (2 * 5 + 2 * 2 + 2)

        def stat(w):
            return 8 + 2 * (w % 3)

        z_at = {9 * m + 3 * i + 1: NBR * m + 2 + i for m in range(KD) for i in range(NBR) if NBR * m + 2 + i < NBR * KD}

        halves_at = {w: range(2 * w, 2 * w + 2) if w < 6 else range(w + 6, w + 7) for w in range(18)}
        norm_at = {0: 0, 4: 1, 10: 2, 18: 3}

        block = ctx.enter_context(nc.Block())

        @block.sync
        def _(sp):
            for t in range(TT):
                src = I["x_prompt"][0, t * P:(t + 1) * P, :] if t < 4 else I["x_sample"].rearrange("b t d -> (b t) d")
                sp.dma_start(x_first[0:rows(t), t], src).then_inc(x_in[t], 16)
            sp.dma_start(vec_rows[0:W], I["a_conv_w"][0]).then_inc(S["vec_in"], 16)
            for n, name in enumerate(("a_norm_pre", "a_conv_b", "a_ln_g", "a_ln_b", "kv_norm", "b_norm_pre")):
                src = I[name].rearrange("(a n) -> a n", a=1) if name == "kv_norm" else I[name]
                sp.dma_start(vec_rows[W + n:W + n + 1], src).then_inc(S["vec_in"], 16)

            def tables(m):
                if m < 2:
                    sp.wait_ge(S["line_out"], 80)
                    sp.wait_ge(S["cp_mm"], 4)
                else:
                    sp.wait_ge(S["e2_ready"], m - 1)
                    sp.wait_ge(S["l_ready"], UPM * (m - 1))
                for half in range(2):
                    h = 8 * (m // 4) + 4 * half + m % 4
                    src = bass.AP(bias_copies.tensor, h * P * NX + P - 1, [[NX - 1, P], [1, SEQ]])
                    sp.dma_start(tb[:, m % 2, half], src).then_inc(tb_in[m % 2], 16)

            cache = I["cache_cmp"].rearrange("g (s a) c k d -> g s a c k d", a=2)

            def past_cmp(n):
                c, b = n // DB, n % DB
                if n >= 4:
                    sp.wait_ge(S["ct_tr"], n - 3)
                for pg in range(2):
                    v = sp.value_load(page_sb[0:1, 2 * b + pg:2 * b + pg + 1], min_val=0, max_val=I["cache_cmp"].shape[0] - 1)
                    for par in range(2):
                        src = cache[bass.ds(v, 1), :, par, c, :, :]
                        sp.dma_start(rows_slot(n)[pg * 64:pg * 64 + 64, :, par * HD:(par + 1) * HD],
                                     src.rearrange("g s k d -> (g s) k d")).then_inc(rows_in[n % 4], 16)

            past_cmp_at = {3: range(4), 7: range(4, 7), 10: range(7, 10), 13: range(10, 12)}
            tables_at = {C_Z + 6: (0, 1), C_Z + 12: (2,), C_Z + 15: (3,), C_Z + 18: (4,), C_Z + 21: (5,), C_OB: (6, 7)}
            for c, parts in enumerate(chunks):
                for m in tables_at.get(c, ()):
                    tables(m)
                for name, count in frees(c):
                    sp.wait_ge(S[name], count)
                for src, how in parts:
                    sp.dma_start(chunk_dst(c, how), src).then_inc(place[c][2], 16)
                if c == 0:
                    for i in range(2):
                        sp.dma_start(state_rows[0:120, i], I["state_conv"][0, 4 * i:4 * i + 4].rearrange("b r n -> (b r) n")).then_inc(S["state_in"], 16)
                    sp.dma_start(rel_rows, I["rel_bias"]).then_inc(S["bias_in"], 16)
                    sp.dma_start(hot_rows, I["bucket_rows"]).then_inc(S["bias_in"], 16)
                    for k in range(2):
                        sp.dma_start(pe_rows[:, k], I["cmp_pe"][k].rearrange("(j a) d -> j (a d)", a=2)).then_inc(S["pe_in"], 16)
                if c == 3:
                    for k in range(2):
                        for ht in range(2):
                            for dup in range(2):
                                sp.dma_start(w2_sb[:, k, ht, dup * HD:(dup + 1) * HD], I["cmp_w2"][k, ht * P:(ht + 1) * P, :]).then_inc(S["w2_in"], 16)
                if c == 6:
                    sp.wait_ge(S["line_part"], 2)
                    sp.dma_start(bias_dram, line).then_inc(S["line_out"], 16)
                if 7 <= c < 11:
                    sp.wait_ge(S["line_out"], 16 * (c - 6))
                    h0 = 4 * (c - 7)
                    sp.dma_start(bias_copies[h0:h0 + 4], bias_dram[h0:h0 + 4].unsqueeze(1).broadcast_to([4, P, NX])).then_inc(S["line_out"], 16)
                if c == 2:
                    sp.dma_start(w1_sb, I["cmp_w1"][0].rearrange("(j p) n -> p j n", p=P)).then_inc(S["w1_in"], 16)
                if c in past_cmp_at:
                    sp.wait_ge(S["page_in"], 16)
                    for n in past_cmp_at[c]:
                        past_cmp(n)
                if c == C_OA:
                    sp.wait_ge(S["cs_mm"], 2)
                    sp.dma_start(w1_sb, I["cmp_w1"][1].rearrange("(j p) n -> p j n", p=P)).then_inc(S["w1_in"], 16)
                    for n in range(12, 16):
                        past_cmp(n)
                    sp.wait_ge(S["proj_a"], C_OA)
                    for t in range(4):
                        sp.dma_start(x_sb[:, t], I["x_prompt"][0, t * P:(t + 1) * P, :]).then_inc(x_in[t], 16)
                if c == C_OA + 1:
                    sp.wait_ge(S["conv_step"], CONV * KD)
                    sp.dma_start(x_sb[0:NS, 4], I["x_sample"].rearrange("b t d -> (b t) d")).then_inc(x_in[4], 16)
                    sp.wait_ge(S["line_out"], 80)
                    sp.dma_start(bs, bass.AP(bias_copies.tensor, SEQ - 1 - PAST, [[P * NX, H], [NX - 1, DS], [1, KS]])).then_inc(S["bs_in"], 16)
                if c == C_Q + 5:
                    sp.wait_ge(S["cp_mm"], 2)
                    sp.dma_start(w1_sb, I["cmp_w1"][0].rearrange("(j p) n -> p j n", p=P)).then_inc(S["w1_in"], 16)
            sp.wait_ge(S["z_mm"], 24)
            sp.wait_ge(S["page_in"], 16)

            def past_rows(n):
                b, br = n // 2, n % 2
                for pg in range(2):
                    if br == 0:
                        v = sp.value_load(page_sb[0:1, 2 * b + pg:2 * b + pg + 1], min_val=0, max_val=I["cache_slc"].shape[0] - 1)
                        src = I["cache_slc"].rearrange("g s c k d -> g s (c k d)")[bass.ds(v, 1), :, :].rearrange("a s n -> (a s) n")
                    else:
                        src = I["state_win"][b, pg * P:(pg + 1) * P].rearrange("s c k d -> s (c k d)")
                    sp.dma_start(cache_sb[n % 6][:, pg], src).then_inc(slot_in[n % 6], 16)

            def new_v_rows(n):
                b, br = n // 2, n % 2
                sp.dma_start(vnew[:, n % 6], v_sb[NS + DS * b:NS + DS * b + DS, br, 4, :]).then_inc(slot_in[n % 6], 16)

            def x1_rows(t):
                if t >= 2:
                    sp.wait_ge(S["fy"], t - 1)
                if t < 4:
                    sp.dma_start(x1_back[:, t % 2], x1_dram[t * P:(t + 1) * P, :]).then_inc(x_in[t % 2], 16)
                else:
                    for half in range(2):
                        sp.dma_start(x1_back[half * NS:half * NS + NS, 0, 0:D // 2],
                                     x1_dram[SEQ:NT, half * D // 2:(half + 1) * D // 2]).then_inc(x_in[0], 16)

            for n in range(4):
                past_rows(n)
            sp.wait_ge(S["x1_out"], 16 * TT)
            sp.wait_ge(S["t_done"], N_UNITS)
            sp.dma_start(gpost_b, I["b_norm_post"][0:1, :].broadcast_to([P, D])).then_inc(S["gpost_in"], 16)
            x1_rows(0)
            x1_rows(1)
            sp.wait_ge(S["y_mul"], 24)
            sp.wait_ge(S["pv_done"], len(items))
            sp.wait_ge(S["y_add"], 2 * KD)
            for n in range(2 * DB):
                if n >= 6:
                    sp.wait_ge(S["so_mm"], n - 4)
                if n >= 4:
                    past_rows(n)
                new_v_rows(n)
                if n in (8, 12):
                    x1_rows(n // 4)
            x1_rows(4)
            sp.wait_ge(x_in[0], 16 * 6)
            sp.wait_ge(x_in[1], 16 * 4)

        @block.gpsimd
        def _(pool):
            pool.memset(ident, 0.0).then_inc(S["zeroed"], 1)
            pool.wait_ge(S["zeroed"], 1)
            pool.affine_select(out=ident, in_=ident, compare_op=ALU.not_equal, fill=1.0, base=0,
                               pattern=[[-1, P]], channel_multiplier=1).then_inc(S["ident_ready"], 1)
            pool.dma_start(page_sb[:, :], I["page_table"].rearrange("b (g a) -> a (b g)", a=1)).then_inc(S["page_in"], 16)
            pool.memset(line[:, SEQ:NX], BIG).then_inc(S["line_part"], 1)
            pool.memset(ones, 1.0 / D).then_inc(S["ones_ready"], 1)
            pool.memset(ctS[:, :, 32, :], 0.0).then_inc(S["zeroes"], 1)
            pool.memset(kcbd, 0.0).then_inc(S["zeroes"], 1)
            pool.memset(vcbd, 0.0).then_inc(S["zeroes"], 1)
            pool.memset(bsc, BIG).then_inc(S["zeroes"], 1)
            pool.wait_ge(S["xn_a_ready"], TT)
            pool.memset(glu_p[:, :, 0:W - 1], 0.0).then_inc(S["zeroes"], 1)

            def split_lo_a(j):
                pool.wait_ge(S["hi_ready"], j + 1)
                pool.tensor_tensor(out=tile_lo[:, j % TRING], in0=tile_w[:, j % TRING], in1=tile_hi[:, j % HRING],
                                   op=ALU.subtract).then_inc(S["lo_pool"], 1)

            split_lo_a(1)
            split_lo_a(2)
            for m in range(KD):
                if m + 1 < KD:
                    split_lo_a(3 * m + 3)
                    split_lo_a(3 * m + 4)
                for i in range(1, W_OFF):
                    if m + 1 < KD and i == 1:
                        split_lo_a(3 * m + 5)
                    pool.wait_ge(S["term_ready"], W_OFF * m + i + 1)
                    if i > 1:
                        pool.wait_ge(S["term_added"], (W_OFF - 1) * m + i - 1)
                    pool.tensor_tensor(out=tap_sum, in0=tap_sum, in1=tap_term, op=ALU.add).then_inc(S["term_added"], 1)
            pool.dma_start(O["conv_sample"][0, :, 0:W - 1 - DS, :], I["state_conv"][0, :, DS:W - 1, :]).then_inc(S["late"], 16)
            pool.dma_start(O["win_sample"][:, 0:PAST], I["state_win"]).then_inc(S["late"], 16)
            pool.wait_ge(S["z_ready"], KD)
            for m in range(KD):
                pool.wait_ge(S["lns_ready"], m + 1)
                pool.tensor_tensor(out=zA[:, m], in0=conv[:, m], in1=zA[:, m], op=ALU.mult).then_inc(S["y_ready"], 1)
            pool.wait_ge(S["tr_b"], TT)
            pool.wait_ge(S["x1_ready"], TT)
            pool.wait_ge(S["sq_c"], TT)
            for lo in range(2):
                for br in range(2):
                    pool.memset(ktz[64 - 64 * lo:P - 64 * lo, br, lo:KV:2, :], 0.0).then_inc(S["zeroes"], 1)
            pool.wait_ge(S["x1_out"], 16 * TT)
            pool.wait_ge(S["xn_b_ready"], TT)
            pool.wait_ge(S["zeroes"], ZEROED["keys"])
            pool.memset(pc_sb, 0.0).then_inc(S["zeroes"], 1)
            pool.wait_ge(S["kv_ready"], 30)
            for kind in range(2):
                for b in range(DB):
                    pool.dma_start(O["win_sample"][b, PAST:KS, kind].rearrange("t k d -> t (k d)"),
                                   (v_sb if kind else k_stage)[kind * NS + DS * b:kind * NS + DS * b + DS, 1, 4]).then_inc(S["late"], 16)
            pool.wait_ge(S["cpp_mm"], 2)
            pool.wait_ge(S["gate_mm"], 1)
            pool.wait_ge(S["kv_out"], KV_OUT)
            pool.memset(e2, BIG).then_inc(S["zeroes"], 1)
            pool.memset(qbd, 0.0).then_inc(S["zeroes"], 1)
            pool.wait_ge(S["gR_ready"], 5)
            for w in range(len(items) + 3):
                if w < len(items):
                    m, br, i, us = items[w]
                    pool.wait_ge(S["den_ready"], w + 1)
                    if br == 0:
                        if m == 0:
                            pool.wait_ge(S["zeroes"], ZEROED["probs"])
                        else:
                            pool.wait_ge(S["t_done"], UPM * (m - 1) + 1)
                        dst = pc_sb[:, :, 0:64].rearrange("q i (h n) -> q i h n", h=2)[:, :, :, 0:NCP]
                        src = l_sb[:, us[0] % 6, 0:8 * NCP].rearrange("q (i h n) -> q i h n", i=4, h=2)
                        r = rden[:, 0:8].rearrange("q (i h) -> q i h", i=4).unsqueeze(3).broadcast_to([P, 4, 2, NCP])
                        pool.tensor_tensor(out=dst, in0=src, in1=r, op=ALU.mult).then_inc(S["pn_ready"], 1)
                    else:
                        for half, u in enumerate(us):
                            h = br * H + 8 * (m // 4) + 4 * half + m % 4
                            L = l_sb[:, u % 6, 0:P * (i + 1)]
                            pool.tensor_scalar(L, L, rden[:, stat(w) + half:stat(w) + half + 1], gR[:, i, h:h + 1],
                                               ALU.mult, ALU.mult).then_inc(S["pn_ready"], 1)
                if w >= 3 and items[w - 3][1] and items[w - 3][2] == 3:
                    m, br = items[w - 3][:2]
                    pool.wait_ge(S["y_mul"], 3 * m + br + 1)
                    if br == 2:
                        pool.wait_ge(S["y_add"], 2 * m + 1)
                    pool.tensor_tensor(out=yT[:, m, 0:SEQ], in0=yT[:, m, 0:SEQ], in1=y_tmp, op=ALU.add).then_inc(S["y_add"], 1)
            for n in range(2 * DB):
                b, br = n // 2, n % 2
                if n >= 2:
                    pool.wait_ge(S["ss_mm"], n)
                else:
                    pool.wait_ge(S["l_ready"], N_UNITS)
                pool.tensor_copy(kts[:, n % 2, :, PAST:KS], kt_new[:, br, :, DS * b:DS * b + DS]).then_inc(S["kts_new"], 1)

        @block.scalar
        def _(act):
            def copy(out, in_, scale=1.0):
                return nc.scalar.activation(out, in_, ACT.Copy, scale=scale)

            for t in range(TT):
                r = rows(t)
                act.wait_ge(x_in[t], 16)
                if t:
                    act.wait_ge(S["sq_a"], t)
                nc.scalar.activation(junk_a[0:r], x_first[0:r, t], ACT.Square, accum_out=ss[0:r, t:t + 1]).then_inc(S["sq_a"], 1)
            for t in range(TT):
                r = rows(t)
                act.wait_ge(S["ms_a"], t + 1)
                nc.scalar.activation(sd[0:r, t:t + 1], ms[0:r, t:t + 1], ACT.Sqrt).then_inc(S["sd_a"], 1)
            act.wait_ge(S["early_mm"], 1)
            copy(line[:, 0:SEQ], pb(0, SEQ, p1=H), -1.0).then_inc(S["line_part"], 1)
            act.wait_ge(S["early_mm"], 2)
            copy(pe_sb, pb(1, 2, 16)).then_inc(S["pe_sb_ready"], 1)
            act.wait_ge(S["pe_sb_ready"], 1)
            act.wait_ge(S["zeroes"], ZEROED["slot"])

            def pe_slot(c):
                copy(ctS[:, :, 32, 0:2].rearrange("p j c -> p c j"), pe_sb[:, c].rearrange("p (c j) -> p c j", c=2)).then_inc(S["pe_ready"], 1)

            pe_slot(0)
            for t in range(TT):
                act.wait_ge(S["h_ready"], t + 1)
                here = slice(t * P, t * P + rows(t))
                copy(h_hi[:, :, here], h_whole[:, :, here]).then_inc(S["hh_ready"], 1)

            def split_hi_a(j):
                act.wait_ge(slot_in[j % TRING], arrived[j])
                if j >= HRING:
                    act.wait_ge(S["proj_a"], j - HRING + 1)
                copy(tile_hi[:, j % HRING], tile_w[:, j % TRING]).then_inc(S["hi_ready"], 1)

            for j in range(HRING):
                split_hi_a(j)
            act.wait_ge(S["xn_a_ready"], TT)
            for n in range(4):
                i, mg = n // 2, n % 2
                act.wait_ge(S["state_tr"], n + 1)
                for b in range(4):
                    copy(glu_s[:, 4 * mg:4 * mg + 4, 4 * i + b, 0:W - 1],
                         pb(6 + n % 2, 4, 120)[:, :, b * (W - 1):(b + 1) * (W - 1)]).then_inc(S["state_ready"], 1)

            def ct_copy(n):
                b = n % DB
                act.wait_ge(S["ct_tr"], n + 1)
                copy(ctS[:, :, KV * b:KV * b + KV, :].rearrange("p j s c -> p s c j"), pb(6 + n % 2, KV, 16, 8)).then_inc(S["ct_ready"], 1)

            def compress_silu(c):
                for ht in range(2):
                    act.wait_ge(S["cs_mm"], 2 * c + ht + 1)
                    copy(pecol[:, 2 * c + ht:2 * c + ht + 1], pb(6 + ht, 495)[:, 480:481]).then_inc(S["pe_col"], 1)
                    act.wait_ge(S["pe_col"], 2 * c + ht + 1)
                    if c:
                        act.wait_ge(S["kc_mm"], 1)
                    nc.scalar.activation(hid[:, ht], pb(6 + ht, 480), ACT.Silu, bias=pecol[:, 2 * c + ht:2 * c + ht + 1]).then_inc(S["hid_ready"], 1)

            for m in range(KD):
                if m == 7:
                    compress_silu(0)
                    pe_slot(1)
                act.wait_ge(S["proj_a"], 3 * m + 2)
                if m >= 2:
                    act.wait_ge(S["glu_ready"], 3 * (m - 1))
                else:
                    act.wait_ge(S["vec_ps"], 1)
                nc.scalar.activation(sg[:, m % 2].rearrange("p (a n) -> p a n", a=2), halves(2), ACT.Sigmoid).then_inc(S["sg_ready"], 1)
                if m + 1 < KD:
                    split_hi_a(3 * m + 3)
                    split_hi_a(3 * m + 4)
                if m < 3:
                    for n in range(3 * m, min(3 * m + 3, DB)):
                        ct_copy(n)
                if m == 7:
                    act.wait_ge(S["kc_mm"], 1)
                    copy(kc_s.rearrange("p b n -> p (b n)"), pb(6, 480)).then_inc(S["kc_ready"], 1)
                act.wait_ge(S["proj_a"], 3 * m + 3)
                if m == 0:
                    act.wait_ge(S["sq_a"], TT)
                if m == 3:
                    act.wait_ge(S["line_out"], 16)
                nc.scalar.activation(zA[:, m].rearrange("p (a n) -> p a n", a=2), halves(4), ACT.Silu).then_inc(S["z_ready"], 1)
                if m + 1 < KD:
                    split_hi_a(3 * m + 5)
                act.wait_ge(S["glu_ready"], 3 * m + 3)
                for i in range(W_OFF):
                    w = W - W_OFF + i
                    if m == KD - 1 and 0 < i < 5:
                        ct_copy(DB + i - 1)
                    if i == 0 and m > 0:
                        act.wait_ge(S["conv_step"], CONV * m)
                    if i > 0 and (W_OFF - 1) * m + i > 1:
                        act.wait_ge(S["term_added"], (W_OFF - 1) * m + i - 1)
                    nc.scalar.activation(tap_term if i else tap_sum, glu_p[:, m, w:w + SEQ], ACT.Copy,
                                         scale=vecT[:, m, w:w + 1]).then_inc(S["term_ready"], 1)

            act.wait_ge(S["glu_ready"], 3 * KD)
            for m in range(KD):
                act.wait_ge(S["centred"], m + 1)
                if m >= 2:
                    act.wait_ge(S["stat_mm"], m)
                nc.scalar.activation(sg[:, m % 2], conv[:, m], ACT.Square).then_inc(S["sqd"], 1)
            for b in range(4, DB):
                ct_copy(DB + b)
            act.wait_ge(S["eps_ready"], 1)
            nc.scalar.activation(rstd_ln, rstd_ln, ACT.Sqrt).then_inc(S["std_ready"], 1)
            for m in range(KD):
                act.wait_ge(S["lnx_ready"], m + 1)
                nc.scalar.activation(conv[:, m], conv[:, m], ACT.Silu, scale=vecT[:, m, W + 2:W + 3],
                                     bias=vecT[:, m, W + 3:W + 4]).then_inc(S["lns_ready"], 1)
            compress_silu(1)
            act.wait_ge(S["vc_mm"], 1)
            copy(vc_s[0:60].rearrange("p b n -> p (b n)"), pb(4, 1024, p1=60)).then_inc(S["vc_ready"], 1)
            act.wait_ge(S["co_tr"], 1)
            copy(conv_out_p[0:W - 1], pb(0, D, p1=W - 1)).then_inc(S["co_ready"], 1)
            act.wait_ge(S["co_tr"], 2)
            copy(conv_out_s[0:NS], pb(2, D, p1=NS)).then_inc(S["co_ready"], 1)
            act.wait_ge(S["co_ready"], 2)
            act.dma_start(O["conv_prompt"][0, 0], conv_out_p[0:W - 1]).then_inc(S["co_out"], 16)
            for b in range(DB):
                act.dma_start(O["conv_sample"][0, b, W - 1 - DS:W - 1], conv_out_s[DS * b:DS * b + DS]).then_inc(S["co_out"], 16)
            act.dma_start(gpost_a, I["a_norm_post"][0:1, :].broadcast_to([P, D])).then_inc(S["gpost_in"], 16)

            for t in range(TT):
                r = rows(t)
                act.wait_ge(S["o_mm"], t + 1)
                if t:
                    act.wait_ge(S["sq_c"], t)
                    act.wait_ge(S["o_scaled"], t)
                nc.scalar.activation(junk_b[0:r], pb(2 * (t % 2), D, p1=r), ACT.Square, accum_out=ss[0:r, 0:1]).then_inc(S["sq_b"], 1)
                act.wait_ge(S["ms_b"], t + 1)
                nc.scalar.activation(sd[0:r, 0:1], ms[0:r, 0:1], ACT.Sqrt).then_inc(S["sd_b"], 1)
                act.wait_ge(S["x1_ready"], t + 1)
                act.dma_start(x1_dram[t * P:t * P + r, :], x_sb[0:r, t]).then_inc(S["x1_out"], 16)
                act.wait_ge(S["sq_b"], t + 1)
                nc.scalar.activation(junk_b[0:r], x_sb[0:r, t], ACT.Square, accum_out=ss[0:r, 1:2]).then_inc(S["sq_c"], 1)
                act.wait_ge(S["ms_c"], t + 1)
                nc.scalar.activation(sd[0:r, 1:2], ms[0:r, 1:2], ACT.Sqrt).then_inc(S["sd_c"], 1)

            act.wait_ge(S["vc_mm"], 1)
            act.dma_start(wgate, b_w[:, 4 * D:4 * D + 48].rearrange("(k p) n -> p k n", p=P)).then_inc(S["wg_in"], 16)
            def split_hi(j):
                if j == KD:
                    act.wait_ge(S["wg_in"], 16)
                    act.wait_ge(S["o_mm"], TT)
                    copy(wgate_hi, wgate).then_inc(S["hi_ready"], 1)
                    return
                j -= j > KD
                act.wait_ge(slot_in[j % TRING], arrived[C_Q + j])
                if j >= HRING:
                    name, count = product_before(j)
                    act.wait_ge(S[name], count)
                copy(tile_hi[:, j % HRING], tile_w[:, j % TRING]).then_inc(S["hi_ready"], 1)

            for n in range(30):
                br, (c, t) = n // 10, kv_jobs[n]
                kind = c % 2
                if n == 10:
                    act.wait_ge(S["x1_out"], 16 * TT)
                    act.wait_ge(S["xn_b_ready"], TT)
                    act.wait_ge(S["hu_ready"], 2 * TT)
                    for m in range(KD):
                        copy(u_hi[:, m], uT[:, m]).then_inc(S["uh_ready"], 1)
                if n == 24:
                    split_hi(0)
                    split_hi(1)
                p0 = kind * NS if t == 4 else 0
                here = slice(p0, p0 + rows(t))
                act.wait_ge(S["kv_mm"], n + 1)
                src = pb(kv_bank(n), CH)[here]
                if br == 0 and t < 4:
                    dst = cmp_rows[:, t // 2, kind, :, HD * (t % 2):HD * (t % 2) + HD]
                    src = src.rearrange("p (k d) -> p k d", d=HD)
                elif br == 0:
                    dst = cmp_rows_s[here, kind * CH:(kind + 1) * CH]
                else:
                    dst = (v_sb if kind else k_stage)[here, br - 1, t]
                copy(dst, src).then_inc(S["kv_ready"], 1)
                if n % 10 < 9:
                    continue
                act.wait_ge(S["kv_ready"], n + 1)
                for kind in range(2):
                    here = slice(kind * NS, kind * NS + NS)
                    if br == 0:
                        for gi in range(2):
                            for par in range(2):
                                dst = O["cmp_prompt"][0, gi * 256:(gi + 1) * 256, kind].rearrange("(q a) k d -> q a k d", a=2)[:, par]
                                act.dma_start(dst, cmp_rows[:, gi, kind, :, par * HD:par * HD + HD]).then_inc(S["kv_out"], 16)
                        act.dma_start(O["cmp_sample"][:, :, kind].rearrange("b t k d -> (b t) (k d)"),
                                      cmp_rows_s[here, kind * CH:(kind + 1) * CH]).then_inc(S["kv_out"], 16)
                        continue
                    name, R = ("slc", "win")[br - 1], (v_sb if kind else k_stage)
                    dst = O[name + "_prompt"][0, :, kind].rearrange("(t p) k d -> p t (k d)", p=P)
                    act.dma_start(dst, R[:, br - 1, 0:4]).then_inc(S["kv_out"], 16)
                    if br == 1:
                        act.dma_start(O["slc_sample"][:, :, kind].rearrange("b t k d -> (b t) (k d)"), R[here, 0, 4]).then_inc(S["kv_out"], 16)
            split_hi(2)

            def compress_p_silu(n, c):
                for ht in range(2):
                    act.wait_ge(S["cp_mm"], 2 * n + ht + 1)
                    if n:
                        act.wait_ge(S["cpp_mm"], 1)
                    nc.scalar.activation(hid_p[:, ht], pb(4 + ht, 124), ACT.Silu, bias=pecol[:, 2 * c + ht:2 * c + ht + 1]).then_inc(S["hidp_ready"], 1)
                act.wait_ge(S["cpp_mm"], n + 1)
                act.wait_ge(S["zeroes"], ZEROED["blocks"])
                for p in range(2):
                    for half in range(2):
                        lo = HD * half
                        if c:
                            copy(vcbd[32 * half:32 * half + NCP, p, lo:lo + HD],
                                 pb(2 + p, HD, p0=32 * half, p1=32 * half + NCP)).then_inc(S["bd_ready"], 1)
                        else:
                            copy(kcbd[lo:lo + HD, p, 32 * half:32 * half + NCP],
                                 pb(0, KV, NCP, p0=lo, p1=lo + HD)[:, 2 * p + half]).then_inc(S["bd_ready"], 1)

            compress_p_silu(0, 1)
            for m in range(KD):
                act.wait_ge(S["q_mm"], m + 1)
                copy(qT[:, m].rearrange("p (a n) -> p a n", a=2), halves(2 * (m % 3)), QSCALE).then_inc(S["q_ready"], 1)
                split_hi(m + HRING)
            split_hi(KD + HRING)
            act.wait_ge(S["gate_mm"], 1)
            nc.scalar.activation(gateT[0:48].rearrange("p (a n) -> p a n", a=2), halves(6)[0:48], ACT.Sigmoid).then_inc(S["gate_ready"], 1)
            act.wait_ge(S["gate_ready"], 1)
            copy(gate_tb[0:48], gateT[0:48, SEQ:NT].rearrange("r (b t) -> r t b", b=DB)).then_inc(S["gate_ready"], 1)
            act.wait_ge(S["gate_ready"], 2)
            act.dma_start(gate_dram, gate_tb[0:48].rearrange("r t b -> r (t b)")).then_inc(S["gate_out"], 16)
            compress_p_silu(1, 0)
            act.wait_ge(S["gate_out"], 16)
            for br in range(NBR):
                act.dma_start(gS[:, br], bass.AP(gate_dram.tensor, br * H * NS, [[DB, P], [1, DB]])).then_inc(S["gS_in"], 16)

            def z_copy(n, b0):
                m, br = n // NBR, n % NBR
                act.wait_ge(S["z_mm"], n + 1)
                if m >= 2:
                    act.wait_ge(S["y_mul"], 3 * (m - 2) + br + 1)
                lo, hi = pb(b0, HT), pb(b0 + 1, HT)
                copy(sz[:, br, m % 2, 0:HT], lo).then_inc(S["zb_ready"], 1)
                copy(sz[:, br, m % 2, HT:SEQ], hi[:, 0:SEQ - HT]).then_inc(S["zb_ready"], 1)
                copy(szs[:, br, m], hi[:, SEQ - HT:HT]).then_inc(S["zb_ready"], 1)

            def silu(z):
                nc.scalar.activation(z, z, ACT.Silu).then_inc(S["silu_ready"], 1)

            def z_silu(m):
                act.wait_ge(S["zb_ready"], 3 * min(NBR * m + 5, NBR * KD))
                silu(sz[:, 2, m % 2])
                silu(szs[:, 2, m])
                if m + 1 < KD:
                    silu(sz[:, 0:2, (m + 1) % 2])
                    silu(szs[:, 0:2, m + 1])

            act.wait_ge(S["x1_out"], 16 * TT)
            act.wait_ge(S["cp_mm"], 4)
            act.wait_ge(S["kv_out"], KV_OUT)
            for n in range(2):
                z_copy(n, 2 * n)
                split_hi(KD + 1 + n + HRING)
            act.wait_ge(S["zb_ready"], 6)
            silu(sz[:, 0:2, 0])
            silu(szs[:, 0:2, 0])

            for w in range(len(items) + 2):
                if w < len(items):
                    m, br, i, us = items[w]
                    act.wait_ge(S["l_ready"], us[-1] + 1)
                    if br == 0:
                        act.wait_ge(S["cmin_ready"], m + 1)
                        L = l_sb[:, us[0] % 6, 0:8 * NCP]
                        nc.scalar.activation(L, L, ACT.Exp, scale=-1.0).then_inc(S["exp_done"], 1)
                    else:
                        if w >= 3:
                            act.wait_ge(S["den_ready"], w - 2)
                        for half, u in enumerate(us):
                            L = l_sb[:, u % 6, 0:P * (i + 1)]
                            k = stat(w) + half
                            nc.scalar.activation(L, L, ACT.Exp, scale=-1.0, bias=mn[:, k:k + 1],
                                                 accum_out=den[:, k:k + 1]).then_inc(S["exp_done"], 1)
                if w >= 2 and items[w - 2][1]:
                    i, u = items[w - 2][2], items[w - 2][3][0]
                    act.wait_ge(S["t_done"], u + 1)
                    if u >= 4:
                        act.wait_ge(S["pv_done"], item_of[u - 4] + 1)
                    copy(pt_sb[:, u % 4, 0:P * (i + 1)], pb(3 + u % 2, P * (i + 1))).then_inc(S["pt_a"], 1)
                if w in z_at:
                    z_copy(z_at[w], 6)
                if w - 1 in z_at and z_at[w - 1] + HRING < NBR * KD:
                    split_hi(KD + 1 + z_at[w - 1] + HRING)
                if w % 9 == 8 and w < len(items):
                    z_silu(w // 9)

            def last_square(t):
                r = rows(t)
                act.wait_ge(S["fo_mm"], t + 1)
                if t:
                    act.wait_ge(S["sq_a"], TT + t)
                else:
                    act.wait_ge(S["t_done"], N_UNITS)
                nc.scalar.activation(junk_c[0:r], pb(4 + 2 * (t % 2), D, p1=r), ACT.Square, accum_out=ss[0:r, t:t + 1]).then_inc(S["sq_a"], 1)

            def last_root(t):
                r = rows(t)
                act.wait_ge(S["ms_a"], TT + t + 1)
                nc.scalar.activation(sd[0:r, t:t + 1], ms[0:r, t:t + 1], ACT.Sqrt).then_inc(S["sd_a"], 1)

            def last_out(t):
                act.wait_ge(S["fy"], t + 1)
                act.dma_start(O["y_prompt"][0, t * P:(t + 1) * P], y_out[:, t % 2]).then_inc(fy_out[t % 2], 16)

            act.wait_ge(S["cmin_ready"], KD + 1)
            L = l_sb[:, 0, 0:480]
            nc.scalar.activation(L, L, ACT.Exp, scale=-1.0).then_inc(S["exp_done"], 1)
            for n in range(2 * DB + 5):
                if n < 2 * DB:
                    act.wait_ge(S["skt_tr"], n + 1)
                    if n >= 2:
                        act.wait_ge(S["ss_mm"], n)
                    act.wait_ge(S["l_ready"], N_UNITS)
                    copy(kts[:, n % 2, :, 0:PAST], pb(0, 2, PAST)).then_inc(S["skt_ready"], 1)
                if 1 <= n <= 2 * DB:
                    k = n - 1
                    act.wait_ge(S["sl_ready"], k + 2)
                    if k >= 4:
                        act.wait_ge(S["sp_ready"], k - 2)
                    L = l_sb[:, 1 + k % 3, 0:KS]
                    nc.scalar.activation(L, L, ACT.Exp, scale=-1.0, bias=mn[:, 8 + k % 4:9 + k % 4],
                                         accum_out=den[:, 8 + k % 4:9 + k % 4]).then_inc(S["se_ready"], 1)
                if n in norm_at:
                    last_square(norm_at[n])
                    last_root(norm_at[n])
                if n - 2 in norm_at:
                    last_out(norm_at[n - 2])
            act.wait_ge(S["fo_mm"], TT)
            act.wait_ge(S["sq_a"], TT + 4)
            nc.scalar.activation(junk_c[:, 0:D // 2], pb(4, D // 2), ACT.Square, accum_out=ss[:, 4:5]).then_inc(S["sq_a"], 1)
            act.wait_ge(S["ms_a"], 2 * TT)
            nc.scalar.activation(sd[:, 4:5], ms[:, 4:5], ACT.Sqrt).then_inc(S["sd_a"], 1)
            act.wait_ge(S["fy"], 6)
            for half in range(2):
                act.dma_start(O["y_sample"].rearrange("b t d -> (b t) d")[:, half * D // 2:(half + 1) * D // 2],
                              y_out[half * NS:half * NS + NS, 0, 0:D // 2]).then_inc(fy_out[0], 16)
            act.wait_ge(fy_out[0], 16 * 4)
            act.wait_ge(fy_out[1], 16 * 2)
            act.wait_ge(S["co_out"], 16 * (1 + DB))
            act.wait_ge(S["late"], 16 * (2 + 2 * DB))

        @block.vector
        def _(dve):
            V = nc.vector
            def mean_sq(col, r, name):
                V.tensor_scalar(ms[0:r, col:col + 1], ss[0:r, col:col + 1], 1.0 / D, EPS, ALU.mult, ALU.add).then_inc(S[name], 1)

            def gain(k, r):
                return vecT[:, :, W + k:W + k + 1].broadcast_to([P, KD, r])

            for t in range(TT):
                dve.wait_ge(S["sq_a"], t + 1)
                mean_sq(t, rows(t), "ms_a")
            for t in range(TT + 1):
                if t == 1:
                    dve.wait_ge(S["vec_ps"], 1)
                    V.tensor_copy(vecT, pb(2, KD, 37)).then_inc(S["vec_ready"], 1)
                    dve.wait_ge(S["vec_ready"], 1)
                if t < TT:
                    r = rows(t)
                    dve.wait_ge(S["sd_a"], t + 1)
                    link(dve, V.reciprocal(rs[0:r, t:t + 1], sd[0:r, t:t + 1]))
                    if t >= 2:
                        dve.wait_ge(S["tr_a"], t - 1)
                    V.tensor_scalar(xn_a[0:r, t % 2], x_first[0:r, t], rs[0:r, t:t + 1], None, ALU.mult).then_inc(S["xn_a_ready"], 1)
                if t:
                    k, r = t - 1, rows(t - 1)
                    dve.wait_ge(S["tr_a"], k + 1)
                    V.tensor_tensor(out=h_whole[:, :, k * P:k * P + r], in0=pb(4 + 2 * (k % 2), KD, P)[:, :, 0:r], in1=gain(0, r),
                                    op=ALU.mult).then_inc(S["h_ready"], 1)
            for t in range(TT):
                dve.wait_ge(S["hh_ready"], t + 1)
                here = slice(t * P, t * P + rows(t))
                V.tensor_tensor(out=h_lo[:, :, here], in0=h_whole[:, :, here], in1=h_hi[:, :, here], op=ALU.subtract).then_inc(S["hl_ready"], 1)

            def split_lo_a(j):
                dve.wait_ge(S["hi_ready"], j + 1)
                V.tensor_tensor(out=tile_lo[:, j % TRING], in0=tile_w[:, j % TRING], in1=tile_hi[:, j % HRING],
                                op=ALU.subtract).then_inc(S["lo_ready"], 1)

            split_lo_a(0)
            dve.wait_ge(S["zeroes"], ZEROED["pad"])
            dve.wait_ge(S["state_ready"], 16)
            for m in range(KD):
                dve.wait_ge(S["proj_a"], 3 * m + 2)
                dve.wait_ge(S["sg_ready"], m + 1)
                a, g = pb(0, 1024), sg[:, m % 2]
                V.tensor_tensor(out=glu_p[:, m, W - 1:W - 1 + HT], in0=a[:, 0:HT], in1=g[:, 0:HT], op=ALU.mult).then_inc(S["glu_ready"], 1)
                V.tensor_tensor(out=glu_p[:, m, W - 1 + HT:W - 1 + SEQ], in0=a[:, 512:512 + SEQ - HT], in1=g[:, HT:SEQ],
                                op=ALU.mult).then_inc(S["glu_ready"], 1)
                V.tensor_tensor(out=glu_s[:, m, :, W - 1:W - 1 + DS],
                                in0=a[:, 512 + SEQ - HT:512 + HT].rearrange("p (b t) -> p b t", b=DB),
                                in1=g[:, SEQ:NT].rearrange("p (b t) -> p b t", b=DB), op=ALU.mult).then_inc(S["glu_ready"], 1)
                dve.wait_ge(S["glu_ready"], 3 * (m + 1))
                before = CONV * m
                for w in range(W):
                    parts = [(glu_s[:, m, :, w:w + DS], conv[:, m, SEQ:NT].rearrange("p (b t) -> p b t", b=DB))]
                    if w < W - W_OFF:
                        parts.append((glu_p[:, m, w:w + SEQ], conv[:, m, 0:SEQ]))
                    for part, (src, dst) in enumerate(parts):
                        tap = vecT[:, m, w:w + 1]
                        if w == 0:
                            ins = V.tensor_scalar(dst, src, tap, vecT[:, m, W + 1:W + 2], ALU.mult, ALU.add)
                        else:
                            dve.wait_ge(S["conv_step"], before + min(2 * w - 1 + part, w + W - W_OFF))
                            ins = V.scalar_tensor_tensor(out=dst, in0=src, scalar=tap, in1=dst, op0=ALU.mult, op1=ALU.add)
                        ins.then_inc(S["conv_step"], 1)
                dve.wait_ge(S["term_added"], (W_OFF - 1) * (m + 1))
                V.tensor_tensor(out=conv[:, m, 0:SEQ], in0=conv[:, m, 0:SEQ], in1=tap_sum, op=ALU.add).then_inc(S["conv_step"], 1)
            dve.wait_ge(S["stat_mm"], 1)
            for m in range(KD):
                dve.wait_ge(S["conv_step"], CONV * (m + 1))
                V.tensor_tensor(out=conv[:, m].rearrange("p (a n) -> p a n", a=2), in0=conv[:, m].rearrange("p (a n) -> p a n", a=2),
                                in1=halves(0), op=ALU.subtract).then_inc(S["centred"], 1)
            dve.wait_ge(S["stat_mm"], 1 + KD)
            V.tensor_scalar(rstd_ln.rearrange("p (a n) -> p a n", a=2), halves(2), EPS, None, ALU.add).then_inc(S["eps_ready"], 1)
            dve.wait_ge(S["std_ready"], 1)
            link(dve, V.reciprocal(rstd_ln, rstd_ln))
            dve.wait_ge(S["sqd"], KD)
            for m in range(KD):
                dve.wait_ge(S["centred"], m + 1)
                V.tensor_tensor(out=conv[:, m], in0=conv[:, m], in1=rstd_ln, op=ALU.mult).then_inc(S["lnx_ready"], 1)
            dve.wait_ge(S["bs_in"], 16)
            dve.wait_ge(S["zeroes"], ZEROED["bias"])
            for kv in range(KV):
                V.tensor_copy(bsc[32 * kv:32 * kv + 32, NCS * kv:NCS * (kv + 1)],
                              bs[32 * kv:32 * kv + 32, 31:31 + 16 * (NCS - 1) + 1:16]).then_inc(S["bsc_ready"], 1)
            dve.wait_ge(S["ct_tr"], 2 * DB)
            for b in range(DB):
                V.tensor_copy(new_rows[:, :, DS * b:DS * b + DS], glu_s[:, :, b, W - 1:W - 1 + DS]).then_inc(S["new_packed"], 1)

            dve.wait_ge(S["gpost_in"], 16)
            for t in range(TT + 1):
                if t < TT:
                    r = rows(t)
                    dve.wait_ge(S["sq_b"], t + 1)
                    mean_sq(0, r, "ms_b")
                    dve.wait_ge(S["sd_b"], t + 1)
                    link(dve, V.reciprocal(rs[0:r, 0:1], sd[0:r, 0:1]))
                    V.scalar_tensor_tensor(out=scaled_b[0:r], in0=pb(2 * (t % 2), D, p1=r), scalar=rs[0:r, 0:1],
                                           in1=gpost_a[0:r], op0=ALU.mult, op1=ALU.mult).then_inc(S["o_scaled"], 1)
                    dve.wait_ge(S["o_scaled"], t + 1)
                    dve.wait_ge(x_in[t], 32)
                    V.tensor_tensor(out=x_sb[0:r, t], in0=x_sb[0:r, t], in1=scaled_b[0:r], op=ALU.add).then_inc(S["x1_ready"], 1)
                if t:
                    k, rk = t - 1, rows(t - 1)
                    if k == 0:
                        dve.wait_ge(S["y_ready"], KD)
                        dve.wait_ge(S["co_out"], 16 * (1 + DB))
                    dve.wait_ge(S["tr_b"], k + 1)
                    for q, T in enumerate((hT, uT)):
                        V.tensor_tensor(out=T[:, :, k * P:k * P + rk], in0=pb(4 + 2 * (k % 2), KD, P)[:, :, 0:rk],
                                        in1=gain(4 + q, rk), op=ALU.mult).then_inc(S["hu_ready"], 1)
                if t < TT:
                    dve.wait_ge(S["sq_c"], t + 1)
                    mean_sq(1, r, "ms_c")
                    dve.wait_ge(S["sd_c"], t + 1)
                    link(dve, V.reciprocal(rs[0:r, 1:2], sd[0:r, 1:2]))
                    if t >= 2:
                        dve.wait_ge(S["tr_b"], t - 1)
                    dve.wait_ge(S["x1_ready"], t + 1)
                    V.tensor_scalar(xn_b[0:r, t % 2], x_sb[0:r, t], rs[0:r, 1:2], None, ALU.mult).then_inc(S["xn_b_ready"], 1)

            def split_lo(j):
                dve.wait_ge(S["hi_ready"], C_OA + j + 1)
                if j == KD:
                    V.tensor_tensor(out=wgate_lo, in0=wgate, in1=wgate_hi, op=ALU.subtract).then_inc(S["lo_ready"], 1)
                    return
                j -= j > KD
                V.tensor_tensor(out=tile_lo[:, j % TRING], in0=tile_w[:, j % TRING], in1=tile_hi[:, j % HRING],
                                op=ALU.subtract).then_inc(S["lo_ready"], 1)

            dve.wait_ge(S["hu_ready"], 2 * TT)
            for m in range(KD):
                dve.wait_ge(S["uh_ready"], m + 1)
                V.tensor_tensor(out=u_lo[:, m], in0=uT[:, m], in1=u_hi[:, m], op=ALU.subtract).then_inc(S["ul_ready"], 1)
            dve.wait_ge(S["zeroes"], ZEROED["keys"])
            for n in range(2 * TT):
                if n == TT:
                    split_lo(0)
                    split_lo(1)
                br, t = n // TT, n % TT
                dve.wait_ge(S["kt_tr"], n + 1)
                if t < 4:
                    for lo in range(2):
                        V.tensor_copy(ktz[HD * lo:HD * lo + HD, br, lo:KV:2, t * P:(t + 1) * P],
                                      pb(6 + n % 2, 2, P, p0=HD * lo, p1=HD * lo + HD)).then_inc(S["kt_ready"], 1)
                else:
                    V.tensor_copy(kt_new[:, br], pb(6 + n % 2, 2, P)[:, :, 0:NS]).then_inc(S["kt_ready"], 1)
            dve.wait_ge(S["cs_mm"], 4)
            for n in range(4):
                c, gi = n // 2, n % 2
                dve.wait_ge(S["ctp_tr"], n + 1)
                V.tensor_copy(ctP[:, c, :, :, 16 * gi:16 * gi + 16].rearrange("p j k c -> p k c j"),
                              pb(6 + n % 2, KV, 16, 8)).then_inc(S["ctp_ready"], 1)
            for j in range(2, KD + HRING):
                split_lo(j)
            dve.wait_ge(S["zeroes"], ZEROED["queries"])
            dve.wait_ge(S["q_ready"], KD)
            for p in range(2):
                for half in range(2):
                    lo = HD * half
                    V.tensor_copy(qbd[lo:lo + HD, :, p, 32 * half:32 * half + 32].rearrange("p b (g t) -> p b g t", g=G),
                                  qT[lo:lo + HD, 4 * p:4 * p + 4, SEQ:NT].rearrange("p g (b t) -> p b g t", b=DB)).then_inc(S["qbd_ready"], 1)
            split_lo(KD + HRING)
            dve.wait_ge(S["gate_tr"], 1)
            V.tensor_copy(gR, pb(2, 4, 48)).then_inc(S["gR_ready"], 1)
            dve.wait_ge(S["gR_ready"], 1)
            for i in range(4):
                V.tensor_copy(gRr[:, i], gR[:, 3 - i, 0:H]).then_inc(S["gR_ready"], 1)
            dve.wait_ge(S["gR_ready"], 5)

            for n in range(2):
                split_lo(KD + 1 + n + HRING)

            dve.wait_ge(S["zeroes"], ZEROED["table"])
            dve.wait_ge(S["x1_out"], 16 * TT)
            dve.wait_ge(S["kv_out"], KV_OUT)
            dve.wait_ge(S["late"], 16 * (2 + 2 * DB))
            dve.wait_ge(S["gate_out"], 16)
            for w in range(len(items) + 3):
                if w < len(items):
                    m, br, i, us = items[w]
                    u = us[0]
                    if br == 0:
                        dve.wait_ge(tb_in[m % 2], 32 * (m // 2 + 1))
                        if m:
                            dve.wait_ge(S["l_ready"], UPM * (m - 1) + 1)
                        V.tensor_copy(e2[:, :, 0:31], tb[:, m % 2, :, 31:SEQ:16]).then_inc(S["e2_ready"], 1)
                        dve.wait_ge(S["e2_ready"], m + 1)
                        dve.wait_ge(S["s_done"], u + 1)
                        if u >= 6:
                            dve.wait_ge(S["t_done"], u - 5)
                        L3 = l_sb[:, u % 6, 0:8 * NCP].rearrange("q (i h n) -> q i h n", i=4, h=2)
                        sc = pb(u % 3, 4, 64).rearrange("q i (h n) -> q i h n", h=2)
                        for ir in range(4):
                            ins = V.tensor_tensor(out=L3[:, ir], in0=sc[:, ir, :, 0:NCP], in1=e2[:, :, 8 * ir:8 * ir + NCP], op=ALU.add)
                        ins.then_inc(S["l_ready"], 1)
                        dve.wait_ge(S["l_ready"], u + 1)
                        L2 = l_sb[:, u % 6, 0:8 * NCP].rearrange("q (r n) -> q r n", n=NCP)
                        link(dve, V.tensor_reduce(mn[:, 0:8], L2, AX.X, ALU.min))
                        link(dve, V.tensor_scalar(mn[:, 0:8], mn[:, 0:8], 0.1 * BIG, None, ALU.min))
                        V.tensor_tensor(out=L2, in0=L2, in1=mn[:, 0:8].unsqueeze(2).broadcast_to([P, 8, NCP]),
                                        op=ALU.subtract).then_inc(S["cmin_ready"], 1)
                    else:
                        for half, u in enumerate(us):
                            dve.wait_ge(S["s_done"], u + 1)
                            if u >= 6:
                                dve.wait_ge(S["t_done"], u - 5)
                            k = stat(w) + half
                            if w >= 3:
                                dve.wait_ge(S["exp_done"], items[w - 3][3][-1] + 1)
                            V.tensor_tensor_reduce(l_sb[:, u % 6, 0:P * (i + 1)], pb(u % 3, P * (i + 1)),
                                                   tb[:, m % 2, half, 384 - P * i:SEQ], 1.0, 3 * BIG, ALU.add, ALU.min,
                                                   mn[:, k:k + 1]).then_inc(S["l_ready"], 1)
                if 1 <= w <= len(items):
                    m, br, i, us = items[w - 1]
                    dve.wait_ge(S["exp_done"], us[-1] + 1)
                    if br == 0:
                        if m:
                            dve.wait_ge(S["pn_ready"], UPM * (m - 1) + 1)
                        L2 = l_sb[:, us[0] % 6, 0:8 * NCP].rearrange("q (r n) -> q r n", n=NCP)
                        link(dve, V.tensor_reduce(den[:, 0:8], L2, AX.X, ALU.add))
                        link(dve, V.tensor_scalar(den[:, 0:8], den[:, 0:8], 1e-30, None, ALU.max))
                        link(dve, V.reciprocal(rden[:, 0:8], den[:, 0:8]))
                        h0 = 8 * (m // 4) + m % 4
                        V.tensor_tensor(out=rden[:, 0:8].rearrange("q (i h) -> q i h", h=2),
                                        in0=rden[:, 0:8].rearrange("q (i h) -> q i h", h=2),
                                        in1=gRr[:, :, h0:h0 + 5:4], op=ALU.mult).then_inc(S["den_ready"], 1)
                    else:
                        k = stat(w - 1)
                        if w >= 4:
                            dve.wait_ge(S["pn_ready"], items[w - 4][3][-1] + 1)
                        link(dve, V.tensor_scalar(den[:, k:k + 2], den[:, k:k + 2], 1e-30, None, ALU.max))
                        V.reciprocal(rden[:, k:k + 2], den[:, k:k + 2]).then_inc(S["den_ready"], 1)
                if 2 <= w < len(items) + 2:
                    m, br, i, us = items[w - 2]
                    u = us[-1]
                    n = SEQ if br == 0 else P * (i + 1)
                    dve.wait_ge(S["t_done"], u + 1)
                    if u >= 4:
                        dve.wait_ge(S["pv_done"], item_of[u - 4] + 1)
                    V.tensor_copy(pt_sb[:, u % 4, 0:n], pb(3 + u % 2, n)).then_inc(S["pt_d"], 1)
                if w >= 3 and (items[w - 3][1] == 0 or items[w - 3][2] == 3):
                    m, br = items[w - 3][:2]
                    dve.wait_ge(S["silu_ready"], 4 * m + (4 if br == 2 else 2))
                    dve.wait_ge(S["pv_done"], w - 2)
                    if br:
                        prev = 2 * m + br - 1
                        if prev:
                            dve.wait_ge(S["y_add"], prev)
                    V.tensor_tensor(out=y_tmp if br else yT[:, m, 0:SEQ], in0=pb(5, SEQ), in1=sz[:, br, m % 2], op=ALU.mult).then_inc(S["y_mul"], 1)

                if w - 1 in z_at and z_at[w - 1] + HRING < NBR * KD:
                    split_lo(KD + 1 + z_at[w - 1] + HRING)

            dve.wait_ge(S["ss_mm"], 1)
            dve.wait_ge(S["bsc_ready"], KV)
            dve.wait_ge(S["t_done"], N_UNITS)
            dve.wait_ge(S["gS_in"], 16 * NBR)
            L3 = l_sb[:, 0, 0:480].rearrange("q (b n) -> q b n", b=DB)
            V.tensor_tensor(out=L3, in0=pb(1, DB, 60), in1=bsc.unsqueeze(1).broadcast_to([P, DB, 60]), op=ALU.add).then_inc(S["sl_ready"], 1)
            dve.wait_ge(S["sl_ready"], 1)
            link(dve, V.tensor_reduce(mn[:, 0:8], L3, AX.X, ALU.min))
            link(dve, V.tensor_scalar(mn[:, 0:8], mn[:, 0:8], 0.1 * BIG, None, ALU.min))
            V.tensor_tensor(out=L3, in0=L3, in1=mn[:, 0:8].unsqueeze(2).broadcast_to([P, DB, 60]), op=ALU.subtract).then_inc(S["cmin_ready"], 1)
            dve.wait_ge(S["exp_done"], N_UNITS + 1)
            link(dve, V.tensor_reduce(den[:, 0:8], L3, AX.X, ALU.add))
            link(dve, V.tensor_scalar(den[:, 0:8], den[:, 0:8], 1e-30, None, ALU.max))
            link(dve, V.reciprocal(rden[:, 0:8], den[:, 0:8]))
            link(dve, V.tensor_tensor(out=rden[:, 0:8], in0=rden[:, 0:8], in1=gS[:, 0], op=ALU.mult))
            V.tensor_tensor(out=L3, in0=L3, in1=rden[:, 0:8].unsqueeze(2).broadcast_to([P, DB, 60]), op=ALU.mult).then_inc(S["sp_ready"], 1)
            dve.wait_ge(S["st_tr"], 1)
            dve.wait_ge(S["qbd_ready"], 4)
            V.tensor_copy(ptc.rearrange("p b n -> p (b n)"), pb(2, 1024, p1=60)).then_inc(S["pts_ready"], 1)
            dve.wait_ge(S["so_mm"], 1)
            V.tensor_copy(orc.rearrange("p b n -> p (b n)"), pb(0, 1024)).then_inc(S["or_ready"], 1)
            dve.wait_ge(S["silu_ready"], 4 * KD)

            def gate_sample(dst, src, br, b):
                for half in range(2):
                    lo = HD * half
                    o_ = src[lo:lo + HD].rearrange("q (p h g t) -> q p h g t", p=2, h=2, g=G)[:, :, half]
                    z_ = szs[lo:lo + HD, br, :, DS * b:DS * b + DS].rearrange("q (p g) t -> q p g t", p=2)
                    d_ = dst[lo:lo + HD].rearrange("q (p g) t -> q p g t", p=2)
                    V.tensor_tensor(out=d_, in0=o_, in1=z_, op=ALU.mult).then_inc(S["ys_mul"], 1)

            dve.wait_ge(S["ot_tr"], 1)
            for b in range(DB):
                gate_sample(yT[:, :, SEQ + DS * b:SEQ + DS * b + DS], pb(2, 1024)[:, b * P:(b + 1) * P], 0, b)
            def last_mean(t):
                dve.wait_ge(S["sq_a"], TT + t + 1)
                mean_sq(t, rows(t), "ms_a")

            def last_rows(t):
                r = rows(t)
                dve.wait_ge(S["sd_a"], TT + t + 1)
                link(dve, V.reciprocal(rs[0:r, t:t + 1], sd[0:r, t:t + 1]))
                if t >= 2:
                    dve.wait_ge(fy_out[t % 2], 16 * (t // 2))
                dve.wait_ge(S["gpost_in"], 32)
                dve.wait_ge(x_in[t % 2], 16 * (t // 2 + 3))
                link(dve, V.scalar_tensor_tensor(out=y_out[0:r, t % 2], in0=pb(4 + 2 * (t % 2), D, p1=r), scalar=rs[0:r, t:t + 1],
                                                 in1=gpost_b[0:r], op0=ALU.mult, op1=ALU.mult))
                V.tensor_tensor(out=y_out[0:r, t % 2], in0=y_out[0:r, t % 2], in1=x1_back[0:r, t % 2], op=ALU.add).then_inc(S["fy"], 1)

            dve.wait_ge(S["pv_done"], len(items))
            for half in range(2):
                V.tensor_tensor(out=fold[:, half * NS:half * NS + NS], in0=ident[:, 0:NS], in1=ident[:, NS:P], op=ALU.add).then_inc(S["ones_ready"], 1)
            for w in range(2 * DB + 4):
                n = w - 4
                if 0 <= n < 2 * DB:
                    b, br = n // 2, n % 2
                    dve.wait_ge(S["ot_tr"], n + 2)
                    gate_sample(y_br[:, br, :, DS * b:DS * b + DS], pb(3, P), 1 + br, b)
                n = w - 2
                if 0 <= n < 2 * DB:
                    b, br = n // 2, n % 2
                    dve.wait_ge(S["se_ready"], n + 1)
                    k = 8 + n % 4
                    link(dve, V.tensor_scalar(den[:, k:k + 1], den[:, k:k + 1], 1e-30, None, ALU.max))
                    link(dve, V.reciprocal(rden[:, k:k + 1], den[:, k:k + 1]))
                    L = l_sb[:, 1 + n % 3, 0:KS]
                    V.tensor_scalar(L, L, rden[:, k:k + 1], gS[:, 1 + br, b:b + 1], ALU.mult, ALU.mult).then_inc(S["sp_ready"], 1)
                n = w - 1
                if 0 <= n < 2 * DB:
                    dve.wait_ge(S["ss_mm"], n + 2)
                    if n >= 3:
                        dve.wait_ge(S["st_tr"], n - 1)
                    if n >= 4:
                        dve.wait_ge(S["se_ready"], n - 3)
                    k = 8 + n % 4
                    V.tensor_tensor_reduce(l_sb[:, 1 + n % 3, 0:KS], pb(1, KS), bs, 1.0, 3 * BIG, ALU.add, ALU.min,
                                           mn[:, k:k + 1]).then_inc(S["sl_ready"], 1)
                n = w - 2
                if 0 <= n < 2 * DB:
                    dve.wait_ge(S["st_tr"], n + 2)
                    if n >= 2:
                        dve.wait_ge(S["so_mm"], n)
                    else:
                        dve.wait_ge(S["pv_done"], len(items))
                    V.tensor_copy(pts[:, n % 2, 0:2], pb(2, 2, P)).then_inc(S["pts_ready"], 1)
                    V.tensor_copy(pts[0:DS, n % 2, 2], pb(2, 3, P, p1=DS)[:, 2]).then_inc(S["pts_ready"], 1)
                n = w - 3
                if 0 <= n < 2 * DB:
                    dve.wait_ge(S["so_mm"], n + 2)
                    if n >= 2:
                        dve.wait_ge(S["ot_tr"], n)
                    for p in range(2):
                        V.tensor_copy(orow[64 * p:64 * p + 64, n % 2], pb(3, 2, P, p0=64 * p, p1=64 * p + 64)[:, p]).then_inc(S["or_ready"], 1)
                if w in norm_at:
                    last_mean(norm_at[w])
                if w - 1 in norm_at:
                    last_rows(norm_at[w - 1])
            dve.wait_ge(S["ys_mul"], 2 * DB * 3)
            ys = yT[:, :, SEQ:NT]
            for br in range(2):
                V.tensor_tensor(out=ys, in0=ys, in1=y_br[:, br], op=ALU.add).then_inc(S["y_s"], 1)
                dve.wait_ge(S["y_s"], br + 1)

            dve.wait_ge(S["fo_mm"], TT + 1)
            V.tensor_scalar(ms[:, 4:5], pb(5, 1), 1.0 / D, EPS, ALU.mult, ALU.add).then_inc(S["ms_a"], 1)
            dve.wait_ge(S["sd_a"], 2 * TT)
            link(dve, V.reciprocal(rs[:, 4:5], sd[:, 4:5]))
            dve.wait_ge(fy_out[0], 16 * 2)
            dve.wait_ge(x_in[0], 16 * 6)
            for half in range(2):
                here = slice(half * NS, half * NS + NS)
                link(dve, V.scalar_tensor_tensor(out=y_out[here, 0, 0:D // 2], in0=pb(4, D // 2)[here], scalar=rs[here, 4:5],
                                                 in1=gpost_b[here, half * D // 2:(half + 1) * D // 2], op0=ALU.mult, op1=ALU.mult))
                V.tensor_tensor(out=y_out[here, 0, 0:D // 2], in0=y_out[here, 0, 0:D // 2], in1=x1_back[here, 0, 0:D // 2],
                                op=ALU.add).then_inc(S["fy"], 1)

        @block.tensor
        def _(pe):
            def product(out, pairs):
                pairs = list(pairs)
                for k, (l, r) in enumerate(pairs):
                    ins = pe.matmul(out, l, r, start=(k == 0), stop=(k == len(pairs) - 1))
                return ins

            def await_chunk(c):
                pe.wait_ge(place[c][2], arrived[c])

            def split_product(b0, w_hi, w_lo, x_hi=u_hi, x_lo=u_lo):
                for k in range(KD):
                    for hf in range(2):
                        out = pb(b0 + hf, HT)[0:w_hi.shape[2]]
                        h, l = (x[:, k, hf * HT:(hf + 1) * HT] for x in (x_hi, x_lo))
                        pe.matmul(out, w_hi[:, k], h, start=(k == 0), stop=False)
                        pe.matmul(out, w_hi[:, k], l, start=False, stop=False)
                        ins = pe.matmul(out, w_lo[:, k], h, start=False, stop=(k == KD - 1))
                return ins

            def tile_product(b0, j):
                c = j - (j > KD)
                pe.wait_ge(S["lo_ready"], j + 2)
                return split_product(b0, tile_hi[:, c % HRING], tile_lo[:, c % TRING])

            pe.wait_ge(S["ident_ready"], 1)
            for t in range(TT):
                r = rows(t)
                pe.wait_ge(S["xn_a_ready"], t + 1)
                if t >= 2:
                    pe.wait_ge(S["h_ready"], t - 1)
                for k in range(KD):
                    ins = pe.transpose(pb(4 + 2 * (t % 2), KD, P)[:, k, 0:r], xn_a[0:r, t % 2, k * P:(k + 1) * P], ident[0:r, 0:r])
                ins.then_inc(S["tr_a"], 1)
                if t == 0:
                    pe.wait_ge(S["vec_in"], 16 * 7)
                    for k in range(KD):
                        ins = pe.transpose(pb(2, KD, 37)[:, k], vec_rows[0:37, k * P:(k + 1) * P], ident[0:37, 0:37])
                    ins.then_inc(S["vec_ps"], 1)
                if t == 1:
                    pe.wait_ge(S["bias_in"], 32)
                    pe.matmul(pb(0, SEQ, p1=H), rel_rows, hot_rows, start=True, stop=True).then_inc(S["early_mm"], 1)
                    pe.wait_ge(S["pe_in"], 32)
                    for c in range(2):
                        ins = pe.transpose(pb(1, 2, 16)[:, c], pe_rows[:, c], ident[0:16, 0:16])
                    ins.then_inc(S["early_mm"], 1)
            pe.wait_ge(S["state_in"], 32)
            pe.wait_ge(S["h_ready"], 4)
            for n in range(4):
                i, mg = n // 2, n % 2
                if n >= 2:
                    pe.wait_ge(S["state_ready"], 4 * (n - 1))
                for k in range(4):
                    ins = pe.transpose(pb(6 + n % 2, 4, 120)[:, k], state_rows[0:120, i, (4 * mg + k) * P:(4 * mg + k + 1) * P],
                                       ident[0:120, 0:120])
                ins.then_inc(S["state_tr"], 1)

            def ct_transposes(n):
                pe.wait_ge(rows_in[n % 4], 64 * (n // 4 + 1))
                if n == DB:
                    pe.wait_ge(S["hid_ready"], 2)
                    pe.wait_ge(S["kc_ready"], 1)
                if n >= 2:
                    pe.wait_ge(S["ct_ready"], n - 1)
                else:
                    pe.wait_ge(S["state_ready"], 16)
                for kv in range(KV):
                    ins = pe.transpose(pb(6 + n % 2, KV, P)[:, kv], rows_slot(n)[:, kv], ident)
                ins.then_inc(S["ct_tr"], 1)

            def compress(c, ht, part):
                if ht == 0 and part == 0:
                    pe.wait_ge(S["w1_in"], 16 * (c + 1))
                    pe.wait_ge(S["ct_ready"], DB * (c + 1))
                    pe.wait_ge(S["pe_ready"], c + 1)
                for j in range(8 * part, 8 * part + 8):
                    ins = pe.matmul(pb(6 + ht, 33, NCS), w1_sb[:, j, ht * P:(ht + 1) * P],
                                    ctS[:, j % 8, :, j // 8:j // 8 + NCS], start=(j == 0), stop=(j == 15))
                if part:
                    ins.then_inc(S["cs_mm"], 1)

            pe.wait_ge(S["hl_ready"], TT)
            pe.wait_ge(S["line_part"], 2)
            pe.wait_ge(S["pe_sb_ready"], 1)
            pe.wait_ge(S["vec_ready"], 1)
            for m in range(KD):
                for j in range(3):
                    if m + j == 0:
                        pe.wait_ge(S["lo_ready"], 1)
                    else:
                        pe.wait_ge(S["lo_pool"], 3 * m + j)
                    if m:
                        pe.wait_ge(*((S["glu_ready"], 3 * m), (S["sg_ready"], m), (S["z_ready"], m))[j])
                    c = 3 * m + j
                    ins = split_product(2 * j, tile_hi[:, c % HRING], tile_lo[:, c % TRING], h_hi, h_lo)
                    ins.then_inc(S["proj_a"], 1)
                    if j == 1 and m < 3:
                        for n in range(3 * m, min(3 * m + 3, DB)):
                            ct_transposes(n)
                    if j == 1 and 3 <= m < 7:
                        compress(0, (m - 3) // 2, (m - 3) % 2)
                    if j == 1 and m == 7:
                        pe.wait_ge(S["w2_in"], 16 * 8)
                        pe.wait_ge(S["hid_ready"], 2)
                        product(pb(6, 480), ((w2_sb[:, 0, ht], hid[:, ht]) for ht in range(2))).then_inc(S["kc_mm"], 1)
            for b in range(4):
                ct_transposes(DB + b)
            pe.wait_ge(S["ones_ready"], 1)
            pe.wait_ge(S["glu_ready"], 3 * KD)
            for m in range(KD):
                pe.wait_ge(S["conv_step"], CONV * (m + 1))
                for hf in range(2):
                    ins = pe.matmul(pb(hf, HT), ones, conv[:, m, hf * HT:(hf + 1) * HT], start=(m == 0), stop=(m == KD - 1))
            ins.then_inc(S["stat_mm"], 1)

            for m in range(KD):
                pe.wait_ge(S["sqd"], m + 1)
                for hf in range(2):
                    ins = pe.matmul(pb(2 + hf, HT), ones, sg[:, m % 2, hf * HT:(hf + 1) * HT], start=(m == 0), stop=(m == KD - 1))
                ins.then_inc(S["stat_mm"], 1)
            for b in range(4, DB):
                ct_transposes(DB + b)
            for ht in range(2):
                for part in range(2):
                    compress(1, ht, part)
            pe.wait_ge(S["hid_ready"], 4)
            pe.wait_ge(S["z_ready"], KD)
            for b in range(DB):
                ins = product(pb(4, DB, P, p1=60)[:, b], ((hid[:, ht, 60 * b:60 * b + 60], w2_sb[:, 1, ht]) for ht in range(2)))
            ins.then_inc(S["vc_mm"], 1)
            pe.wait_ge(S["centred"], KD)
            for k in range(KD):
                ins = pe.transpose(pb(0, KD, P, p1=W - 1)[:, k], glu_p[:, k, SEQ:SEQ + W - 1], ident)
            ins.then_inc(S["co_tr"], 1)
            pe.wait_ge(S["eps_ready"], 1)
            pe.wait_ge(S["new_packed"], DB)
            for k in range(KD):
                ins = pe.transpose(pb(2, KD, P, p1=NS)[:, k], new_rows[:, k], ident)
            ins.then_inc(S["co_tr"], 1)

            pe.wait_ge(S["y_ready"], KD)
            pe.wait_ge(S["co_ready"], 2)
            pe.wait_ge(S["vc_ready"], 1)
            pe.wait_ge(S["hid_ready"], 4)

            def turn_b(t):
                r = rows(t)
                pe.wait_ge(S["xn_b_ready"], t + 1)
                if t >= 2:
                    pe.wait_ge(S["hu_ready"], 2 * (t - 1))
                for k in range(KD):
                    ins = pe.transpose(pb(4 + 2 * (t % 2), KD, P)[:, k, 0:r], xn_b[0:r, t % 2, k * P:(k + 1) * P], ident[0:r, 0:r])
                ins.then_inc(S["tr_b"], 1)

            def row_product(t, src, c0, done):
                r = rows(t)
                for c in range(4):
                    await_chunk(c0 + c)
                    ins = product(pb(2 * (t % 2), 4, CH, p1=r)[:, c], ((src[:, k, t * P:t * P + r], chunk_sb(c0 + c)[:, k]) for k in range(KD)))
                ins.then_inc(S[done], 1)
                return ins

            for t in range(TT):
                if t >= 2:
                    pe.wait_ge(S["o_scaled"], t - 1)
                ins = row_product(t, zA, C_OA, "o_mm")
                if t >= 1:
                    turn_b(t - 1)

            def kt_transposes(br):
                for t in range(TT):
                    n = TT * br + t
                    r = rows(t)
                    pe.wait_ge(S["kv_ready"], kv_at(2 * br + 2, t) + 1)
                    if n >= 2:
                        pe.wait_ge(S["kt_ready"], sum(2 if q % TT < 4 else 1 for q in range(n - 1)))
                    for p in range(2):
                        ins = pe.transpose(pb(6 + n % 2, 2, P)[:, p, 0:r], k_stage[0:r, br, t, p * P:(p + 1) * P], ident[0:r, 0:r])
                    ins.then_inc(S["kt_tr"], 1)

            for n in range(30):
                c, t = kv_jobs[n]
                await_chunk(C_KV + c)
                if n == 2:
                    turn_b(TT - 1)
                if n < 2:
                    pe.wait_ge(S["hu_ready"], 2 * (n + 1))
                    pe.wait_ge(S["o_scaled"], 4)
                elif n < 6:
                    pe.wait_ge(S["hu_ready"], 2 * TT if n >= 4 else 2 * (n + 1))
                    pe.wait_ge(S["o_scaled"], TT)
                else:
                    pe.wait_ge(S["kv_ready"], n - 5)
                if t < 4:
                    if c < 2:
                        lhs = hT[:, :, (t // 2) * 256 + t % 2:(t // 2) * 256 + 256:2]
                    else:
                        lhs = hT[:, :, t * P:(t + 1) * P]
                    product(pb(kv_bank(n), CH), ((lhs[:, k], chunk_sb(C_KV + c)[:, k]) for k in range(KD))).then_inc(S["kv_mm"], 1)
                elif c % 2:
                    for k in range(KD):
                        for kind in range(2):
                            ins = pe.matmul(pb(kv_bank(n - 1 + kind), CH, p0=kind * NS, p1=kind * NS + NS), hT[:, k, SEQ:NT],
                                            chunk_sb(C_KV + c - 1 + kind)[:, k], start=(k == 0), stop=(k == KD - 1))
                            if k == KD - 1:
                                ins.then_inc(S["kv_mm"], 1)
                if n == 23:
                    kt_transposes(0)
            kt_transposes(1)
            for n in range(4):
                c, gi = n // 2, n % 2
                if n >= 2:
                    pe.wait_ge(S["ctp_ready"], n - 1)
                else:
                    pe.wait_ge(S["kt_ready"], 18)
                for kv in range(KV):
                    ins = pe.transpose(pb(6 + n % 2, KV, P)[:, kv], cmp_rows[:, gi, c, kv], ident)
                ins.then_inc(S["ctp_tr"], 1)
            pe.wait_ge(S["kv_ready"], 30)
            pe.wait_ge(S["ctp_ready"], 4)

            def compress_p(n, c):
                pe.wait_ge(S["w1_in"], 16 * (2 + n))
                if n:
                    pe.wait_ge(S["hidp_ready"], 2)
                for ht in range(2):
                    product(pb(4 + ht, KV, NCP), ((w1_sb[:, j, ht * P:(ht + 1) * P], ctP[:, c, j % 8, :, j // 8:j // 8 + NCP])
                                                  for j in range(16))).then_inc(S["cp_mm"], 1)

            compress_p(0, 1)
            pe.wait_ge(S["hidp_ready"], 2)
            for p in range(2):
                for half in range(2):
                    kv = 2 * p + half
                    ins = product(pb(2 + p, HD, p0=32 * half, p1=32 * half + NCP),
                                  ((hid_p[:, ht, NCP * kv:NCP * (kv + 1)], w2_sb[:, 1, ht, 0:HD]) for ht in range(2)))
            ins.then_inc(S["cpp_mm"], 1)
            pe.wait_ge(S["ul_ready"], KD)
            for m in range(KD):
                if m >= 3:
                    pe.wait_ge(S["q_ready"], m - 2)
                if m == 1:
                    pe.wait_ge(S["bd_ready"], 4)
                if m == 2:
                    pe.wait_ge(S["hidp_ready"], 2)
                tile_product(2 * (m % 3), m).then_inc(S["q_mm"], 1)
            pe.wait_ge(S["lo_ready"], KD + 2)
            split_product(6, wgate_hi, wgate_lo).then_inc(S["gate_mm"], 1)
            pe.wait_ge(S["q_ready"], 7)
            compress_p(1, 0)
            pe.wait_ge(S["hidp_ready"], 4)
            product(pb(0, 124), ((w2_sb[:, 0, ht], hid_p[:, ht]) for ht in range(2))).then_inc(S["cpp_mm"], 1)
            pe.wait_ge(S["gate_ready"], 1)
            pe.wait_ge(S["q_ready"], KD)
            for i in range(4):
                ins = pe.transpose(pb(2, 4, 48)[:, i], gateT[0:48, i * P:(i + 1) * P], ident[0:48, 0:48])
            ins.then_inc(S["gate_tr"], 1)
            pe.wait_ge(S["gR_ready"], 1)
            pe.wait_ge(S["bd_ready"], 8)

            def z_product(n, b0):
                tile_product(b0, KD + 1 + n).then_inc(S["z_mm"], 1)

            z_product(0, 0)
            z_product(1, 2)

            pe.wait_ge(S["zb_ready"], 6)
            pe.wait_ge(S["kt_ready"], 18)
            pe.wait_ge(S["zeroes"], ZEROED["keys"])
            for w in range(len(items) + 3):
                if w < len(items):
                    m, br, i, us = items[w]
                    for half, u in enumerate(us):
                        if u >= 3:
                            pe.wait_ge(S["l_ready"], u - 2)
                        if br == 0:
                            for ir in range(4):
                                ins = pe.matmul(pb(u % 3, 4, 64)[:, ir], qT[:, m, (3 - ir) * P:(4 - ir) * P], kcbd[:, m // 4],
                                                start=True, stop=True)
                        else:
                            n = P * (i + 1)
                            ins = pe.matmul(pb(u % 3, n), qT[:, m, i * P:(i + 1) * P], ktz[:, br - 1, 2 * (m // 4) + half, 0:n],
                                            start=True, stop=True)
                        ins.then_inc(S["s_done"], 1)
                if w in z_at:
                    n = z_at[w]
                    pe.wait_ge(S["zb_ready"], 3 * n)
                    z_product(n, 6)
                if 2 <= w < len(items) + 2:
                    m, br, i, us = items[w - 2]
                    for u in us:
                        pe.wait_ge(S["pn_ready"], u + 1)
                        if u >= 2:
                            name, count = pt_by[u - 2]
                            pe.wait_ge(S[name], count)
                        if br == 0:
                            for ir in range(4):
                                ins = pe.transpose(pb(3 + u % 2, 4, P)[:, 3 - ir], pc_sb[:, ir], ident)
                        else:
                            for j in range(i + 1):
                                ins = pe.transpose(pb(3 + u % 2, 4, P)[:, j], l_sb[:, u % 6, j * P:(j + 1) * P], ident)
                        ins.then_inc(S["t_done"], 1)
                if w >= 3:
                    m, br, i, us = items[w - 3]
                    for u in us:
                        name, count = pt_by[u]
                        pe.wait_ge(S[name], count)
                    if 3 * m + br and (br == 0 or i == 0):
                        pe.wait_ge(S["y_mul"], 3 * m + br)
                    if br == 0:
                        ins = pe.matmul(pb(5, SEQ), vcbd[:, m // 4], pt_sb[:, us[0] % 4], start=True, stop=True)
                    else:
                        for j in range(i + 1):
                            for half, u in enumerate(us):
                                kv = 2 * (m // 4) + half
                                ins = pe.matmul(pb(5, SEQ, p0=HD * half, p1=HD * half + HD)[:, i * P:(i + 1) * P],
                                                v_sb[:, br - 1, j, kv * HD:(kv + 1) * HD], pt_sb[:, u % 4, j * P:(j + 1) * P],
                                                start=(j == 0), stop=(j == i))
                    ins.then_inc(S["pv_done"], 1)

            def last_part(job, ks=range(KD)):
                t, c = job // 4, job % 4
                if job == 0:
                    pe.wait_ge(S["y_add"], 2 * KD)
                    pe.wait_ge(S["pv_done"], len(items))
                    pe.wait_ge(S["zb_ready"], 72)
                if c == 0 and t >= 2:
                    pe.wait_ge(S["fy"], t - 1)
                await_chunk(C_OB + c)
                for k in ks:
                    ins = pe.matmul(pb(4 + 2 * (t % 2), 4, CH)[:, c], yT[:, k, t * P:(t + 1) * P], chunk_sb(C_OB + c)[:, k],
                                    start=(k == 0), stop=(k == KD - 1))
                if c == 3 and KD - 1 in ks:
                    ins.then_inc(S["fo_mm"], 1)

            pe.wait_ge(S["l_ready"], N_UNITS)
            pe.wait_ge(S["qbd_ready"], 4)
            pe.wait_ge(S["kc_ready"], 1)
            for b in range(DB):
                for p in range(2):
                    ins = pe.matmul(pb(1, DB, 60, p0=64 * p, p1=64 * p + 64)[:, b], qbd[:, b, p], kc_s[:, b], start=True, stop=True)
            ins.then_inc(S["ss_mm"], 1)
            last_part(0)
            last_part(1)
            pe.wait_ge(S["sp_ready"], 1)
            for b in range(DB):
                ins = pe.transpose(pb(2, DB, P, p1=60)[:, b], l_sb[:, 0, 60 * b:60 * b + 60], ident)
            ins.then_inc(S["st_tr"], 1)
            last_part(2)
            pe.wait_ge(S["pts_ready"], 1)
            for b in range(DB):
                ins = pe.matmul(pb(0, DB, P)[:, b], ptc[:, b], vc_s[0:60, b], start=True, stop=True)
            ins.then_inc(S["so_mm"], 1)
            last_part(3)
            pe.wait_ge(S["or_ready"], 1)
            for b in range(DB):
                ins = pe.transpose(pb(2, DB, P)[:, b], orc[:, b], ident)
            ins.then_inc(S["ot_tr"], 1)
            for w in range(2 * DB + 4):
                n = w
                if n < 2 * DB:
                    pe.wait_ge(slot_in[n % 6], totals[slot_in[n % 6]] + 48 * (n // 6 + 1))
                    if n:
                        pe.wait_ge(S["skt_ready"], n)
                    for p in range(2):
                        for pg in range(2):
                            ins = pe.transpose(pb(0, 2, 2, P)[:, p, pg], cache_sb[n % 6][:, pg, p * P:(p + 1) * P], ident)
                    ins.then_inc(S["skt_tr"], 1)
                n = w - 4
                if 0 <= n < 2 * DB:
                    pe.wait_ge(S["or_ready"], 1 + 2 * (n + 1))
                    pe.transpose(pb(3, P), orow[:, n % 2], ident).then_inc(S["ot_tr"], 1)
                for h in halves_at.get(w, ()):
                    last_part(4 + h // 2, range(4 * (h % 2), 4 * (h % 2) + 4))
                n = w - 1
                if 0 <= n < 2 * DB:
                    pe.wait_ge(S["skt_ready"], n + 1)
                    pe.wait_ge(S["kts_new"], n + 1)
                    pe.wait_ge(S["sl_ready"], n + 1)
                    for p in range(2):
                        ins = pe.matmul(pb(1, KS, p0=64 * p, p1=64 * p + 64), qbd[:, n // 2, p], kts[:, n % 2, p],
                                        start=True, stop=True)
                    ins.then_inc(S["ss_mm"], 1)
                n = w - 2
                if 0 <= n < 2 * DB:
                    pe.wait_ge(S["sp_ready"], n + 2)
                    if n == 0:
                        pe.wait_ge(S["ys_mul"], 2 * DB)
                    else:
                        pe.wait_ge(S["pts_ready"], 1 + 2 * n)
                    for j in range(3):
                        k = min(P, KS - j * P)
                        ins = pe.transpose(pb(2, 3, P, p1=k)[:, j], l_sb[:, 1 + n % 3, j * P:j * P + k], ident)
                    ins.then_inc(S["st_tr"], 1)
                n = w - 3
                if 0 <= n < 2 * DB:
                    pe.wait_ge(S["pts_ready"], 1 + 2 * (n + 1))
                    pe.wait_ge(S["ys_mul"], 2 * DB + 2 * n)
                    parts = [(pts[:, n % 2, j], cache_sb[n % 6][:, j, CH:2 * CH]) for j in range(2)]
                    parts.append((pts[0:DS, n % 2, 2], vnew[:, n % 6]))
                    product(pb(3, CH), parts).then_inc(S["so_mm"], 1)
            pe.wait_ge(S["y_s"], 2)
            pe.wait_ge(S["fy"], 3)
            for c in range(2):
                for k in range(KD):
                    for half in range(2):
                        ins = pe.matmul(pb(4, 2, CH, p0=half * NS, p1=half * NS + NS)[:, c], yT[:, k, SEQ:NT],
                                        chunk_sb(C_OB + 2 * half + c)[:, k], start=(k == 0), stop=(k == KD - 1))
            ins.then_inc(S["fo_mm"], 1)
            pe.wait_ge(S["ones_ready"], 3)
            pe.wait_ge(S["sq_a"], 2 * TT)
            pe.matmul(pb(5, 1), fold, ss[:, 4:5], start=True, stop=True).then_inc(S["fo_mm"], 1)


INPUTS = ['x_prompt', 'x_sample', 'state_conv', 'cache_cmp', 'cache_slc', 'state_win', 'page_table', 'rel_bias',
          'a_norm_pre', 'a_w_in', 'a_conv_w', 'a_conv_b', 'a_ln_g', 'a_ln_b', 'a_w_out', 'a_norm_post',
          'kv_norm', 'w_kv', 'cmp_pe', 'cmp_w1', 'cmp_w2', 'b_norm_pre', 'b_w_in', 'b_w_out', 'b_norm_post']
OUTPUTS = [('y_prompt', (1, SEQ, D)), ('y_sample', (DB, DS, D)), ('conv_prompt', (1, 1, W - 1, D)),
           ('conv_sample', (1, DB, W - 1, D)), ('cmp_prompt', (1, SEQ, 2, KV, HD)), ('cmp_sample', (DB, DS, 2, KV, HD)),
           ('slc_prompt', (1, SEQ, 2, KV, HD)), ('slc_sample', (DB, DS, 2, KV, HD)),
           ('win_prompt', (1, SEQ, 2, KV, HD)), ('win_sample', (DB, KS, 2, KV, HD))]


def kernel(**inputs):
    import numpy as _np
    import concourse.bacc as _bacc
    from concourse import mybir as _mybir
    from concourse.bass_utils import run_bass_kernel_spmd as _run

    nc = _bacc.Bacc("TRN2", target_bir_lowering=False, num_devices=1)
    arrays, ins = {}, {}
    for name in INPUTS:
        a = _np.ascontiguousarray(inputs[name])
        arrays[f"in_{name}"] = a
        ins[name] = nc.dram_tensor(f"in_{name}", a.shape, _mybir.dt.from_np(a.dtype), kind="ExternalInput").ap()
    a = bucket_rows()
    arrays["bucket_rows"] = a
    ins["bucket_rows"] = nc.dram_tensor("bucket_rows", a.shape, _mybir.dt.float32, kind="ExternalInput").ap()
    outs = {name: nc.dram_tensor(f"out_{name}", shape, _mybir.dt.float32, kind="ExternalOutput").ap() for name, shape in OUTPUTS}
    build(nc, ins, outs)
    r = _run(nc, [arrays], core_ids=[0])
    return tuple(r.results[0][f"out_{name}"] for name, _ in OUTPUTS)
```
